# Optimizing a Trainium2 kernel written in Bass

```python
import jax, jax.numpy as jnp
from jax import lax
import numpy as np

D_MODEL = 1024
BATCH = 1
SEQ = 256
DEPTH = 1

SB_HEADS = 8
SB_HEAD_DIM = 64
SB_WIDTH = SB_HEADS * SB_HEAD_DIM
Q_BLOCK = 128
CONV_GROUPS = 8
CONV_GROUP_DIM = 64
CONV_WIDTH = CONV_GROUPS * CONV_GROUP_DIM
CONV_KSIZE = 3
N_BRANCHES = 2
N_GROUPS = 4
EXPERTS_PER_GROUP = 8
N_EXPERTS = N_GROUPS * EXPERTS_PER_GROUP
TOP_K_IN_GROUP = 2
D_EXPERT = 256
NORM_EPS = 1e-6
IN_SIZES = (SB_WIDTH, SB_WIDTH, SB_WIDTH, CONV_WIDTH, CONV_WIDTH, CONV_WIDTH, D_MODEL, D_MODEL)
IN_PROJ_WIDTH = sum(IN_SIZES)
IN_SPLITS = tuple(int(s) for s in np.cumsum(IN_SIZES)[:-1])


def rms_norm(x, g):
    xf = x.astype(jnp.float32)
    y = xf * lax.rsqrt(jnp.mean(xf * xf, axis=-1, keepdims=True) + NORM_EPS)
    return (y * g.astype(jnp.float32)).astype(x.dtype)

def stick_breaking_attention(q, k, v):
    B, H, S, dh = q.shape
    n_blocks = S // Q_BLOCK
    scale = SB_HEAD_DIM ** -0.5
    kf = k.astype(jnp.float32)
    vf = v.astype(jnp.float32)
    key_pos = jnp.arange(S)

    def one_block(i):
        start = i * Q_BLOCK
        qb = lax.dynamic_slice_in_dim(q, start, Q_BLOCK, axis=2).astype(jnp.float32)
        z = jnp.einsum('bhqd,bhkd->bhqk', qb, kf) * scale
        q_pos = start + jnp.arange(Q_BLOCK)
        mask = key_pos[None, :] < q_pos[:, None]
        neg_log_1m_beta = jnp.where(mask, jax.nn.softplus(z), 0.0)
        tail = lax.cumsum(neg_log_1m_beta, axis=3, reverse=True) - neg_log_1m_beta
        a = jnp.where(mask, jnp.exp(jax.nn.log_sigmoid(z) - tail), 0.0)
        return jnp.einsum('bhqk,bhkd->bhqd', a, vf)

    out = lax.map(one_block, jnp.arange(n_blocks))
    out = jnp.transpose(out, (1, 0, 3, 2, 4)).reshape(B, S, H * dh)
    return out.astype(q.dtype)

def short_conv_mixer(b_gate, c_gate, u, conv_w):
    S = u.shape[1]
    cu = c_gate * u
    cu_pad = jnp.pad(cu, ((0, 0), (CONV_KSIZE - 1, 0), (0, 0)))
    y = conv_w[0] * cu_pad[:, 0:S]
    for j in range(1, CONV_KSIZE):
        y = y + conv_w[j] * cu_pad[:, j:j + S]
    return b_gate * y

def hierarchical_moe(h, w_rg, b_rg, w_re, b_re, w_gate, w_up, w_down):
    N = h.shape[0]
    hf = h.astype(jnp.float32)
    g_logits = hf @ w_rg.astype(jnp.float32) + b_rg.astype(jnp.float32)
    g_prob = jax.nn.softmax(g_logits, axis=-1)
    _, g_idx = lax.top_k(g_logits, 1)
    g_w = jnp.take_along_axis(g_prob, g_idx, axis=-1)
    e_logits = (hf @ w_re.astype(jnp.float32) + b_re.astype(jnp.float32)).reshape(N, N_GROUPS, EXPERTS_PER_GROUP)
    e_in_group = jnp.take_along_axis(e_logits, g_idx[:, :, None], axis=1)[:, 0]
    top_v, top_i = lax.top_k(e_in_group, TOP_K_IN_GROUP)
    top_w = jax.nn.softmax(top_v, axis=-1)
    within = jnp.sum(jax.nn.one_hot(top_i, EXPERTS_PER_GROUP, dtype=jnp.float32) * top_w[..., None], axis=1)
    combine = (jax.nn.one_hot(g_idx[:, 0], N_GROUPS, dtype=jnp.float32)[:, :, None]
               * within[:, None, :] * g_w[:, :, None]).astype(h.dtype)
    y = jnp.zeros_like(h)
    for g in range(N_GROUPS):
        sl = slice(g * EXPERTS_PER_GROUP, (g + 1) * EXPERTS_PER_GROUP)
        act = jax.nn.silu(jnp.einsum('nd,edf->nef', h, w_gate[sl])) * jnp.einsum('nd,edf->nef', h, w_up[sl])
        act = act * combine[:, g, :, None]
        y = y + jnp.einsum('nef,efd->nd', act, w_down[sl])
    return y

def first_inputs(seed: int = 0) -> dict:
    key = jax.random.key(seed)
    ks = jax.random.split(key, 20)
    f32 = jnp.float32
    nrm = lambda k, shape, fan_in: jax.random.normal(k, shape, f32) * (fan_in ** -0.5)
    gain = lambda k, shape: 1.0 + 0.05 * jax.random.normal(k, shape, f32)
    return {
        "x": jax.random.normal(ks[0], (BATCH, SEQ, D_MODEL), f32),
        "norm_mix_g": gain(ks[1], (DEPTH, D_MODEL)),
        "w_in": nrm(ks[2], (DEPTH, D_MODEL, IN_PROJ_WIDTH), D_MODEL),
        "q_norm_g": gain(ks[3], (DEPTH, SB_HEAD_DIM)),
        "k_norm_g": gain(ks[4], (DEPTH, SB_HEAD_DIM)),
        "conv_w": nrm(ks[5], (DEPTH, CONV_KSIZE, CONV_WIDTH), CONV_KSIZE),
        "w_sb_branch": nrm(ks[6], (DEPTH, SB_WIDTH, D_MODEL), SB_WIDTH),
        "w_conv_branch": nrm(ks[7], (DEPTH, CONV_WIDTH, D_MODEL), CONV_WIDTH),
        "w_out": nrm(ks[8], (DEPTH, D_MODEL, D_MODEL), D_MODEL),
        "norm_ffn_g": gain(ks[9], (DEPTH, D_MODEL)),
        "w_router_group": nrm(ks[10], (DEPTH, D_MODEL, N_GROUPS), D_MODEL),
        "b_router_group": 0.01 * jax.random.normal(ks[11], (DEPTH, N_GROUPS), f32),
        "w_router_expert": nrm(ks[12], (DEPTH, D_MODEL, N_EXPERTS), D_MODEL),
        "b_router_expert": 0.01 * jax.random.normal(ks[13], (DEPTH, N_EXPERTS), f32),
        "w_gate_e": nrm(ks[14], (DEPTH, N_EXPERTS, D_MODEL, D_EXPERT), D_MODEL),
        "w_up_e": nrm(ks[15], (DEPTH, N_EXPERTS, D_MODEL, D_EXPERT), D_MODEL),
        "w_down_e": nrm(ks[16], (DEPTH, N_EXPERTS, D_EXPERT, D_MODEL), D_EXPERT),
    }

def first_block(x, norm_mix_g, w_in, q_norm_g, k_norm_g, conv_w, w_sb_branch, w_conv_branch,
              w_out, norm_ffn_g, w_router_group, b_router_group, w_router_expert,
              b_router_expert, w_gate_e, w_up_e, w_down_e):
    B, S, D = x.shape
    for l in range(DEPTH):
        h = rms_norm(x, norm_mix_g[l])
        proj = h @ w_in[l]
        q, k, v, c_b, c_c, c_u, g_a, g_b = jnp.split(proj, IN_SPLITS, axis=-1)
        q = rms_norm(q.reshape(B, S, SB_HEADS, SB_HEAD_DIM), q_norm_g[l]).transpose(0, 2, 1, 3)
        k = rms_norm(k.reshape(B, S, SB_HEADS, SB_HEAD_DIM), k_norm_g[l]).transpose(0, 2, 1, 3)
        v = v.reshape(B, S, SB_HEADS, SB_HEAD_DIM).transpose(0, 2, 1, 3)
        branch_a = stick_breaking_attention(q, k, v) @ w_sb_branch[l]
        branch_b = short_conv_mixer(c_b, c_c, c_u, conv_w[l]) @ w_conv_branch[l]
        merged = jax.nn.sigmoid(g_a) * branch_a + jax.nn.sigmoid(g_b) * branch_b
        x = x + merged @ w_out[l]
        h2 = rms_norm(x, norm_ffn_g[l]).reshape(B * S, D)
        y = hierarchical_moe(h2, w_router_group[l], b_router_group[l], w_router_expert[l],
                             b_router_expert[l], w_gate_e[l], w_up_e[l], w_down_e[l])
        x = x + y.reshape(B, S, D)
    return x


HEAD_DIM = 64
N_ATTN_HEADS = D_MODEL // (2 * HEAD_DIM)
N_GMLP_GROUPS = D_MODEL // (2 * HEAD_DIM)
ATTN_WIDTH = N_ATTN_HEADS * HEAD_DIM
GMLP_WIDTH = N_GMLP_GROUPS * HEAD_DIM
MIX_WIDTH = ATTN_WIDTH + GMLP_WIDTH
IN_PROJ_WIDTH_2 = 3 * ATTN_WIDTH + 2 * GMLP_WIDTH
MOBA_BLOCK = 256
MOBA_TOPK = 3
Q_CHUNK = 128
GMLP_CHUNK = 128
ROPE_THETA = 10000.0
FFN_HIDDEN = -(-(8 * D_MODEL) // (3 * 256)) * 256
DEEPNORM_ALPHA = (2 * DEPTH) ** 0.25
DEEPNORM_BETA = (8 * DEPTH) ** -0.25
LN_EPS = 1e-5
RMS_EPS = 1e-6
NEG_INF = -1e30


def layer_norm(x, g, b):
    xf = x.astype(jnp.float32)
    mu = jnp.mean(xf, axis=-1, keepdims=True)
    var = jnp.mean(jnp.square(xf - mu), axis=-1, keepdims=True)
    return ((xf - mu) * lax.rsqrt(var + LN_EPS) * g.astype(jnp.float32) + b.astype(jnp.float32)).astype(x.dtype)

def rms_norm_2(x, g):
    xf = x.astype(jnp.float32)
    ms = jnp.mean(jnp.square(xf), axis=-1, keepdims=True)
    return (xf * lax.rsqrt(ms + RMS_EPS) * g.astype(jnp.float32)).astype(x.dtype)

def rope(t, pos):
    inv_freq = ROPE_THETA ** (-jnp.arange(0, HEAD_DIM, 2, dtype=jnp.float32) / HEAD_DIM)
    ang = pos.astype(jnp.float32)[:, None] * inv_freq[None, :]
    ang = jnp.concatenate([ang, ang], axis=-1)
    cos = jnp.cos(ang).astype(t.dtype)
    sin = jnp.sin(ang).astype(t.dtype)
    t1, t2 = t[..., : HEAD_DIM // 2], t[..., HEAD_DIM // 2:]
    rot = jnp.concatenate([-t2, t1], axis=-1)
    return t * cos + rot * sin

def moba_attention(q, k, v):
    B, H, S, hd = q.shape
    nb = -(-S // MOBA_BLOCK)
    pad = nb * MOBA_BLOCK - S
    kb = jnp.pad(k, ((0, 0), (0, 0), (0, pad), (0, 0))).reshape(B, H, nb, MOBA_BLOCK, hd)
    vb = jnp.pad(v, ((0, 0), (0, 0), (0, pad), (0, 0))).reshape(B, H, nb, MOBA_BLOCK, hd)
    pos = jnp.arange(S, dtype=jnp.int32)
    own = pos // MOBA_BLOCK
    own_idx = jnp.broadcast_to(own[None, None, :, None], (B, H, S, 1)).astype(jnp.int32)
    n_sel = min(MOBA_TOPK, nb - 1)
    if n_sel > 0:
        k_mean = jnp.mean(kb.astype(jnp.float32), axis=3)
        gate = jnp.einsum('bhsd,bhnd->bhsn', q.astype(jnp.float32), k_mean)
        past = jnp.arange(nb, dtype=jnp.int32)[None, :] < own[:, None]
        gate = jnp.where(past[None, None], gate, NEG_INF)
        _, sel = lax.top_k(gate, n_sel)
        idx = jnp.concatenate([sel.astype(jnp.int32), own_idx], axis=-1)
    else:
        idx = own_idx
    nsb = idx.shape[-1]
    n_chunks = S // Q_CHUNK
    q_c = q.reshape(B, H, n_chunks, Q_CHUNK, hd).transpose(2, 0, 1, 3, 4)
    idx_c = idx.reshape(B, H, n_chunks, Q_CHUNK, nsb).transpose(2, 0, 1, 3, 4)
    pos_c = pos.reshape(n_chunks, Q_CHUNK)
    b_ix = jnp.arange(B)[:, None, None, None]
    h_ix = jnp.arange(H)[None, :, None, None]
    key_off = jnp.arange(MOBA_BLOCK, dtype=jnp.int32)
    slot_own = jnp.arange(nsb) == nsb - 1
    scale = HEAD_DIM ** -0.5

    def attend(args):
        qc, ic, pc = args
        kg = kb[b_ix, h_ix, ic]
        vg = vb[b_ix, h_ix, ic]
        s = jnp.einsum('bhqd,bhqnkd->bhqnk', qc, kg).astype(jnp.float32) * scale
        own_c = pc // MOBA_BLOCK
        valid_blk = slot_own | (ic < own_c[:, None])
        key_pos = ic[..., None] * MOBA_BLOCK + key_off
        mask = valid_blk[..., None] & (key_pos <= pc[:, None, None])
        s = jnp.where(mask, s, NEG_INF)
        p = jax.nn.softmax(s.reshape(B, H, Q_CHUNK, nsb * MOBA_BLOCK), axis=-1)
        p = p.reshape(B, H, Q_CHUNK, nsb, MOBA_BLOCK).astype(vg.dtype)
        return jnp.einsum('bhqnk,bhqnkd->bhqd', p, vg)

    out = lax.map(attend, (q_c, idx_c, pos_c))
    return out.transpose(1, 2, 0, 3, 4).reshape(B, H, S, hd)

def spatial_gating(u, z, ln_g, ln_b, w_s, b_s):
    B, S, G, dg = z.shape
    z = layer_norm(z, ln_g, ln_b)
    nc = S // GMLP_CHUNK
    zc = z.reshape(B, nc, GMLP_CHUNK, G, dg)
    tril = jnp.tril(jnp.ones((GMLP_CHUNK, GMLP_CHUNK), dtype=bool))
    w = jnp.where(tril[None], w_s, jnp.zeros_like(w_s))
    mixed = jnp.einsum('gij,bcjgd->bcigd', w, zc) + b_s.T[None, None, :, :, None]
    return u * mixed.reshape(B, S, G, dg)

def hybrid_mixer(x, w_in, attn_out_g, gmlp_out_g, gmlp_ln_g, gmlp_ln_b, w_spatial, b_spatial, w_out):
    B, S, _ = x.shape
    h = x @ w_in
    A, G = ATTN_WIDTH, GMLP_WIDTH
    q, k, v, u, z = jnp.split(h, [A, 2 * A, 3 * A, 3 * A + G], axis=-1)

    def heads(t):
        return t.reshape(B, S, N_ATTN_HEADS, HEAD_DIM).transpose(0, 2, 1, 3)

    pos = jnp.arange(S, dtype=jnp.int32)
    qh = rope(heads(q), pos)
    kh = rope(heads(k), pos)
    attn = moba_attention(qh, kh, heads(v)).transpose(0, 2, 1, 3).reshape(B, S, A)

    u = jax.nn.gelu(u, approximate=False).reshape(B, S, N_GMLP_GROUPS, HEAD_DIM)
    z = jax.nn.gelu(z, approximate=False).reshape(B, S, N_GMLP_GROUPS, HEAD_DIM)
    sg = spatial_gating(u, z, gmlp_ln_g, gmlp_ln_b, w_spatial, b_spatial).reshape(B, S, G)

    merged = jnp.concatenate([rms_norm_2(attn, attn_out_g), rms_norm_2(sg, gmlp_out_g)], axis=-1)
    return merged @ w_out

def swiglu_ffn(x, w_gate, w_up, w_down):
    return (jax.nn.silu(x @ w_gate) * (x @ w_up)) @ w_down

def second_inputs(seed: int = 0) -> dict:
    key = jax.random.key(seed)
    ks = jax.random.split(key, 16)
    nrm = jax.random.normal
    f32 = jnp.float32
    x = nrm(ks[0], (BATCH, SEQ, D_MODEL), f32)
    w_in = nrm(ks[1], (DEPTH, D_MODEL, IN_PROJ_WIDTH_2), f32) * D_MODEL ** -0.5
    attn_out_g = 1.0 + 0.1 * nrm(ks[2], (DEPTH, ATTN_WIDTH), f32)
    gmlp_out_g = 1.0 + 0.1 * nrm(ks[3], (DEPTH, GMLP_WIDTH), f32)
    gmlp_ln_g = 1.0 + 0.1 * nrm(ks[4], (DEPTH, N_GMLP_GROUPS, HEAD_DIM), f32)
    gmlp_ln_b = 0.02 * nrm(ks[5], (DEPTH, N_GMLP_GROUPS, HEAD_DIM), f32)
    w_spatial = nrm(ks[6], (DEPTH, N_GMLP_GROUPS, GMLP_CHUNK, GMLP_CHUNK), f32) * GMLP_CHUNK ** -0.5
    b_spatial = 1.0 + 0.1 * nrm(ks[7], (DEPTH, N_GMLP_GROUPS, GMLP_CHUNK), f32)
    w_out = nrm(ks[8], (DEPTH, MIX_WIDTH, D_MODEL), f32) * (MIX_WIDTH ** -0.5 * DEEPNORM_BETA)
    ln1_g = 1.0 + 0.1 * nrm(ks[9], (DEPTH, D_MODEL), f32)
    ln1_b = 0.02 * nrm(ks[10], (DEPTH, D_MODEL), f32)
    w_gate = nrm(ks[11], (DEPTH, D_MODEL, FFN_HIDDEN), f32) * D_MODEL ** -0.5
    w_up = nrm(ks[12], (DEPTH, D_MODEL, FFN_HIDDEN), f32) * D_MODEL ** -0.5
    w_down = nrm(ks[13], (DEPTH, FFN_HIDDEN, D_MODEL), f32) * (FFN_HIDDEN ** -0.5 * DEEPNORM_BETA)
    ln2_g = 1.0 + 0.1 * nrm(ks[14], (DEPTH, D_MODEL), f32)
    ln2_b = 0.02 * nrm(ks[15], (DEPTH, D_MODEL), f32)
    return {"x": x, "w_in": w_in, "attn_out_g": attn_out_g, "gmlp_out_g": gmlp_out_g,
            "gmlp_ln_g": gmlp_ln_g, "gmlp_ln_b": gmlp_ln_b, "w_spatial": w_spatial,
            "b_spatial": b_spatial, "w_out": w_out, "ln1_g": ln1_g, "ln1_b": ln1_b,
            "w_gate": w_gate, "w_up": w_up, "w_down": w_down, "ln2_g": ln2_g, "ln2_b": ln2_b}

def second_block(x, w_in, attn_out_g, gmlp_out_g, gmlp_ln_g, gmlp_ln_b, w_spatial, b_spatial,
              w_out, ln1_g, ln1_b, w_gate, w_up, w_down, ln2_g, ln2_b):
    for l in range(DEPTH):
        mix = hybrid_mixer(x, w_in[l], attn_out_g[l], gmlp_out_g[l], gmlp_ln_g[l], gmlp_ln_b[l],
                           w_spatial[l], b_spatial[l], w_out[l])
        x = layer_norm(DEEPNORM_ALPHA * x + mix, ln1_g[l], ln1_b[l])
        ffn = swiglu_ffn(x, w_gate[l], w_up[l], w_down[l])
        x = layer_norm(DEEPNORM_ALPHA * x + ffn, ln2_g[l], ln2_b[l])
    return x


def setup_inputs(seed=0):
    out = dict(first_inputs(seed))
    for name, value in second_inputs(seed + 1).items():
        if name != "x":
            out[name + "_2"] = value
    return out


def reference(
    x, norm_mix_g, w_in, q_norm_g, k_norm_g, conv_w, w_sb_branch, w_conv_branch, w_out,
    norm_ffn_g, w_router_group, b_router_group, w_router_expert, b_router_expert, w_gate_e,
    w_up_e, w_down_e, w_in_2, attn_out_g_2, gmlp_out_g_2, gmlp_ln_g_2, gmlp_ln_b_2, w_spatial_2,
    b_spatial_2, w_out_2, ln1_g_2, ln1_b_2, w_gate_2, w_up_2, w_down_2, ln2_g_2, ln2_b_2,
):
    x = first_block(
        x, norm_mix_g, w_in, q_norm_g, k_norm_g, conv_w, w_sb_branch, w_conv_branch, w_out,
        norm_ffn_g, w_router_group, b_router_group, w_router_expert, b_router_expert, w_gate_e,
        w_up_e, w_down_e,
    )
    return second_block(
        x, w_in_2, attn_out_g_2, gmlp_out_g_2, gmlp_ln_g_2, gmlp_ln_b_2, w_spatial_2,
        b_spatial_2, w_out_2, ln1_g_2, ln1_b_2, w_gate_2, w_up_2, w_down_2, ln2_g_2, ln2_b_2,
    )


_drawn_inputs = setup_inputs


def setup_inputs(seed=0):
    import zlib

    import numpy as np

    out = dict(_drawn_inputs(seed))
    spreads = {}
    factors = {'k_norm_g': 3.503,
     'b_router_group': 8.998,
     'gmlp_ln_g_2': 3.726,
     'gmlp_ln_b_2': 41.809,
     'ln1_b_2': 2.773,
     'ln2_b_2': 2.9,
     'b_spatial_2': 4.707}
    for name, (base, spread) in spreads.items():
        noise = np.random.default_rng([zlib.crc32(name.encode()), seed]).standard_normal(out[name].shape)
        drawn = base * np.exp(spread * noise) if base else spread * noise
        out[name] = __import__('jax').numpy.asarray(drawn.astype(out[name].dtype))
    for name, factor in factors.items():
        out[name] = (out[name] * factor).astype(out[name].dtype)
    return out
```

```python
from contextlib import ExitStack

import numpy as np

import concourse.bass as bass
from concourse import mybir

F32 = mybir.dt.float32
F32R = mybir.dt.float32r
BF16 = mybir.dt.bfloat16
I32 = mybir.dt.int32
ALU = mybir.AluOpType
ACT = mybir.ActivationFunctionType
AX = mybir.AxisListType.X

P = 128
KB = 1024
SEQ, D = 256, 1024
T = SEQ // P
KD = D // P
HD = 64
NH = 8
W = NH * HD
PAIRS = NH // 2
NG, EPG = 4, 8
NE = NG * EPG
FE = 256
KF = FE // P
QUAD = 4
NQ = NE // QUAD
CAP = 32
FFN = -(-(8 * D) // (3 * 256)) * 256
FCHUNK = 256
NCH = FFN // FCHUNK
MF = FCHUNK // P
ALPHA = 2.0 ** 0.25
RMS_EPS, LN_EPS = 1e-6, 1e-5
NEG = -1e30

N_SMALL = 14

RING = 12
UNIT = 2048
KU = 4
UPQ = 12
B1_UNITS = 28
MOE_UNITS = UPQ * NQ
B2_PRE = 14
S1 = B1_UNITS
SFF = S1 + B2_PRE

C_ID, C_NEGU, C_NEGO, C_LTRI, C_ONE, C_TRIU, C_MK1, C_MK2 = (P * i for i in range(8))
C_COS = 8 * P
C_SIN = C_COS + T * HD
C_IOTA = C_SIN + T * HD
C_THR = C_IOTA + CAP
C_N = C_THR + 8


def shape_constants():
    c = np.zeros((P, C_N), np.float32)
    r, k = np.arange(P)[:, None], np.arange(P)[None, :]
    c[:, C_ID:C_ID + P] = r == k
    c[:, C_NEGU:C_NEGU + P] = -(r >= k).astype(np.float32)
    c[:, C_NEGO:C_NEGO + P] = -1.0
    c[:, C_LTRI:C_LTRI + P] = r < k
    c[:, C_ONE:C_ONE + P] = 1.0
    c[:, C_TRIU:C_TRIU + P] = k >= r
    c[:, C_MK1:C_MK1 + P] = np.where(r < k, 0.0, NEG)
    c[:, C_MK2:C_MK2 + P] = np.where(k <= r, 0.0, NEG)
    inv = (np.float32(10000.0) ** (-np.arange(0, HD, 2, dtype=np.float32) / np.float32(HD))).astype(np.float32)
    ang = np.arange(SEQ, dtype=np.float32)[:, None] * inv[None, :]
    cos, sin = np.cos(ang).astype(np.float32), np.sin(ang).astype(np.float32)
    cos = np.concatenate([cos, cos], -1).reshape(T, P, HD)
    sin = np.concatenate([-sin, sin], -1).reshape(T, P, HD)
    c[:, C_COS:C_COS + T * HD] = cos.transpose(1, 0, 2).reshape(P, T * HD)
    c[:, C_SIN:C_SIN + T * HD] = sin.transpose(1, 0, 2).reshape(P, T * HD)
    c[:, C_IOTA:C_IOTA + CAP] = np.arange(CAP)
    c[:, C_THR:C_THR + 8] = CAP * (np.arange(8) + 1)
    return c


def build(nc, consts, x, norm_mix_g, w_in, q_norm_g, k_norm_g, conv_w, w_sb_branch, w_conv_branch, w_out,
          norm_ffn_g, w_router_group, b_router_group, w_router_expert, b_router_expert, w_gate_e, w_up_e,
          w_down_e, w_in_2, attn_out_g_2, gmlp_out_g_2, gmlp_ln_g_2, gmlp_ln_b_2, w_spatial_2, b_spatial_2,
          w_out_2, ln1_g_2, ln1_b_2, w_gate_2, w_up_2, w_down_2, ln2_g_2, ln2_b_2, out):
    with ExitStack() as ctx:
        def sem(name):
            return ctx.enter_context(nc.semaphore(name))

        def at(name, kib, shape, dt=F32):
            return nc.alloc_sbuf_tensor_at(name, shape, dt, offset=256 + int(kib * KB))

        ps = ctx.enter_context(nc.psum_tensor("ps", [P, 8, 512], F32))

        ring = at("ring", 0, [P, RING, UNIT])
        w_hi = at("w_hi", 96, [P, 2, UNIT], F32R)
        w_lo = at("w_lo", 112, [P, 2, UNIT], F32R)
        hT_hi = at("hT_hi", 128, [P, KD, SEQ], F32R)
        hT_lo = at("hT_lo", 136, [P, KD, SEQ], F32R)
        mgT_hi = at("mgT_hi", 128, [P, KD, SEQ], F32R)
        mgT_lo = at("mgT_lo", 136, [P, KD, SEQ], F32R)
        brT_hi = at("brT_hi", 144, [P, 2, 4, SEQ], F32R)
        brT_lo = at("brT_lo", 152, [P, 2, 4, SEQ], F32R)
        h2T = at("h2T", 128, [P, KD, SEQ])
        heT = at("heT", 136, [P, KD, P])
        pick = at("pick", 140, [P, T, P])
        pickw = at("pickw", 141, [P, T, P])
        pickT = at("pickT", 142, [P, T, P])
        actT = at("actT", 143, [P, KF, P])
        ysb = at("ysb", 144, [P, D])
        sil = at("sil", 148, [P, FE])
        act_e = at("act_e", 149, [P, FE])
        rt = at("rt", 150, [P, 1024])
        xT_hi = at("xT_hi", 128, [P, KD, SEQ], F32R)
        xT_lo = at("xT_lo", 136, [P, KD, SEQ], F32R)
        pT = at("pT", 144, [P, 2, 2, 384])
        gT_hi = at("gT_hi", 144, [P, KD, SEQ], F32R)
        gT_lo = at("gT_lo", 152, [P, KD, SEQ], F32R)
        hid_hi = at("hid_hi", 144, [P, MF, SEQ], F32R)
        hid_lo = at("hid_lo", 146, [P, MF, SEQ], F32R)
        hid = at("hid", 148, [P, MF, SEQ])
        sil2 = at("sil2", 150, [P, MF, SEQ])
        cst = at("cst", 160, [P, C_N])
        bfc = at("bfc", 160 + 5.5, [P, 3, P], BF16)
        wr = at("wr", 160 + 6.25, [P, KD, 36])
        gain = at("gain", 160 + 7.5, [P, 112])
        X = at("X", 168, [P, T, D])
        xn = at("xn", 176, [P, T, D])
        qk = at("qk", 176, [P, 2, T, W])
        ga = at("ga", 176, [P, KD, SEQ])
        h2n = at("h2n", 176, [P, T, D])
        prob = at("prob", 176, [P, 2, 2, 384])
        gcat = at("gcat", 176, [P, T, D])
        qkT = at("qkT", 184, [P, 2, PAIRS, SEQ])
        gb = at("gb", 184, [P, KD, SEQ])
        v = at("v", 192, [P, T, W])
        stick = at("stick", 196, [P, 2, 384])
        attw = at("attw", 200, [P, 2, 384])
        cu = at("cu", 196, [P, 4, SEQ])
        cy = at("cy", 200, [P, 4, SEQ])
        uu = at("uu", 196, [P, T, W])
        zz = at("zz", 200, [P, T, W])
        sq = at("sq", 204, [P, T, W])
        full = at("full", 208, [P, 4, 512])
        mg1 = at("mg1", 204, [P, 4, SEQ])
        mg2 = at("mg2", 208, [P, 4, SEQ])
        spT = at("spT", 216, [P, NH, P])
        spraw = at("spraw", 216, [P, NH, P])
        lngb = at("lngb", 212, [P, 2, W])
        atto = at("atto", 192, [P, T, W])
        ln1 = at("ln1", 184, [P, 2, D])
        ln2 = at("ln2", 212, [P, 2, D])
        st = at("st", 220, [P, 512])
        cnt = at("cnt", 222, [P, 8], I32)

        ident = cst[:, C_ID:C_ID + P]
        negu = cst[:, C_NEGU:C_NEGU + P]
        nego = cst[:, C_NEGO:C_NEGO + P]
        ltri = cst[:, C_LTRI:C_LTRI + P]
        ones = cst[:, C_ONE:C_ONE + P]
        triu = cst[:, C_TRIU:C_TRIU + P]
        cos = cst[:, C_COS:C_COS + T * HD].rearrange("p (t d) -> p t d", t=T)
        sin = cst[:, C_SIN:C_SIN + T * HD].rearrange("p (t d) -> p t d", t=T)
        iota = cst[:, C_IOTA:C_IOTA + CAP]
        thr = cst[:, C_THR:C_THR + 7]
        ident_b, mask1_b, mask2_b = bfc[:, 0, :], bfc[:, 1, :], bfc[:, 2, :]
        g1 = gain[:, 0:8]
        g2 = gain[:, 8:16]
        gq, gk = gain[:, 16:17], gain[:, 17:18]
        cw = gain[:, 18:30].rearrange("p (j m) -> p j m", j=3)
        rbias = gain[:, 30:66]
        gmix = gain[:, 66:74]
        bsp = gain[:, 74:82]

        ss1, y1, n1 = st[:, 0:2], st[:, 2:4], st[:, 4:10]
        ssk, yk, nk = st[:, 16:32], st[:, 32:48], st[:, 48:96]
        ssq, yq = st[:, 96:112], st[:, 112:128]
        ss2, y2 = st[:, 128:130], st[:, 130:132]
        bst = st[:, 136:160].rearrange("p (t c s) -> p t c s", t=T, c=2)
        mv = st[:, 160:164].rearrange("p (t s) -> p t s", t=T)
        yl = st[:, 164:166]
        mx = st[:, 176:192].rearrange("p (h t) -> p h t", t=T)
        mxn = st[:, 192:208].rearrange("p (h t) -> p h t", t=T)
        rsum = st[:, 208:224].rearrange("p (h t) -> p h t", t=T)
        rinv = st[:, 224:240].rearrange("p (h t) -> p h t", t=T)
        zs, zy = st[:, 240:256], st[:, 256:272]
        ssg, yg = st[:, 272:276], st[:, 276:280]
        nw = st[:, 288:400].rearrange("p (i n) -> p i n", n=16)

        land = [sem(f"land{i}") for i in range(RING)]
        land_x = [sem(f"land_x{t}") for t in range(T)]
        land_small = sem("land_small")
        land_taps = sem("land_taps")
        land_b2 = sem("land_b2")
        land_ln1 = sem("land_ln1")
        land_ln2 = sem("land_ln2")
        out_stored = sem("out_stored")
        hi_made = sem("hi_made")
        lo_made = sem("lo_made")
        unit_used = sem("unit_used")
        pair_free = [sem("pair_free0"), sem("pair_free1")]
        dve_own = sem("dve_own")
        act_own = sem("act_own")
        x_sq = sem("x_sq")
        bf_made = sem("bf_made")
        y1_made = sem("y1_made")
        xn_made = sem("xn_made")
        hT_ps = sem("hT_ps")
        full_made = sem("full_made")
        hThi_made = sem("hThi_made")
        hT_made = sem("hT_made")
        qk_sq = sem("qk_sq")
        qk_ss = sem("qk_ss")
        qk_y = sem("qk_y")
        qk_made = sem("qk_made")
        qkT_ps = sem("qkT_ps")
        qkT_made = sem("qkT_made")
        v_made = sem("v_made")
        z_ps = sem("z_ps")
        log_made = sem("log_made")
        sp_made = sem("sp_made")
        la_ps = sem("la_ps")
        attw_made = sem("attw_made")
        av_ps = sem("av_ps")
        brhi_made = sem("brhi_made")
        br_made = sem("br_made")
        cc_made = sem("cc_made")
        conv_made = sem("conv_made")
        convhi_made = sem("convhi_made")
        conv_split = sem("conv_split")
        ga_sig = sem("ga_sig")
        gb_sig = sem("gb_sig")
        mg_made = sem("mg_made")
        mghi_made = sem("mghi_made")
        mgT_made = sem("mgT_made")
        x2_made = sem("x2_made")
        x2_sq = sem("x2_sq")
        y2_made = sem("y2_made")
        h2n_made = sem("h2n_made")
        h2T_ps = sem("h2T_ps")
        h2T_made = sem("h2T_made")
        logit_ps = sem("logit_ps")
        gdiff_made = sem("gdiff_made")
        gexp_made = sem("gexp_made")
        assign_made = sem("assign_made")
        rank_ps = sem("rank_ps")
        count_made = sem("count_made")

        def moe_sems(tag):
            names = ("pick_made", "gath_ps", "heT_made", "pickT_made", "used", "sil_made", "act_made", "aT_ps",
                     "actT_made", "y_made", "spread")
            return {n: sem(f"{n}{tag}") for n in names}

        STARTED = ("y_made", "act_made", "actT_made", "gath_ps", "spread")
        first = moe_sems("_a")
        more = moe_sems("_b")
        land_more = [sem(f"land_more{i}") for i in range(UPQ)]
        spT_ps = sem("spT_ps")
        spT_made = sem("spT_made")
        xT_ps = sem("xT_ps")
        xThi_made = sem("xThi_made")
        xT_made = sem("xT_made")
        rope_made = sem("rope_made")
        rT_ps = sem("rT_ps")
        rT_made = sem("rT_made")
        v2_made = sem("v2_made")
        s_ps = sem("s_ps")
        mx_made = sem("mx_made")
        p_made = sem("p_made")
        pT_ps = sem("pT_ps")
        pT_made = sem("pT_made")
        o_ps = sem("o_ps")
        o_made = sem("o_made")
        zg_made = sem("zg_made")
        zc_made = sem("zc_made")
        zq_made = sem("zq_made")
        zss_made = sem("zss_made")
        zy_made = sem("zy_made")
        z_made = sem("z_made")
        u_made = sem("u_made")
        mix_ps = sem("mix_ps")
        sg_made = sem("sg_made")
        cat_sq = sem("cat_sq")
        cat_y = sem("cat_y")
        cat_made = sem("cat_made")
        gT_ps = sem("gT_ps")
        gfull_made = sem("gfull_made")
        gThi_made = sem("gThi_made")
        gT_made = sem("gT_made")
        var_made = sem("var_made")
        yl_made = sem("yl_made")
        x3_made = sem("x3_made")
        x3T_ps = sem("x3T_ps")
        x3Thi_made = sem("x3Thi_made")
        x3T_made = sem("x3T_made")
        sil2_made = sem("sil2_made")
        hid_made = sem("hid_made")
        hidhi_made = sem("hidhi_made")
        hidT_made = sem("hidT_made")
        y_out = sem("y_out")

        win = w_in[0].rearrange("(p k) n -> p k n", k=KD)
        win2 = w_in_2[0].rearrange("(p k) n -> p k n", k=KD)
        wsb = w_sb_branch[0].rearrange("(k p) n -> p k n", p=P)
        wcv = w_conv_branch[0].rearrange("(k p) n -> p k n", p=P)
        wo = w_out[0].rearrange("(k p) n -> p k n", p=P)
        wo2 = w_out_2[0].rearrange("(p k) n -> p k n", k=KD)
        wg2 = w_gate_2[0].rearrange("(p k) n -> p k n", k=KD)
        wu2 = w_up_2[0].rearrange("(p k) n -> p k n", k=KD)
        wd2 = w_down_2[0].rearrange("(c m p) n -> p c m n", m=MF, p=P)
        wge = w_gate_e[0].rearrange("(q j) (p k) f -> q p j k f", j=QUAD, k=KD)
        wue = w_up_e[0].rearrange("(q j) (p k) f -> q p j k f", j=QUAD, k=KD)
        wde = w_down_e[0].rearrange("(e) (p k) n -> e p (k n)", k=KF)

        CH_K, CH_Q, CH_V, CH_GA, CH_CC, CH_CU, CH_CB, CH_GB = 0, 1, 2, 3, 5, 6, 7, 8
        WIN_COL = [1, 0, 2, 6, 7, 4, 5, 3, 8, 9]
        units1 = []
        for c in WIN_COL:
            for h in range(2):
                units1.append(win[:, KU * h:KU * h + KU, 512 * c:512 * c + 512])
        for h in range(2):
            units1.append(wsb[:, :, 512 * h:512 * h + 512])
            units1.append(wcv[:, :, 512 * h:512 * h + 512])
        for h in range(2):
            for kh in range(2):
                units1.append(wo[:, KU * kh:KU * kh + KU, 512 * h:512 * h + 512])
        assert len(units1) == B1_UNITS
        WIN2_COL = [1, 0, 2, 4, 3]
        units2 = []
        for c in WIN2_COL:
            for h in range(2):
                units2.append(win2[:, KU * h:KU * h + KU, 512 * c:512 * c + 512])
        for h in range(2):
            for kh in range(2):
                units2.append(wo2[:, KU * kh:KU * kh + KU, 512 * h:512 * h + 512])
        assert len(units2) == B2_PRE

        def slot_of(n):
            return n % RING, 16 * (n // RING + 1)

        def load_of(i):
            return i if i < B1_UNITS else i + MOE_UNITS

        QS = [(B1_UNITS + u) % RING for u in range(UPQ)]
        LOOP_B = RING // 3
        LOOP_N = (NCH - 3) // LOOP_B
        assert 2 + LOOP_N * LOOP_B == NCH - 1

        def body_unit(c):
            return SFF + 2 + 3 * (c - 1)

        block = ctx.enter_context(nc.Block())

        @block.sync
        def _(sp):
            for t in range(T):
                sp.dma_start(X[:, t, :], x[0, t * P:(t + 1) * P, :]).then_inc(land_x[t], 16)
            for i, src in enumerate(units1):
                slot, _ = slot_of(i)
                if i >= RING:
                    sp.wait_ge(lo_made, i - RING + 1)
                sp.dma_start(ring[:, slot, :].rearrange("p (k n) -> p k n", k=KU), src).then_inc(land[slot], 16)

            def quad_unit(q, u, sems):
                if u < 8:
                    src = (wge if u < 4 else wue)[q, :, :, 2 * (u % 4):2 * (u % 4) + 2, :]
                    sp.dma_start(ring[:, QS[u], :].rearrange("p (j k f) -> p j k f", j=QUAD, k=2),
                                 src).then_inc(sems[u], 16)
                else:
                    sp.dma_start(ring[:, QS[u], :], wde[q * QUAD + (u - 8)]).then_inc(sems[u], 16)

            main_sems = [land[s] for s in QS]
            for u in range(UPQ):
                sp.wait_ge(lo_made, B1_UNITS + u - RING + 1)
                quad_unit(0, u, main_sems)
            with sp.Fori(1, NQ) as q:
                for u in range(UPQ):
                    sp.wait_ge(first["used"], q * UPQ + (u + 1 - UPQ))
                    quad_unit(q, u, main_sems)

            sp.wait_ge(count_made, 1)
            extra = sp.value_load(cnt[0:1, 0:1], min_val=0, max_val=7)
            with sp.If(extra > 0):
                sp.wait_ge(first["used"], MOE_UNITS)
                with sp.Fori(0, extra) as r:
                    with sp.Fori(0, NQ) as q:
                        for u in range(UPQ):
                            sp.wait_ge(more["used"], (r * NQ + q) * UPQ + (u + 1))
                            quad_unit(q, u, land_more)
            sp.wait_ge(more["used"], extra * MOE_UNITS + UPQ)

            sp.wait_ge(first["pick_made"], 1)
            sp.dma_start(spraw[:], w_spatial_2[0].rearrange("g i j -> i g j")).then_inc(land_b2, 16)
            for i, g in enumerate((gmlp_ln_g_2, gmlp_ln_b_2)):
                sp.dma_start(lngb[:, i, :], g[0].rearrange("g d -> (g d)").partition_broadcast(P)
                             ).then_inc(land_b2, 16)

            def b2_free(i):
                n = load_of(i)
                if n - RING < B1_UNITS + MOE_UNITS:
                    sp.wait_ge(first["used"], n - RING - B1_UNITS + 1)
                else:
                    sp.wait_ge(lo_made, i - RING + 1)

            for j, src in enumerate(units2):
                i = S1 + j
                slot, _ = slot_of(load_of(i))
                b2_free(i)
                sp.dma_start(ring[:, slot, :].rearrange("p (k n) -> p k n", k=KU), src).then_inc(land[slot], 16)

            def ffn_gu(i, w, c, turn=None):
                slot, _ = slot_of(load_of(i))
                if turn is None:
                    b2_free(i)
                else:
                    sp.wait_ge(lo_made, turn * RING + (i - RING + 1))
                if turn is not None:
                    src = w[:, :, bass.ds(turn * (LOOP_B * FCHUNK) + c * FCHUNK, FCHUNK)]
                else:
                    src = w[:, :, c * FCHUNK:(c + 1) * FCHUNK]
                sp.dma_start(ring[:, slot, :].rearrange("p (k n) -> p k n", k=KD), src).then_inc(land[slot], 16)

            def ffn_d(i, c, turn=None):
                slot, _ = slot_of(load_of(i))
                if turn is None:
                    b2_free(i)
                else:
                    sp.wait_ge(lo_made, turn * RING + (i - RING + 1))
                src = wd2[:, c] if turn is None else wd2[:, bass.ds(turn * LOOP_B + c, 1)].rearrange(
                    "p o m n -> p (o m) n")
                sp.dma_start(ring[:, slot, :].rearrange("p (m n) -> p m n", m=MF), src).then_inc(land[slot], 16)

            def ffn_body(c, turn=None):
                i = body_unit(c)
                ffn_gu(i, wg2, c, turn)
                ffn_gu(i + 1, wu2, c, turn)
                ffn_d(i + 2, c - 1, turn)

            ffn_gu(SFF, wg2, 0)
            ffn_gu(SFF + 1, wu2, 0)
            ffn_body(1)
            with sp.Fori(0, LOOP_N) as turn:
                for c in range(2, 2 + LOOP_B):
                    ffn_body(c, turn)
            ffn_body(NCH - 1)
            ffn_d(body_unit(NCH), NCH - 1)
            for t in range(T):
                sp.wait_ge(y_out, t + 1)
                sp.dma_start(out[0, t * P:(t + 1) * P, :], X[:, t, :]).then_inc(out_stored, 16)
            sp.wait_ge(out_stored, 16 * T)

        @block.tensor
        def _(pe):
            mm = nc.tensor.matmul

            def mm3(o, a_hi, a_lo, b_hi, b_lo, start, stop):
                mm(o, a_hi, b_hi, start=start, stop=False, skip_group_check=True)
                mm(o, a_hi, b_lo, start=False, stop=False, skip_group_check=True)
                return mm(o, a_lo, b_hi, start=False, stop=stop, skip_group_check=True)

            def token_unit(i, c, k0, aT_hi, aT_lo, n_k=KD):
                bank = 2 * (c % 2)
                if c >= 2 and k0 == 0:
                    pe.wait_ge(pair_free[c % 2], c // 2)
                pe.wait_ge(lo_made, i + 1)
                b = i % 2
                hi = w_hi[:, b, :].rearrange("p (k n) -> p k n", k=KU)
                lo = w_lo[:, b, :].rearrange("p (k n) -> p k n", k=KU)
                for t in range(T):
                    for kk in range(KU):
                        k = k0 + kk
                        tok = slice(t * P, (t + 1) * P)
                        last = mm3(ps[:, bank + t, :], aT_hi[:, k, tok], aT_lo[:, k, tok], hi[:, kk, :],
                                   lo[:, kk, :], start=(k == 0), stop=(k == n_k - 1))
                last.then_inc(unit_used, 1)

            def feature_unit(i, c, k0, aT_hi, aT_lo, n_k=KD):
                bank = 2 * (c % 2)
                if c >= 2 and k0 == 0:
                    pe.wait_ge(pair_free[c % 2], c // 2)
                pe.wait_ge(lo_made, i + 1)
                b = i % 2
                hi = w_hi[:, b, :].rearrange("p (k n) -> p k n", k=KU)
                lo = w_lo[:, b, :].rearrange("p (k n) -> p k n", k=KU)
                for m in range(4):
                    o = ps[:, bank + m // 2, (m % 2) * SEQ:(m % 2 + 1) * SEQ]
                    for kk in range(KU):
                        k = k0 + kk
                        col = slice(m * P, (m + 1) * P)
                        last = mm3(o, hi[:, kk, col], lo[:, kk, col], aT_hi[:, k, :], aT_lo[:, k, :],
                                   start=(k == 0 and m % 2 == 0), stop=(k == n_k - 1))
                last.then_inc(unit_used, 1)

            def transposes(src, bank, done):
                for t in range(T):
                    for k in range(KD):
                        tile = src[:, t, k:D:KD]
                        ins = nc.tensor.transpose(ps[:, bank + 2 * t + k // 4, (k % 4) * P:(k % 4 + 1) * P],
                                                  tile, ident)
                        if k % 4 == 3:
                            ins.then_inc(done, 1)

            pe.wait_ge(land_small, 16 * N_SMALL)
            pe.wait_ge(xn_made, T)
            transposes(xn, 0, hT_ps)
            pe.wait_ge(hT_made, 4)

            def proj(i, feature):
                (feature_unit if feature else token_unit)(i, i // 2, KU * (i % 2), hT_hi, hT_lo)

            def head_transposes(which):
                pe.wait_ge(qk_made, which + 1)
                for t in range(T):
                    for p in range(PAIRS):
                        ins = nc.tensor.transpose(ps[:, 4 + 2 * which + t, p * P:(p + 1) * P],
                                                  qk[:, which, t, p * P:(p + 1) * P], ident)
                ins.then_inc(qkT_ps, 1)

            def zbank(p):
                return 4 + 2 * (p % 2)

            def z_step(p):
                if p == 0:
                    pe.wait_ge(qkT_made, 2)
                    pe.wait_ge(bf_made, 1)
                if p >= 2:
                    pe.wait_ge(br_made, p - 1)
                for h in range(2):
                    row = slice(HD * h, HD * h + HD)
                    o = ps[:, zbank(p) + h, :]
                    mm(o[:, 0:SEQ], qkT[row, 0, p, 0:P], qkT[row, 1, p, :], start=True, stop=False,
                       skip_group_check=True)
                    mm(o[:, SEQ:SEQ + P], qkT[row, 0, p, P:SEQ], qkT[row, 1, p, P:SEQ], start=False, stop=False,
                       skip_group_check=True)
                for h in range(2):
                    o = ps[:, zbank(p) + h, :]
                    mm(o[:, 0:P], ident_b, mask1_b, start=False, stop=False, skip_group_check=True)
                    last = mm(o[:, SEQ:SEQ + P], ident_b, mask1_b, start=False, stop=True, skip_group_check=True)
                last.then_inc(z_ps, 1)

            def la_step(p):
                pe.wait_ge(sp_made, p + 1)
                for h in range(2):
                    o = ps[:, zbank(p) + h, :]
                    mm(o[:, 0:SEQ], negu, stick[:, h, 0:SEQ], start=False, stop=False, skip_group_check=True)
                    mm(o[:, P:SEQ], nego, stick[:, h, SEQ:SEQ + P], start=False, stop=False, skip_group_check=True)
                    last = mm(o[:, SEQ:SEQ + P], negu, stick[:, h, SEQ:SEQ + P], start=False, stop=True,
                              skip_group_check=True)
                last.then_inc(la_ps, 1)

            def av_step(p):
                pe.wait_ge(attw_made, p + 1)
                if p == 0:
                    pe.wait_ge(v_made, 1)
                for h in range(2):
                    head = slice((2 * p + h) * HD, (2 * p + h + 1) * HD)
                    o = ps[HD * h:HD * h + HD, zbank(p), 0:SEQ]
                    mm(o, v[:, 0, head], attw[:, h, 0:SEQ], start=True, stop=False, skip_group_check=True)
                    last = mm(o[:, P:SEQ], v[:, 1, head], attw[:, h, SEQ:SEQ + P], start=False, stop=True,
                              skip_group_check=True)
                last.then_inc(av_ps, 1)

            for i in range(4):
                proj(i, False)
            head_transposes(0)
            proj(4, False)
            proj(5, False)
            head_transposes(1)
            proj(6, True)
            z_step(0)
            proj(7, True)
            z_step(1)
            la_step(0)
            proj(8, True)
            av_step(0)
            la_step(1)
            proj(9, True)
            av_step(1)
            z_step(2)
            proj(10, True)
            z_step(3)
            la_step(2)
            proj(11, True)
            av_step(2)
            la_step(3)
            proj(12, True)
            av_step(3)
            for i in range(13, 20):
                proj(i, True)
            pe.wait_ge(br_made, PAIRS)
            pe.wait_ge(conv_split, 1)
            for h in range(2):
                for branch in range(2):
                    feature_unit(20 + 2 * h + branch, 10 + 2 * h + branch, 0, brT_hi[:, branch], brT_lo[:, branch],
                                 n_k=KU)
            for h in range(2):
                for kh in range(2):
                    pe.wait_ge(mgT_made, kh + 1)
                    token_unit(24 + 2 * h + kh, 14 + h, KU * kh, mgT_hi, mgT_lo)

            pe.wait_ge(h2n_made, T)
            transposes(h2n, 4, h2T_ps)
            pe.wait_ge(h2T_made, 4)
            for t in range(T):
                for k in range(KD):
                    last = mm(ps[:, 6, t * 36:t * 36 + 36], h2T[:, k, t * P:(t + 1) * P], wr[:, k, :],
                              start=(k == 0), stop=(k == KD - 1))
            last.then_inc(logit_ps, 1)
            for t in range(T):
                for h in range(2):
                    mm(ps[:, 2 * t + h, :], ident, X[:, t, h * 512:(h + 1) * 512], start=True, stop=False,
                       skip_group_check=True)
            pe.wait_ge(assign_made, 1)
            asg = rt[:, 0:64].rearrange("p (t e) -> p t e", t=T)
            mm(ps[:, 7, 0:NE], ltri, asg[:, 0, :], start=True, stop=True)
            mm(ps[:, 7, NE:2 * NE], ones, asg[:, 0, :], start=True, stop=False)
            mm(ps[:, 7, NE:2 * NE], ltri, asg[:, 1, :], start=False, stop=True)
            mm(ps[:, 7, 2 * NE:3 * NE], ones, asg[:, 0, :], start=True, stop=False)
            mm(ps[:, 7, 2 * NE:3 * NE], ones, asg[:, 1, :], start=False, stop=True).then_inc(rank_ps, 1)

            def quad(it, s, landed):
                pe.wait_ge(s["pick_made"], it + 1)
                pe.wait_ge(s["y_made"], it * 2 + 1)
                for k in range(KD):
                    for t in range(T):
                        mm(ps[:, 6 + k // 4, (k % 4) * P:(k % 4 + 1) * P], h2n[:, t, k:D:KD], pick[:, t, :],
                           start=(t == 0), stop=(t == T - 1))
                pe.wait_ge(s["act_made"], it + 1)
                for t in range(T):
                    last = nc.tensor.transpose(ps[:, 5, t * P:(t + 1) * P], pickw[:, t, :], ident)
                last.then_inc(s["gath_ps"], 1)
                pe.wait_ge(s["heT_made"], it + 1)
                pe.wait_ge(s["actT_made"], it + 1)
                for u in range(8):
                    if u == 4:
                        pe.wait_ge(s["pickT_made"], it + 1)
                    landed(pe, it, u)
                    wv = ring[:, QS[u], :].rearrange("p (j k f) -> p j k f", j=QUAD, k=2)
                    for kk in range(2):
                        k = 2 * (u % 4) + kk
                        for j in range(QUAD):
                            last = mm(ps[32 * j:32 * j + 32, 4 + u // 4, 0:FE], heT[:, k, 32 * j:32 * j + 32],
                                      wv[:, j, kk, :], start=(k == 0), stop=(k == KD - 1))
                    last.then_inc(s["used"], 1)
                pe.wait_ge(s["act_made"], it + 2)
                for k in range(KF):
                    last = nc.tensor.transpose(ps[:, 4, FE + k * P:FE + (k + 1) * P], act_e[:, k:FE:KF], ident)
                last.then_inc(s["aT_ps"], 1)
                pe.wait_ge(s["actT_made"], it + 2)
                for u in range(8, UPQ):
                    landed(pe, it, u)
                for h in range(2):
                    for k in range(KF):
                        for j in range(QUAD):
                            wv = ring[:, QS[8 + j], :].rearrange("p (k n) -> p k n", k=KF)
                            last = mm(ps[32 * j:32 * j + 32, 6 + h, :], actT[:, k, 32 * j:32 * j + 32],
                                      wv[:, k, h * 512:(h + 1) * 512], start=(k == 0), stop=(k == KF - 1))
                            if h == 1 and k == KF - 1:
                                last.then_inc(s["used"], 1)
                pe.wait_ge(s["y_made"], it * 2 + 3)
                for t in range(T):
                    for h in range(2):
                        last = mm(ps[:, 2 * t + h, :], pickT[:, t, :], ysb[:, h * 512:(h + 1) * 512], start=False,
                                  stop=False, skip_group_check=True)
                last.then_inc(s["spread"], 1)

            def landed_first(eng, it, u):
                eng.wait_ge(land[QS[u]], it * 16 + slot_of(B1_UNITS + u)[1])

            def landed_more(eng, it, u):
                eng.wait_ge(land_more[u], it * 16 + 16)

            for s in (first, more):
                for name in STARTED:
                    pe.sem_inc(s[name], 1)
            pe.sem_inc(more["used"], UPQ)
            with pe.Fori(0, NQ) as q:
                quad(q, first, landed_first)
            pe.wait_ge(count_made, 1)
            extra = pe.value_load(cnt[0:1, 0:1], min_val=0, max_val=7)
            with pe.If(extra > 0):
                with pe.Fori(0, extra) as r:
                    with pe.Fori(0, NQ) as q:
                        quad(r * NQ + q, more, landed_more)

            pe.wait_ge(land_b2, 16 * 3)
            for g in range(NH):
                ins = nc.tensor.transpose(ps[:, 4 + g // 4, (g % 4) * P:(g % 4 + 1) * P], spraw[:, g, :], ident)
            ins.then_inc(spT_ps, 1)
            pe.wait_ge(x2_made, 2 * T + 4)
            pe.wait_ge(spT_made, 1)
            transposes(X, 4, xT_ps)
            pe.wait_ge(xT_made, 4)

            def proj2(j):
                token_unit(S1 + j, 16 + j // 2, KU * (j % 2), xT_hi, xT_lo)

            def rope_transposes(which):
                pe.wait_ge(rope_made, which + 1)
                for t in range(T):
                    for p in range(PAIRS):
                        ins = nc.tensor.transpose(ps[:, 4 + 2 * which + t, p * P:(p + 1) * P],
                                                  qk[:, which, t, p * P:(p + 1) * P], ident)
                ins.then_inc(rT_ps, 1)

            def score_step(p):
                if p == 0:
                    pe.wait_ge(rT_made, 2)
                else:
                    pe.wait_ge(pT_made, p)
                for h in range(2):
                    row = slice(HD * h, HD * h + HD)
                    o = ps[:, 4 + h, :]
                    mm(o[:, 0:P], qkT[row, 1, p, 0:P], qkT[row, 0, p, 0:P], start=True, stop=False,
                       skip_group_check=True)
                    mm(o[:, P:P + SEQ], qkT[row, 1, p, P:SEQ], qkT[row, 0, p, :], start=False, stop=False,
                       skip_group_check=True)
                for h in range(2):
                    o = ps[:, 4 + h, :]
                    mm(o[:, 0:P], ident_b, mask2_b, start=False, stop=False, skip_group_check=True)
                    last = mm(o[:, SEQ:SEQ + P], ident_b, mask2_b, start=False, stop=True, skip_group_check=True)
                last.then_inc(s_ps, 1)

            def prob_transposes(p):
                pe.wait_ge(p_made, 4 * (p + 1))
                for h in range(2):
                    for j in range(3):
                        ins = nc.tensor.transpose(ps[:, 4 + h, j * P:(j + 1) * P],
                                                  prob[:, p % 2, h, j * P:(j + 1) * P], ident)
                ins.then_inc(pT_ps, 1)

            def out_step(p):
                pe.wait_ge(pT_made, p + 1)
                if p == 0:
                    pe.wait_ge(v2_made, 1)
                for h in range(2):
                    head = slice((2 * p + h) * HD, (2 * p + h + 1) * HD)
                    w = pT[:, p % 2, h, :]
                    mm(ps[:, 6, head], w[:, 0:P], v[:, 0, head], start=True, stop=True)
                    mm(ps[:, 7, head], w[:, P:SEQ], v[:, 0, head], start=True, stop=False)
                    last = mm(ps[:, 7, head], w[:, SEQ:SEQ + P], v[:, 1, head], start=False, stop=True)
                last.then_inc(o_ps, 1)

            for j in range(4):
                proj2(j)
            rope_transposes(0)
            proj2(4)
            proj2(5)
            rope_transposes(1)
            proj2(6)
            score_step(0)
            proj2(7)
            prob_transposes(0)
            proj2(8)
            out_step(0)
            score_step(1)
            proj2(9)
            prob_transposes(1)
            out_step(1)
            score_step(2)
            pe.wait_ge(pair_free[1], 10)
            pe.wait_ge(z_made, 1)
            for g in range(NH):
                for t in range(T):
                    last = mm(ps[:, 2 + t, g * HD:(g + 1) * HD], spT[:, g, :], zz[:, t, g * HD:(g + 1) * HD],
                              start=True, stop=True)
            last.then_inc(mix_ps, 1)
            prob_transposes(2)
            out_step(2)
            score_step(3)
            prob_transposes(3)
            out_step(3)
            pe.wait_ge(cat_made, 4)
            pe.wait_ge(o_made, 1)
            transposes(gcat, 4, gT_ps)
            pe.wait_ge(gT_made, 4)
            for h in range(2):
                for kh in range(2):
                    token_unit(S1 + 10 + 2 * h + kh, 22 + h, KU * kh, gT_hi, gT_lo)
            pe.wait_ge(x3_made, T)
            transposes(X, 4, x3T_ps)
            pe.wait_ge(x3T_made, 4)

            def ffn_up(i, c, kind, turn=None):
                off = 0 if turn is None else turn * RING
                done = c - 1 if turn is None else turn * LOOP_B + (c - 1)
                if c >= 2:
                    pe.wait_ge((sil2_made, hid_made)[kind], done)
                pe.wait_ge(lo_made, off + (i + 1))
                hi = w_hi[:, i % 2, :].rearrange("p (k n) -> p k n", k=KD)
                lo = w_lo[:, i % 2, :].rearrange("p (k n) -> p k n", k=KD)
                for m in range(MF):
                    o = ps[:, 4 + 2 * (c % 2) + kind, m * SEQ:(m + 1) * SEQ]
                    for k in range(KD):
                        col = slice(m * P, (m + 1) * P)
                        last = mm3(o, hi[:, k, col], lo[:, k, col], xT_hi[:, k, :], xT_lo[:, k, :],
                                   start=(k == 0 and m == 0), stop=(k == KD - 1))
                last.then_inc(unit_used, 1)

            def ffn_down(i, c, turn=None):
                off = 0 if turn is None else turn * RING
                done = c + 1 if turn is None else turn * LOOP_B + (c + 1)
                pe.wait_ge(hidT_made, done)
                pe.wait_ge(lo_made, off + (i + 1))
                hi = w_hi[:, i % 2, :].rearrange("p (m n) -> p m n", m=MF)
                lo = w_lo[:, i % 2, :].rearrange("p (m n) -> p m n", m=MF)
                for t in range(T):
                    tok = slice(t * P, (t + 1) * P)
                    for m in range(MF):
                        for h in range(2):
                            last = mm3(ps[:, 2 * t + h, :], hid_hi[:, m, tok], hid_lo[:, m, tok],
                                       hi[:, m, h * 512:(h + 1) * 512], lo[:, m, h * 512:(h + 1) * 512],
                                       start=(c == 0 and m == 0), stop=False)
                last.then_inc(unit_used, 1)

            def ffn_body(c, turn=None):
                i = body_unit(c)
                ffn_up(i, c, 0, turn)
                ffn_up(i + 1, c, 1, turn)
                ffn_down(i + 2, c - 1, turn)

            ffn_up(SFF, 0, 0)
            ffn_up(SFF + 1, 0, 1)
            ffn_body(1)
            with pe.Fori(0, LOOP_N) as turn:
                for c in range(2, 2 + LOOP_B):
                    ffn_body(c, turn)
            ffn_body(NCH - 1)
            ffn_down(body_unit(NCH), NCH - 1)

        @block.scalar
        def _(act):
            own = [0]

            def step(ins):
                own[0] += 1
                ins.then_inc(act_own, 1)
                act.wait_ge(act_own, own[0])

            def copy(o, i):
                return nc.scalar.activation(o, i, ACT.Copy)

            junk = [sq[:].rearrange("p t w -> p (t w)"), full[:, 0:2, :].rearrange("p b n -> p (b n)")]

            def small(dst, src):
                act.dma_start(dst, src).then_inc(land_small, 16)

            small(cst[:], consts)
            small(g1, norm_mix_g[0].rearrange("(p k) -> p k", k=KD))
            small(g2, norm_ffn_g[0].rearrange("(p k) -> p k", k=KD))
            for h in range(2):
                small(gq[HD * h:HD * h + HD, :], q_norm_g[0].rearrange("(d o) -> d o", o=1))
                small(gk[HD * h:HD * h + HD, :], k_norm_g[0].rearrange("(d o) -> d o", o=1))
            small(wr[:, :, 0:NG], w_router_group[0].rearrange("(p k) n -> p k n", k=KD))
            small(wr[:, :, NG:NG + NE], w_router_expert[0].rearrange("(p k) n -> p k n", k=KD))
            small(rbias[:, 0:NG], b_router_group[0].partition_broadcast(P))
            small(rbias[:, NG:NG + NE], b_router_expert[0].partition_broadcast(P))
            small(gmix[0:HD, :], attn_out_g_2[0].rearrange("(p k) -> p k", k=KD))
            small(gmix[HD:P, :], gmlp_out_g_2[0].rearrange("(p k) -> p k", k=KD))
            with nc.allow_non_contiguous_dma(reason="a few hundred gains"):
                small(bsp, b_spatial_2[0].rearrange("g i -> i g"))
                act.dma_start(cw, conv_w[0].rearrange("j (m p) -> p j m", p=P)).then_inc(land_taps, 16)

            def rsqrt(y, ss, n, eps, done):
                step(nc.scalar.activation(y, ss, ACT.Ln, scale=1.0 / n, bias=eps))
                nc.scalar.activation(y, y, ACT.Exp, scale=-0.5).then_inc(done, 1)

            def hi(i):
                slot, value = slot_of(load_of(i))
                act.wait_ge(land[slot], value)
                if i >= 2:
                    act.wait_ge(unit_used, i - 1)
                copy(w_hi[:, i % 2, :], ring[:, slot, :]).then_inc(hi_made, 1)

            for t in range(T):
                act.wait_ge(land_x[t], 16)
                nc.scalar.activation(junk[t], X[:, t, :], ACT.Square, accum_out=ss1[:, t:t + 1]).then_inc(x_sq, 1)
            act.wait_ge(x_sq, T)
            rsqrt(y1, ss1, D, RMS_EPS, y1_made)
            act.wait_ge(land_small, 16 * N_SMALL)
            for j, c in enumerate((C_ID, C_MK1, C_MK2)):
                last = copy(bfc[:, j, :], cst[:, c:c + P])
            last.then_inc(bf_made, 1)
            hi(0)
            for b in range(4):
                t, k0 = b // 2, 4 * (b % 2)
                act.wait_ge(full_made, b + 1)
                copy(hT_hi[:, k0:k0 + 4, t * P:(t + 1) * P],
                     full[:, b, :].rearrange("p (k n) -> p k n", k=4)).then_inc(hThi_made, 1)
            hi(1)
            hi(2)

            def qk_square(which):
                act.wait_ge(unit_used, 2 * which + 2)
                if which == 1:
                    act.wait_ge(qk_ss, 1)
                nc.scalar.activation(sq[:].rearrange("p t w -> p (t w)"),
                                     ps[:, 2 * which:2 * which + 2, :].rearrange("p t w -> p (t w)"),
                                     ACT.Square).then_inc(qk_sq, 1)
                act.wait_ge(qk_ss, which + 1)
                rsqrt((yk, yq)[which], (ssk, ssq)[which], HD, RMS_EPS, qk_y)

            def qkT_copy(which):
                act.wait_ge(qkT_ps, which + 1)
                for t in range(T):
                    last = nc.scalar.activation(
                        qkT[:, which, :, t * P:(t + 1) * P],
                        ps[:, 4 + 2 * which + t, :].rearrange("p (a n) -> p a n", a=PAIRS), ACT.Identity,
                        scale=(gk, gq)[which])
                last.then_inc(qkT_made, 1)

            def chunk_done(c):
                act.wait_ge(unit_used, 2 * c + 2)

            def two_banks(c):
                return ps[:, 2 * (c % 2):2 * (c % 2) + 2, :].rearrange("p b n -> p (b n)")

            def log1p_step(p):
                act.wait_ge(z_ps, p + 1)
                if p >= 1:
                    act.wait_ge(la_ps, p)
                b = 4 + 2 * (p % 2)
                step(nc.scalar.activation(stick[:], ps[:, b:b + 2, 0:384], ACT.Abs))
                step(nc.scalar.activation(stick[:], stick[:], ACT.Exp, scale=-1.0))
                nc.scalar.activation(stick[:], stick[:], ACT.Ln, bias=1.0).then_inc(log_made, 1)

            def attw_step(p):
                act.wait_ge(la_ps, p + 1)
                if p >= 1:
                    act.wait_ge(av_ps, p)
                b = 4 + 2 * (p % 2)
                nc.scalar.activation(attw[:], ps[:, b:b + 2, 0:384], ACT.Exp).then_inc(attw_made, 1)

            def brhi_step(p):
                act.wait_ge(av_ps, p + 1)
                copy(brT_hi[:, 0, p, :], ps[:, 4 + 2 * (p % 2), 0:SEQ]).then_inc(brhi_made, 1)

            hi(3)
            qk_square(0)
            hi(4)
            hi(5)
            qk_square(1)
            qkT_copy(0)
            hi(6)
            qkT_copy(1)
            hi(7)
            chunk_done(CH_V)
            copy(v[:].rearrange("p t w -> p (t w)"), two_banks(CH_V)).then_inc(pair_free[0], 1)
            act.wait_ge(pair_free[0], 2)
            nc.scalar.nop().then_inc(v_made, 1)
            hi(8)
            log1p_step(0)
            hi(9)
            chunk_done(CH_GA)
            copy(ga[:, 0:4, :].rearrange("p m n -> p (m n)"), two_banks(CH_GA)).then_inc(pair_free[1], 1)
            attw_step(0)
            log1p_step(1)
            hi(10)
            brhi_step(0)
            attw_step(1)
            hi(11)
            chunk_done(CH_GA + 1)
            copy(ga[:, 4:8, :].rearrange("p m n -> p (m n)"), two_banks(CH_GA + 1)).then_inc(pair_free[0], 1)
            brhi_step(1)
            log1p_step(2)
            hi(12)
            attw_step(2)
            log1p_step(3)
            hi(13)
            brhi_step(2)
            attw_step(3)
            hi(14)
            brhi_step(3)
            chunk_done(CH_CC)
            act.wait_ge(av_ps, PAIRS)
            copy(cu[:].rearrange("p m n -> p (m n)"), two_banks(CH_CC)).then_inc(cc_made, 1)
            act.wait_ge(cc_made, 1)
            nc.scalar.nop().then_inc(pair_free[1], 1)
            act.wait_ge(pair_free[0], 3)
            nc.scalar.activation(ga[:], ga[:], ACT.Sigmoid).then_inc(ga_sig, 1)
            hi(15)
            hi(16)
            hi(17)
            act.wait_ge(conv_made, 1)
            copy(brT_hi[:, 1], cy[:]).then_inc(convhi_made, 1)
            hi(18)
            hi(19)
            for h in range(2):
                chunk_done(CH_GB + h)
                nc.scalar.activation(gb[:, 4 * h:4 * h + 4, :].rearrange("p m n -> p (m n)"), two_banks(CH_GB + h),
                                     ACT.Sigmoid).then_inc(pair_free[h], 1)
                hi(20 + h)
            act.wait_ge(pair_free[1], 5)
            act.wait_ge(pair_free[0], 5)
            nc.scalar.nop().then_inc(gb_sig, 1)
            hi(22)
            for h in range(2):
                hi(23 + 2 * h)
                act.wait_ge(mg_made, h + 1)
                copy(mgT_hi[:, 4 * h:4 * h + 4, :], mg1[:]).then_inc(mghi_made, 1)
                hi(24 + 2 * h)
            hi(27)

            for t in range(T):
                act.wait_ge(x2_made, T + 1 + t)
                nc.scalar.activation(junk[t], X[:, t, :], ACT.Square, accum_out=ss2[:, t:t + 1]).then_inc(x2_sq, 1)
            act.wait_ge(x2_sq, T)
            rsqrt(y2, ss2, D, RMS_EPS, y2_made)
            for j in range(2):
                act.wait_ge(gdiff_made, j + 1)
                buf = rt[:, 64:72] if j == 0 else rt[:, 72:74]
                nc.scalar.activation(buf, buf, ACT.Exp).then_inc(gexp_made, 1)

            def quad(it, s):
                act.wait_ge(s["gath_ps"], it + 2)
                copy(pickT[:].rearrange("p t n -> p (t n)"), ps[:, 5, 0:T * P]).then_inc(s["pickT_made"], 1)
                act.wait_ge(s["used"], it * UPQ + (4 + s["start"]))
                act.wait_ge(s["act_made"], it + 1)
                nc.scalar.activation(sil[:], ps[:, 4, 0:FE], ACT.Silu).then_inc(s["sil_made"], 1)
                act.wait_ge(s["aT_ps"], it + 1)
                copy(actT[:].rearrange("p k n -> p (k n)"), ps[:, 4, FE:2 * FE]).then_inc(s["actT_made"], 1)
                act.wait_ge(s["used"], it * UPQ + (UPQ + s["start"]))
                copy(ysb[:, 0:512], ps[:, 6, :]).then_inc(s["y_made"], 1)

            with act.Fori(0, NQ) as q:
                quad(q, first | {"start": 0})
            act.wait_ge(count_made, 1)
            extra = act.value_load(cnt[0:1, 0:1], min_val=0, max_val=7)
            with act.If(extra > 0):
                with act.Fori(0, extra) as r:
                    with act.Fori(0, NQ) as q:
                        quad(r * NQ + q, more | {"start": UPQ})
            act.wait_ge(more["spread"], extra * NQ + 1)

            act.wait_ge(first["spread"], NQ + 1)
            for h in range(2):
                copy(X[:, 0, h * 512:(h + 1) * 512], ps[:, h, :]).then_inc(x2_made, 1)
            for i in range(S1, S1 + 2):
                hi(i)
            for b in range(4):
                t, k0 = b // 2, 4 * (b % 2)
                act.wait_ge(xT_ps, b + 1)
                copy(xT_hi[:, k0:k0 + 4, t * P:(t + 1) * P],
                     ps[:, 4 + b, :].rearrange("p (k n) -> p k n", k=4)).then_inc(xThi_made, 1)

            def rT_copy(which):
                act.wait_ge(rT_ps, which + 1)
                for t in range(T):
                    last = copy(qkT[:, which, :, t * P:(t + 1) * P],
                                ps[:, 4 + 2 * which + t, :].rearrange("p (a n) -> p a n", a=PAIRS))
                last.then_inc(rT_made, 1)

            def exp_step(p):
                act.wait_ge(mx_made, p + 1)
                if p >= 2:
                    act.wait_ge(pT_ps, p - 1)
                for h in range(2):
                    for t in range(T):
                        a, b = (0, P) if t == 0 else (P, P + SEQ)
                        head = 2 * p + h
                        nc.scalar.activation(prob[:, p % 2, h, a:b], ps[:, 4 + h, a:b], ACT.Exp,
                                             bias=mxn[:, head, t:t + 1], scale=HD ** -0.5,
                                             accum_out=rsum[:, head, t:t + 1]).then_inc(p_made, 1)

            def pT_copy(p):
                act.wait_ge(pT_ps, p + 1)
                if p >= 2:
                    act.wait_ge(o_ps, p - 1)
                copy(pT[:, p % 2], ps[:, 4:6, 0:384]).then_inc(pT_made, 1)

            def chunk2_done(j):
                act.wait_ge(unit_used, S1 + 2 * j + 2)

            for i in range(S1 + 2, S1 + 6):
                hi(i)
            rT_copy(0)
            hi(S1 + 6)
            rT_copy(1)
            chunk2_done(2)
            copy(v[:].rearrange("p t w -> p (t w)"), two_banks(18)).then_inc(v2_made, 1)
            act.wait_ge(v2_made, 1)
            nc.scalar.nop().then_inc(pair_free[0], 1)
            hi(S1 + 7)
            hi(S1 + 8)
            exp_step(0)
            hi(S1 + 9)
            chunk2_done(3)
            nc.scalar.activation(zz[:].rearrange("p t w -> p (t w)"), two_banks(19), ACT.Gelu).then_inc(zg_made, 1)
            act.wait_ge(zg_made, 1)
            nc.scalar.nop().then_inc(pair_free[1], 1)
            pT_copy(0)
            hi(S1 + 10)
            exp_step(1)
            act.wait_ge(zc_made, 1)
            nc.scalar.activation(sq[:], zz[:], ACT.Square).then_inc(zq_made, 1)
            act.wait_ge(zss_made, 1)
            rsqrt(zy, zs, HD, LN_EPS, zy_made)
            pT_copy(1)
            hi(S1 + 11)
            exp_step(2)
            pT_copy(2)
            exp_step(3)
            pT_copy(3)
            chunk2_done(4)
            nc.scalar.activation(uu[:].rearrange("p t w -> p (t w)"), two_banks(20), ACT.Gelu).then_inc(u_made, 1)
            act.wait_ge(u_made, 1)
            nc.scalar.nop().then_inc(pair_free[0], 1)
            for b, made in enumerate((o_made, sg_made)):
                act.wait_ge(made, 1)
                for t in range(T):
                    nc.scalar.activation(full[:, 2 * b + t, :], (atto, zz)[b][:, t, :], ACT.Square,
                                         accum_out=ssg[:, 2 * b + t:2 * b + t + 1]).then_inc(cat_sq, 1)
                act.wait_ge(cat_sq, T * (b + 1))
                rsqrt(yg[:, 2 * b:2 * b + 2], ssg[:, 2 * b:2 * b + 2], W, RMS_EPS, cat_y)
            for b in range(4):
                t, k0 = b // 2, 4 * (b % 2)
                act.wait_ge(gfull_made, b + 1)
                copy(gT_hi[:, k0:k0 + 4, t * P:(t + 1) * P],
                     full[:, b, :].rearrange("p (k n) -> p k n", k=4)).then_inc(gThi_made, 1)
            act.wait_ge(gT_made, 4)
            for i, g in enumerate((ln1_g_2, ln1_b_2)):
                act.dma_start(ln1[:, i, :], g[0].partition_broadcast(P)).then_inc(land_ln1, 16)
            for i, g in enumerate((ln2_g_2, ln2_b_2)):
                act.dma_start(ln2[:, i, :], g[0].partition_broadcast(P)).then_inc(land_ln2, 16)
            hi(S1 + 12)
            hi(S1 + 13)
            hi(SFF)
            hi(SFF + 1)
            for t in range(T):
                act.wait_ge(var_made, t + 1)
                rsqrt(yl[:, t:t + 1], mv[:, t, 1:2], 1, LN_EPS, yl_made)
            for b in range(4):
                t, k0 = b // 2, 4 * (b % 2)
                act.wait_ge(x3T_ps, b + 1)
                copy(xT_hi[:, k0:k0 + 4, t * P:(t + 1) * P],
                     ps[:, 4 + b, :].rearrange("p (k n) -> p k n", k=4)).then_inc(x3Thi_made, 1)

            def hi_in(i, turn):
                if turn is None:
                    return hi(i)
                slot, value = slot_of(load_of(i))
                act.wait_ge(land[slot], turn * 16 + value)
                act.wait_ge(unit_used, turn * RING + (i - 1))
                copy(w_hi[:, i % 2, :], ring[:, slot, :]).then_inc(hi_made, 1)

            def ffn_hidden(c, turn, between):
                n = c if turn is None else turn * LOOP_B + c
                u = SFF + 1 if c == 0 else body_unit(c)
                act.wait_ge(unit_used, (u if c == 0 else u + 1) if turn is None else turn * RING + (u + 1))
                if c >= 1:
                    act.wait_ge(hid_made, n)
                nc.scalar.activation(sil2[:].rearrange("p m n -> p (m n)"), ps[:, 4 + 2 * (c % 2), :],
                                     ACT.Silu).then_inc(sil2_made, 1)
                between()
                act.wait_ge(hid_made, n + 1)
                if c == NCH - 1:
                    act.wait_ge(unit_used, body_unit(c) + 3)
                copy(hid_hi[:], hid[:]).then_inc(hidhi_made, 1)

            def ffn_body(c, turn=None):
                i = body_unit(c)
                if i >= SFF + 2:
                    hi_in(i, turn)
                ffn_hidden(c - 1, turn, lambda: hi_in(i + 1, turn))
                hi_in(i + 2, turn)

            ffn_body(1)
            with act.Fori(0, LOOP_N) as turn:
                for c in range(2, 2 + LOOP_B):
                    ffn_body(c, turn)
            ffn_body(NCH - 1)
            ffn_hidden(NCH - 1, None, lambda: hi(body_unit(NCH)))
            for t in range(T):
                act.wait_ge(var_made, T + t + 1)
                rsqrt(yl[:, t:t + 1], mv[:, t, 1:2], 1, LN_EPS, yl_made)

        @block.vector
        def _(dve):
            tt, ts, stt = nc.vector.tensor_tensor, nc.vector.tensor_scalar, nc.vector.scalar_tensor_tensor
            red = nc.vector.tensor_reduce
            own = [0]

            def step(ins):
                own[0] += 1
                ins.then_inc(dve_own, 1)
                dve.wait_ge(dve_own, own[0])

            def f32(ap):
                return ap.bitcast(F32)

            def refine(y, ss, n, eps):
                k = y.shape[1]
                a, b = nw[:, 0, 0:k], nw[:, 1, 0:k]
                ts(a, ss, 1.0 / n, eps, ALU.mult, ALU.add)
                step(tt(b, y, y, ALU.mult))
                step(tt(a, a, b, ALU.mult))
                step(ts(a, a, -0.5, 1.5, ALU.mult, ALU.add))
                step(tt(y, y, a, ALU.mult))

            def lo(i):
                slot, _ = slot_of(load_of(i))
                dve.wait_ge(hi_made, i + 1)
                tt(w_lo[:, i % 2, :], ring[:, slot, :], f32(w_hi[:, i % 2, :]), ALU.subtract).then_inc(lo_made, 1)

            def bc(ap, n):
                return ap.unsqueeze(2).to_broadcast([ap.shape[0], ap.shape[1], n])

            dve.wait_ge(y1_made, 1)
            refine(y1, ss1, D, RMS_EPS)
            for t in range(T):
                ts(xn[:, t, :], X[:, t, :], y1[:, t:t + 1], None, ALU.mult).then_inc(xn_made, 1)
            dve.wait_ge(land_small, 16 * N_SMALL)

            def scaled_split(b, arrived, g, made, hi_ready, dst_hi, dst_lo, split, bank):
                dve.wait_ge(arrived, b + 1)
                k0 = 4 * (b % 2)
                tt(full[:, b, :].rearrange("p (k n) -> p k n", k=4),
                   ps[:, bank + b, :].rearrange("p (k n) -> p k n", k=4), bc(g[:, k0:k0 + 4], P),
                   ALU.mult).then_inc(made, 1)

            def lower_split(b, hi_ready, dst_hi, dst_lo, split):
                t, k0 = b // 2, 4 * (b % 2)
                dve.wait_ge(hi_ready, b + 1)
                tok = slice(t * P, (t + 1) * P)
                tt(dst_lo[:, k0:k0 + 4, tok], full[:, b, :].rearrange("p (k n) -> p k n", k=4),
                   f32(dst_hi[:, k0:k0 + 4, tok]), ALU.subtract).then_inc(split, 1)

            for b in range(4):
                scaled_split(b, hT_ps, g1, full_made, hThi_made, hT_hi, hT_lo, hT_made, 0)
            for b in range(4):
                lower_split(b, hThi_made, hT_hi, hT_lo, hT_made)
            ts(gq, gq, HD ** -0.5, None, ALU.mult).then_inc(dve_own, 1)
            own[0] += 1
            for i in range(3):
                lo(i)

            def qk_norm(which):
                dve.wait_ge(qk_sq, which + 1)
                y, ss = (yk, yq)[which], (ssk, ssq)[which]
                red(ss, sq[:].rearrange("p t (h d) -> p (t h) d", d=HD), AX, ALU.add).then_inc(qk_ss, 1)
                dve.wait_ge(qk_y, which + 1)
                refine(y, ss, HD, RMS_EPS)
                tt(qk[:, which].rearrange("p t (h d) -> p (t h) d", d=HD),
                   ps[:, 2 * which:2 * which + 2, :].rearrange("p t (h d) -> p (t h) d", d=HD), bc(y, HD),
                   ALU.mult).then_inc(qk_made, 1)
                dve.wait_ge(qk_made, which + 1)
                nc.vector.engine_nop().then_inc(pair_free[which], 1)

            def zb(p):
                return ps[:, 4 + 2 * (p % 2):6 + 2 * (p % 2), 0:384]

            def sp_step(p):
                dve.wait_ge(log_made, p + 1)
                stt(stick[:], zb(p), 0.0, stick[:], ALU.max, ALU.add).then_inc(sp_made, 1)

            def brlo_step(p):
                dve.wait_ge(brhi_made, p + 1)
                tt(brT_lo[:, 0, p, :], ps[:, 4 + 2 * (p % 2), 0:SEQ], f32(brT_hi[:, 0, p, :]),
                   ALU.subtract).then_inc(br_made, 1)

            lo(3)
            qk_norm(0)
            lo(4)
            lo(5)
            qk_norm(1)
            lo(6)
            lo(7)
            lo(8)
            sp_step(0)
            lo(9)
            sp_step(1)
            lo(10)
            brlo_step(0)
            lo(11)
            brlo_step(1)
            sp_step(2)
            lo(12)
            sp_step(3)
            lo(13)
            brlo_step(2)
            lo(14)
            brlo_step(3)
            lo(15)

            def banks4(c):
                return ps[:, 2 * (c % 2):2 * (c % 2) + 2, :].rearrange("p b (m n) -> p (b m) n", n=SEQ)

            dve.wait_ge(land_taps, 16)
            dve.wait_ge(cc_made, 1)
            dve.wait_ge(unit_used, 2 * CH_CU + 2)
            tt(cu[:], banks4(CH_CU), cu[:], ALU.mult).then_inc(pair_free[0], 1)
            dve.wait_ge(pair_free[0], 4)
            for m in range(4):
                ts(cy[:, m, :], cu[:, m, :], cw[:, 2, m:m + 1], None, ALU.mult).then_inc(dve_own, 1)
            own[0] += 4
            dve.wait_ge(dve_own, own[0])
            lo(16)
            for j in (1, 0):
                off = 2 - j
                for m in range(4):
                    stt(cy[:, m, off:SEQ], cu[:, m, 0:SEQ - off], cw[:, j, m:m + 1], cy[:, m, off:SEQ], ALU.mult,
                        ALU.add).then_inc(dve_own, 1)
                own[0] += 4
                dve.wait_ge(dve_own, own[0])
            lo(17)
            dve.wait_ge(unit_used, 2 * CH_CB + 2)
            tt(cy[:], banks4(CH_CB), cy[:], ALU.mult).then_inc(conv_made, 1)
            dve.wait_ge(conv_made, 1)
            nc.vector.engine_nop().then_inc(pair_free[1], 1)
            dve.wait_ge(convhi_made, 1)
            tt(brT_lo[:, 1], cy[:], f32(brT_hi[:, 1]), ALU.subtract).then_inc(conv_split, 1)
            for i in range(18, 23):
                lo(i)
            dve.wait_ge(ga_sig, 1)
            dve.wait_ge(gb_sig, 1)
            for h in range(2):
                m4 = slice(4 * h, 4 * h + 4)
                dve.wait_ge(unit_used, 21 + 2 * h)
                if h == 1:
                    dve.wait_ge(mgT_made, 1)
                tt(mg1[:], banks4(10 + 2 * h), ga[:, m4, :], ALU.mult).then_inc(pair_free[0], 1)
                lo(23 + 2 * h)
                dve.wait_ge(unit_used, 22 + 2 * h)
                tt(mg2[:], banks4(11 + 2 * h), gb[:, m4, :], ALU.mult).then_inc(pair_free[1], 1)
                dve.wait_ge(pair_free[0], 6 + h)
                dve.wait_ge(pair_free[1], 6 + h)
                tt(mg1[:], mg1[:], mg2[:], ALU.add).then_inc(mg_made, 1)
                dve.wait_ge(mghi_made, h + 1)
                tt(mgT_lo[:, m4, :], mg1[:], f32(mgT_hi[:, m4, :]), ALU.subtract).then_inc(mgT_made, 1)
                lo(24 + 2 * h)
            lo(27)
            for h in range(2):
                dve.wait_ge(unit_used, 26 + 2 * h)
                for t in range(T):
                    tt(X[:, t, h * 512:(h + 1) * 512], ps[:, 2 * h + t, :], X[:, t, h * 512:(h + 1) * 512],
                       ALU.add).then_inc(x2_made, 1)
                dve.wait_ge(x2_made, T * (h + 1))
                nc.vector.engine_nop().then_inc(pair_free[h], 1)

            dve.wait_ge(y2_made, 1)
            refine(y2, ss2, D, RMS_EPS)
            for t in range(T):
                ts(h2n[:, t, :], X[:, t, :], y2[:, t:t + 1], None, ALU.mult).then_inc(h2n_made, 1)
            for b in range(4):
                t, k0 = b // 2, 4 * (b % 2)
                dve.wait_ge(h2T_ps, b + 1)
                tt(h2T[:, k0:k0 + 4, t * P:(t + 1) * P], ps[:, 4 + b, :].rearrange("p (k n) -> p k n", k=4),
                   bc(g2[:, k0:k0 + 4], P), ALU.mult).then_inc(h2T_made, 1)

            pos = [0]

            def cell(n):
                a = pos[0]
                pos[0] += n
                return rt[:, a:a + n]

            def tg(ap, n):
                return ap.rearrange("p (t n) -> p t n", n=n)

            assign = cell(T * NE)
            gexp = cell(T * NG)
            eexp = cell(T)
            comb = cell(T * NE)
            place = cell(T * NE)
            logits = tg(cell(T * 36), 36)
            goh, gtmp = tg(cell(T * NG), NG), tg(cell(T * NG), NG)
            egrp, emask = tg(cell(T * EPG), EPG), tg(cell(T * EPG), EPG)
            oh1, oh2, etmp = (tg(cell(T * EPG), EPG) for _ in range(3))
            prod = cell(T * NE)
            gmax, gi, gsum, m1, m2, i1, den, wt1, wt2, gw = (cell(T) for _ in range(10))
            counts, over = cell(1), cell(8)
            i8 = iota[:, 0:EPG].unsqueeze(1).to_broadcast([P, T, EPG])
            i4 = iota[:, 0:NG].unsqueeze(1).to_broadcast([P, T, NG])

            def first_max(vals, n, mxv, idx, onehot, tmp, iot):
                step(red(mxv, vals, AX, ALU.max))
                step(tt(tmp, vals, bc(mxv, n), ALU.is_ge))
                step(stt(tmp, tmp, -64.0, iot, ALU.mult, ALU.add))
                step(red(idx, tmp, AX, ALU.min))
                step(tt(onehot, tmp, bc(idx, n), ALU.is_equal))

            dve.wait_ge(logit_ps, 1)
            step(tt(logits, ps[:, 6, 0:T * 36].rearrange("p (t n) -> p t n", t=T),
                    rbias.unsqueeze(1).to_broadcast([P, T, 36]), ALU.add))
            lg = logits[:, :, 0:NG]
            first_max(lg, NG, gmax, gi, goh, gtmp, i4)
            tt(tg(gexp, NG), lg, bc(gmax, NG), ALU.subtract).then_inc(gdiff_made, 1)
            for t in range(T):
                tt(prod[:, t * NE:(t + 1) * NE].rearrange("p (g e) -> p g e", g=NG),
                   logits[:, t, NG:NG + NE].rearrange("p (g e) -> p g e", g=NG),
                   bc(goh[:, t, :], EPG), ALU.mult).then_inc(dve_own, 1)
            own[0] += T
            dve.wait_ge(dve_own, own[0])
            step(red(egrp, prod.rearrange("p (t g e) -> p t e g", t=T, g=NG), AX, ALU.add))
            first_max(egrp, EPG, m1, i1, oh1, etmp, i8)
            step(stt(emask, oh1, -3e38, egrp, ALU.mult, ALU.add))
            first_max(emask, EPG, m2, i1, oh2, etmp, i8)
            tt(eexp, m2, m1, ALU.subtract).then_inc(gdiff_made, 1)
            step(tt(etmp, oh1, oh2, ALU.add))
            for t in range(T):
                ins = tt(assign[:, t * NE:(t + 1) * NE].rearrange("p (g e) -> p g e", g=NG), bc(goh[:, t, :], EPG),
                         etmp[:, t, :].unsqueeze(1).to_broadcast([P, NG, EPG]), ALU.mult)
                step(ins)
            nc.vector.engine_nop().then_inc(assign_made, 1)
            dve.wait_ge(gexp_made, 2)
            step(red(gsum, tg(gexp, NG), AX, ALU.add))
            step(nc.vector.reciprocal(gw, gsum))
            step(ts(den, eexp, 1.0, None, ALU.add))
            step(nc.vector.reciprocal(den, den))
            step(tt(wt1, den, gw, ALU.mult))
            step(tt(wt2, wt1, eexp, ALU.mult))
            step(tt(egrp, oh1, bc(wt1, EPG), ALU.mult))
            step(tt(emask, oh2, bc(wt2, EPG), ALU.mult))
            step(tt(egrp, egrp, emask, ALU.add))
            for t in range(T):
                step(tt(comb[:, t * NE:(t + 1) * NE].rearrange("p (g e) -> p g e", g=NG), bc(goh[:, t, :], EPG),
                        egrp[:, t, :].unsqueeze(1).to_broadcast([P, NG, EPG]), ALU.mult))
            dve.wait_ge(rank_ps, 1)
            step(stt(place, ps[:, 7, 0:T * NE], 1.0, assign, ALU.add, ALU.mult))
            step(ts(place, place, -1.0, None, ALU.add))
            step(red(counts, ps[:, 7, T * NE:T * NE + NE], AX, ALU.max))
            step(ts(over[:, 0:7], thr, counts, None, ALU.is_lt))
            step(red(over[:, 7:8], over[:, 0:7], AX, ALU.add))
            nc.vector.tensor_copy(cnt[:, 0:1], over[:, 7:8]).then_inc(count_made, 1)

            def quad(it, q, s, r=None):
                if r is not None:
                    dve.wait_ge(next_round, r + 1)
                dve.wait_ge(s["gath_ps"], it + 1)
                for t in range(T):
                    e = q * QUAD + t * NE
                    ins = tt(pick[:, t, :].rearrange("p (j c) -> p j c", j=QUAD),
                             iota.unsqueeze(1).to_broadcast([P, QUAD, CAP]),
                             place[:, bass.ds(e, QUAD)].unsqueeze(2).to_broadcast([P, QUAD, CAP]), ALU.is_equal)
                ins.then_inc(s["own"], 1)
                dve.wait_ge(s["own"], it + 1)
                for t in range(T):
                    e = q * QUAD + t * NE
                    ins = tt(pickw[:, t, :].rearrange("p (j c) -> p j c", j=QUAD),
                             pick[:, t, :].rearrange("p (j c) -> p j c", j=QUAD),
                             comb[:, bass.ds(e, QUAD)].unsqueeze(2).to_broadcast([P, QUAD, CAP]), ALU.mult)
                ins.then_inc(s["pick_made"], 1)
                dve.wait_ge(s["gath_ps"], it + 2)
                for b in range(2):
                    ins = tt(heT[:, 4 * b:4 * b + 4, :], ps[:, 6 + b, :].rearrange("p (k n) -> p k n", k=4),
                             bc(g2[:, 4 * b:4 * b + 4], P), ALU.mult)
                ins.then_inc(s["heT_made"], 1)
                dve.wait_ge(s["sil_made"], it + 1)
                dve.wait_ge(s["used"], it * UPQ + (8 + s["start"]))
                tt(act_e[:], ps[:, 5, 0:FE], sil[:], ALU.mult).then_inc(s["act_made"], 1)
                dve.wait_ge(s["used"], it * UPQ + (UPQ + s["start"]))
                nc.vector.tensor_copy(ysb[:, 512:1024], ps[:, 7, :]).then_inc(s["y_made"], 1)

            pick_own, pick_own2, next_round = sem("pick_own"), sem("pick_own2"), sem("next_round")
            with dve.Fori(0, NQ) as q:
                quad(q, q, first | {"start": 0, "own": pick_own})
            dve.wait_ge(count_made, 1)
            extra = dve.value_load(cnt[0:1, 0:1], min_val=0, max_val=7)
            with dve.If(extra > 0):
                with dve.Fori(0, extra) as r:
                    ts(place, place, -float(CAP), None, ALU.add).then_inc(next_round, 1)
                    with dve.Fori(0, NQ) as q:
                        quad(r * NQ + q, q, more | {"start": UPQ, "own": pick_own2}, r)
            dve.wait_ge(more["spread"], extra * NQ + 1)

            dve.wait_ge(first["spread"], NQ + 1)
            for h in range(2):
                nc.vector.tensor_copy(X[:, 1, h * 512:(h + 1) * 512], ps[:, 2 + h, :]).then_inc(x2_made, 1)
            dve.wait_ge(spT_ps, 1)
            tt(spT[:], ps[:, 4:6, :].rearrange("p b (g n) -> p (b g) n", n=P),
               triu.unsqueeze(1).to_broadcast([P, NH, P]), ALU.mult).then_inc(spT_made, 1)
            for i in range(S1, S1 + 2):
                lo(i)

            def lower_ps(b, hi_ready, split):
                t, k0 = b // 2, 4 * (b % 2)
                tok = slice(t * P, (t + 1) * P)
                dve.wait_ge(hi_ready, b + 1)
                tt(xT_lo[:, k0:k0 + 4, tok], ps[:, 4 + b, :].rearrange("p (k n) -> p k n", k=4),
                   f32(xT_hi[:, k0:k0 + 4, tok]), ALU.subtract).then_inc(split, 1)

            for b in range(4):
                lower_ps(b, xThi_made, xT_made)

            def rope(which):
                dve.wait_ge(unit_used, S1 + 2 * which + 2)
                if which:
                    dve.wait_ge(rope_made, 1)
                for t in range(T):
                    src = ps[:, 2 * (which % 2) + t, :].rearrange("p (h d) -> p h d", d=HD)
                    dst = qk[:, which, t, :].rearrange("p (h d) -> p h d", d=HD)
                    tmp = sq[:, t, :].rearrange("p (h d) -> p h d", d=HD)

                    def along(tab, a, b):
                        return tab[:, t, a:b].unsqueeze(1).to_broadcast([P, NH, b - a])

                    tt(dst, src, along(cos, 0, HD), ALU.mult)
                    tt(tmp[:, :, 0:HD // 2], src[:, :, HD // 2:HD], along(sin, 0, HD // 2), ALU.mult)
                    ins = tt(tmp[:, :, HD // 2:HD], src[:, :, 0:HD // 2], along(sin, HD // 2, HD), ALU.mult)
                ins.then_inc(pair_free[which], 1)
                dve.wait_ge(pair_free[which], 9)
                tt(qk[:, which], qk[:, which], sq[:], ALU.add).then_inc(rope_made, 1)

            def max_step(p):
                dve.wait_ge(s_ps, p + 1)
                red(mx[:, 2 * p:2 * p + 2, 0], ps[:, 4:6, 0:P], AX, ALU.max)
                step(red(mx[:, 2 * p:2 * p + 2, 1], ps[:, 4:6, P:P + SEQ], AX, ALU.max))
                ts(mxn[:, 2 * p:2 * p + 2, :], mx[:, 2 * p:2 * p + 2, :], -(HD ** -0.5), None,
                   ALU.mult).then_inc(mx_made, 1)

            lo(S1 + 2)
            lo(S1 + 3)
            rope(0)
            lo(S1 + 4)
            lo(S1 + 5)
            rope(1)
            for i in range(6, 9):
                lo(S1 + i)
            max_step(0)
            lo(S1 + 9)
            z3 = zz[:].rearrange("p t (g d) -> p (t g) d", d=HD)
            dve.wait_ge(zg_made, 1)
            step(red(zs, z3, AX, ALU.add))
            step(ts(zs, zs, 1.0 / HD, None, ALU.mult))
            tt(z3, z3, bc(zs, HD), ALU.subtract).then_inc(zc_made, 1)
            lo(S1 + 10)
            max_step(1)
            dve.wait_ge(zq_made, 1)
            red(zs, sq[:].rearrange("p t (g d) -> p (t g) d", d=HD), AX, ALU.add).then_inc(zss_made, 1)
            dve.wait_ge(zy_made, 1)
            refine(zy, zs, HD, LN_EPS)
            step(tt(z3, z3, bc(zy, HD), ALU.mult))
            dve.wait_ge(land_b2, 16 * 3)
            step(tt(zz[:], zz[:], lngb[:, 0, :].unsqueeze(1).to_broadcast([P, T, W]), ALU.mult))
            tt(zz[:], zz[:], lngb[:, 1, :].unsqueeze(1).to_broadcast([P, T, W]), ALU.add).then_inc(z_made, 1)
            lo(S1 + 11)
            max_step(2)
            max_step(3)
            dve.wait_ge(mix_ps, 1)
            for t in range(T):
                ins = tt(zz[:, t, :].rearrange("p (g d) -> p g d", d=HD),
                         ps[:, 2 + t, :].rearrange("p (g d) -> p g d", d=HD), bc(bsp, HD), ALU.add)
            ins.then_inc(pair_free[1], 1)
            dve.wait_ge(pair_free[1], 11)
            dve.wait_ge(u_made, 1)
            tt(zz[:], zz[:], uu[:], ALU.mult).then_inc(sg_made, 1)
            dve.wait_ge(p_made, 4 * PAIRS)
            step(nc.vector.reciprocal(rinv, rsum))
            dve.wait_ge(o_ps, PAIRS)
            for t in range(T):
                ins = tt(atto[:, t, :].rearrange("p (h d) -> p h d", d=HD),
                         ps[:, 6 + t, :].rearrange("p (h d) -> p h d", d=HD),
                         rinv[:, :, t:t + 1].to_broadcast([P, NH, HD]), ALU.mult)
            ins.then_inc(o_made, 1)
            for b in range(2):
                dve.wait_ge(cat_y, b + 1)
                refine(yg[:, 2 * b:2 * b + 2], ssg[:, 2 * b:2 * b + 2], W, RMS_EPS)
                for t in range(T):
                    ts(gcat[:, t, b * W:(b + 1) * W], (atto, zz)[b][:, t, :], yg[:, 2 * b + t:2 * b + t + 1], None,
                       ALU.mult).then_inc(cat_made, 1)
            for b in range(4):
                scaled_split(b, gT_ps, gmix, gfull_made, gThi_made, gT_hi, gT_lo, gT_made, 4)
            for b in range(4):
                lower_split(b, gThi_made, gT_hi, gT_lo, gT_made)
            lo(S1 + 12)
            lo(S1 + 13)

            def residual(h, t, bank):
                half = slice(h * 512, (h + 1) * 512)
                return stt(X[:, t, half], X[:, t, half], ALPHA, ps[:, bank, :], ALU.mult, ALU.add)

            def layer_norm(t, n, lnp, done):
                for c in range(2):
                    ins = nc.vector.bn_stats(bst[:, t, c, :], X[:, t, c * 512:(c + 1) * 512])
                step(ins)
                nc.vector.bn_aggr(mv[:, t, :], bst[:, t, :, :]).then_inc(var_made, 1)
                dve.wait_ge(yl_made, n + 1)
                refine(yl[:, t:t + 1], mv[:, t, 1:2], 1, LN_EPS)
                step(ts(X[:, t, :], X[:, t, :], mv[:, t, 0:1], yl[:, t:t + 1], ALU.subtract, ALU.mult))
                step(tt(X[:, t, :], X[:, t, :], lnp[:, 0, :], ALU.mult))
                tt(X[:, t, :], X[:, t, :], lnp[:, 1, :], ALU.add).then_inc(done, 1)

            for h in range(2):
                dve.wait_ge(unit_used, S1 + 12 + 2 * h)
                for t in range(T):
                    step(residual(h, t, 2 * (h % 2) + t))
                if h == 0:
                    lo(SFF)
            lo(SFF + 1)
            dve.wait_ge(land_ln1, 16 * 2)
            for t in range(T):
                layer_norm(t, t, ln1, x3_made)
            for b in range(4):
                lower_ps(b, x3Thi_made, x3T_made)

            def lo_in(i, turn):
                if turn is None:
                    return lo(i)
                slot, _ = slot_of(load_of(i))
                dve.wait_ge(hi_made, turn * RING + (i + 1))
                tt(w_lo[:, i % 2, :], ring[:, slot, :], f32(w_hi[:, i % 2, :]), ALU.subtract).then_inc(lo_made, 1)

            def ffn_hidden(c, turn, between):
                n = c if turn is None else turn * LOOP_B + c
                u = SFF + 1 if c == 0 else body_unit(c) + 1
                dve.wait_ge(sil2_made, n + 1)
                if c >= 1:
                    dve.wait_ge(hidT_made, n)
                dve.wait_ge(unit_used, u + 1 if turn is None else turn * RING + (u + 1))
                tt(hid[:].rearrange("p m n -> p (m n)"), ps[:, 5 + 2 * (c % 2), :],
                   sil2[:].rearrange("p m n -> p (m n)"), ALU.mult).then_inc(hid_made, 1)
                between()
                dve.wait_ge(hidhi_made, n + 1)
                tt(hid_lo[:], hid[:], f32(hid_hi[:]), ALU.subtract).then_inc(hidT_made, 1)

            def ffn_body(c, turn=None):
                i = body_unit(c)
                lo_in(i, turn)
                ffn_hidden(c - 1, turn, lambda: lo_in(i + 1, turn))
                lo_in(i + 2, turn)

            ffn_body(1)
            with dve.Fori(0, LOOP_N) as turn:
                for c in range(2, 2 + LOOP_B):
                    ffn_body(c, turn)
            ffn_body(NCH - 1)
            ffn_hidden(NCH - 1, None, lambda: lo(body_unit(NCH)))
            dve.wait_ge(unit_used, body_unit(NCH) + 1)
            for t in range(T):
                for h in range(2):
                    step(residual(h, t, 2 * t + h))
            dve.wait_ge(land_ln2, 16 * 2)
            for t in range(T):
                layer_norm(t, T + t, ln2, y_out)


_INS = ["x", "norm_mix_g", "w_in", "q_norm_g", "k_norm_g", "conv_w", "w_sb_branch", "w_conv_branch", "w_out",
        "norm_ffn_g", "w_router_group", "b_router_group", "w_router_expert", "b_router_expert", "w_gate_e",
        "w_up_e", "w_down_e", "w_in_2", "attn_out_g_2", "gmlp_out_g_2", "gmlp_ln_g_2", "gmlp_ln_b_2",
        "w_spatial_2", "b_spatial_2", "w_out_2", "ln1_g_2", "ln1_b_2", "w_gate_2", "w_up_2", "w_down_2",
        "ln2_g_2", "ln2_b_2"]


def kernel(**inputs):
    import concourse.bacc as _bacc
    from concourse import mybir as _mybir
    from concourse.bass_utils import run_bass_kernel_spmd as _run

    nc = _bacc.Bacc("TRN2", target_bir_lowering=False, num_devices=1, dynamic_dma_scratch_size=256)
    arrays = {"in_consts": shape_constants()}
    for name in _INS:
        arrays[f"in_{name}"] = np.ascontiguousarray(inputs[name])
    args = [nc.dram_tensor(n, a.shape, _mybir.dt.from_np(a.dtype), kind="ExternalInput").ap()
            for n, a in arrays.items()]
    res = nc.dram_tensor("out_0", (1, SEQ, D), _mybir.dt.float32, kind="ExternalOutput").ap()
    build(nc, *args, res)
    r = _run(nc, [arrays], core_ids=[0])
    return r.results[0]["out_0"]
```

```python
from contextlib import ExitStack

import numpy as np

import concourse.bass as bass
from concourse import mybir

F32 = mybir.dt.float32
F32R = mybir.dt.float32r
BF16 = mybir.dt.bfloat16
I32 = mybir.dt.int32
ALU = mybir.AluOpType
ACT = mybir.ActivationFunctionType
AX = mybir.AxisListType.X

P = 128
KB = 1024
SEQ, D = 256, 1024
T = SEQ // P
KD = D // P
HD = 64
NH = 8
W = NH * HD
PAIRS = NH // 2
NG, EPG = 4, 8
NE = NG * EPG
FE = 256
KF = FE // P
QUAD = 4
NQ = NE // QUAD
CAP = 32
FFN = -(-(8 * D) // (3 * 256)) * 256
FCHUNK = 256
NCH = FFN // FCHUNK
MF = FCHUNK // P
ALPHA = 2.0 ** 0.25
RMS_EPS, LN_EPS = 1e-6, 1e-5
NEG = -1e30

RING = 12
UNIT = 2048
KU = 4
UPQ = 12
EARLY = 8
B1_UNITS = 28
MOE_UNITS = UPQ * NQ
B2_PRE = 14
S1 = B1_UNITS
SFF = S1 + B2_PRE

C_ID, C_NEGU, C_NEGO, C_LTRI, C_ONE, C_TRIU, C_MK1, C_MK2 = (P * i for i in range(8))
C_COS = 8 * P
C_SIN = C_COS + T * HD
C_IOTA = C_SIN + T * HD
C_THR = C_IOTA + CAP
C_N = C_THR + 8


def shape_constants():
    c = np.zeros((P, C_N), np.float32)
    r, k = np.arange(P)[:, None], np.arange(P)[None, :]
    c[:, C_ID:C_ID + P] = r == k
    c[:, C_NEGU:C_NEGU + P] = -(r >= k).astype(np.float32)
    c[:, C_NEGO:C_NEGO + P] = -1.0
    c[:, C_LTRI:C_LTRI + P] = r < k
    c[:, C_ONE:C_ONE + P] = 1.0
    c[:, C_TRIU:C_TRIU + P] = k >= r
    c[:, C_MK1:C_MK1 + P] = np.where(r < k, 0.0, NEG)
    c[:, C_MK2:C_MK2 + P] = np.where(k <= r, 0.0, NEG)
    inv = (np.float32(10000.0) ** (-np.arange(0, HD, 2, dtype=np.float32) / np.float32(HD))).astype(np.float32)
    ang = np.arange(SEQ, dtype=np.float32)[:, None] * inv[None, :]
    cos, sin = np.cos(ang).astype(np.float32), np.sin(ang).astype(np.float32)
    cos = np.concatenate([cos, cos], -1).reshape(T, P, HD)
    sin = np.concatenate([-sin, sin], -1).reshape(T, P, HD)
    c[:, C_COS:C_COS + T * HD] = cos.transpose(1, 0, 2).reshape(P, T * HD)
    c[:, C_SIN:C_SIN + T * HD] = sin.transpose(1, 0, 2).reshape(P, T * HD)
    c[:, C_IOTA:C_IOTA + CAP] = np.arange(CAP)
    c[:, C_THR:C_THR + 8] = CAP * (np.arange(8) + 1)
    return c


def build(nc, consts, x, norm_mix_g, w_in, q_norm_g, k_norm_g, conv_w, w_sb_branch, w_conv_branch, w_out,
          norm_ffn_g, w_router_group, b_router_group, w_router_expert, b_router_expert, w_gate_e, w_up_e,
          w_down_e, w_in_2, attn_out_g_2, gmlp_out_g_2, gmlp_ln_g_2, gmlp_ln_b_2, w_spatial_2, b_spatial_2,
          w_out_2, ln1_g_2, ln1_b_2, w_gate_2, w_up_2, w_down_2, ln2_g_2, ln2_b_2, out):
    with ExitStack() as ctx:
        def sem(name):
            return ctx.enter_context(nc.semaphore(name))

        def at(name, kib, shape, dt=F32):
            return nc.alloc_sbuf_tensor_at(name, shape, dt, offset=256 + int(kib * KB))

        ps = ctx.enter_context(nc.psum_tensor("ps", [P, 8, 512], F32))

        ring = at("ring", 0, [P, RING, UNIT])
        w_hi = at("w_hi", 96, [P, 2, UNIT], F32R)
        w_lo = at("w_lo", 112, [P, 2, UNIT], F32R)
        hT_hi = at("hT_hi", 128, [P, KD, SEQ], F32R)
        hT_lo = at("hT_lo", 136, [P, KD, SEQ], F32R)
        mgT_hi = at("mgT_hi", 128, [P, KD, SEQ], F32R)
        mgT_lo = at("mgT_lo", 136, [P, KD, SEQ], F32R)
        brT_hi = at("brT_hi", 144, [P, 2, 4, SEQ], F32R)
        brT_lo = at("brT_lo", 152, [P, 2, 4, SEQ], F32R)
        early = at("early", 96, [P, EARLY, UNIT])
        xT_hi = at("xT_hi", 128, [P, KD, SEQ], F32R)
        xT_lo = at("xT_lo", 136, [P, KD, SEQ], F32R)
        pT = at("pT", 144, [P, NH, 384])
        gT_hi = at("gT_hi", 128, [P, KD, SEQ], F32R)
        gT_lo = at("gT_lo", 136, [P, KD, SEQ], F32R)
        hid_hi = at("hid_hi", 144, [P, MF, SEQ], F32R)
        hid_lo = at("hid_lo", 146, [P, MF, SEQ], F32R)
        hid = at("hid", 148, [P, MF, SEQ])
        sil2 = at("sil2", 150, [P, MF, SEQ])
        cst = at("cst", 160, [P, C_N])
        bfc = at("bfc", 160 + 5.5, [P, 3, P], BF16)
        wr = at("wr", 160 + 6.25, [P, KD, 36])
        gain = at("gain", 160 + 7.5, [P, 112])
        X = at("X", 168, [P, T, D])
        xn = at("xn", 176, [P, T, D])
        qk = at("qk", 176, [P, 2, T, W])
        ga = at("ga", 176, [P, KD, SEQ])
        h2n = at("h2n", 176, [P, T, D])
        prob = at("prob", 176, [P, 2, 384])
        h2T = at("h2T", 184, [P, KD, SEQ])
        heT = at("heT", 192, [P, KD, P])
        pick = at("pick", 196, [P, T, P])
        pickw = at("pickw", 197, [P, T, P])
        turned = at("turned", 198, [P, 4, P])
        ysb = at("ysb", 200, [P, D])
        rt = at("rt", 204, [P, 1024])
        sil = at("sil", 208, [P, FE])
        act_e = at("act_e", 209, [P, FE])
        qkT = at("qkT", 184, [P, 2, PAIRS, SEQ])
        gb = at("gb", 184, [P, KD, SEQ])
        v = at("v", 192, [P, T, W])
        stick = at("stick", 196, [P, 2, 384])
        attw = at("attw", 200, [P, 2, 384])
        cu = at("cu", 196, [P, 4, SEQ])
        cy = at("cy", 200, [P, 4, SEQ])
        uu = at("uu", 196, [P, T, W])
        zz = at("zz", 200, [P, T, W])
        sq = at("sq", 204, [P, T, W])
        full = at("full", 208, [P, 4, 512])
        mg1 = at("mg1", 204, [P, 4, SEQ])
        mg2 = at("mg2", 208, [P, 4, SEQ])
        spT = at("spT", 216, [P, NH, P])
        spraw = at("spraw", 216, [P, NH, P])
        lngb = at("lngb", 212, [P, 2, W])
        atto = at("atto", 192, [P, T, W])
        ln1 = at("ln1", 184, [P, 2, D])
        ln2 = at("ln2", 212, [P, 2, D])
        st = at("st", 220, [P, 512])
        cnt = at("cnt", 222, [P, 8], I32)

        ident = cst[:, C_ID:C_ID + P]
        negu = cst[:, C_NEGU:C_NEGU + P]
        nego = cst[:, C_NEGO:C_NEGO + P]
        ltri = cst[:, C_LTRI:C_LTRI + P]
        ones = cst[:, C_ONE:C_ONE + P]
        triu = cst[:, C_TRIU:C_TRIU + P]
        cos = cst[:, C_COS:C_COS + T * HD].rearrange("p (t d) -> p t d", t=T)
        sin = cst[:, C_SIN:C_SIN + T * HD].rearrange("p (t d) -> p t d", t=T)
        iota = cst[:, C_IOTA:C_IOTA + CAP]
        thr = cst[:, C_THR:C_THR + 7]
        ident_b, mask1_b, mask2_b = bfc[:, 0, :], bfc[:, 1, :], bfc[:, 2, :]
        g1 = gain[:, 0:8]
        g2 = gain[:, 8:16]
        gq, gk = gain[:, 16:17], gain[:, 17:18]
        cw = gain[:, 18:30].rearrange("p (j m) -> p j m", j=3)
        rbias = gain[:, 30:66]
        gmix = gain[:, 66:74]
        bsp = gain[:, 74:82]
        ln1gT, ln1bT = gain[:, 82:90], gain[:, 90:98]
        pickT, actT = turned[:, 0:T, :], turned[:, T:T + KF, :]

        ss1, y1, n1 = st[:, 0:2], st[:, 2:4], st[:, 4:10]
        ssk, yk, nk = st[:, 16:32], st[:, 32:48], st[:, 48:96]
        ssq, yq = st[:, 96:112], st[:, 112:128]
        ss2, y2 = st[:, 128:130], st[:, 130:132]
        bst = st[:, 136:160].rearrange("p (t c s) -> p t c s", t=T, c=2)
        mv = st[:, 160:164].rearrange("p (t s) -> p t s", t=T)
        yl = st[:, 164:166]
        mx = st[:, 176:192].rearrange("p (h t) -> p h t", t=T)
        mxn = st[:, 192:208].rearrange("p (h t) -> p h t", t=T)
        rsum = st[:, 208:224].rearrange("p (h t) -> p h t", t=T)
        rinv = st[:, 224:240].rearrange("p (h t) -> p h t", t=T)
        zs, zy, zss = st[:, 240:256], st[:, 256:272], st[:, 400:416]
        ssg, yg = st[:, 272:276], st[:, 276:280]
        nw = st[:, 288:400].rearrange("p (i n) -> p i n", n=16)

        land = [sem(f"land{i}") for i in range(RING)]
        land_x = [sem(f"land_x{t}") for t in range(T)]
        land_id = sem("land_id")
        land_cst = sem("land_cst")
        land_qk = sem("land_qk")
        land_small = sem("land_small")
        land_early = [sem(f"land_early{i}") for i in range(EARLY)]
        land_taps = sem("land_taps")
        land_b2 = sem("land_b2")
        land_ln1 = sem("land_ln1")
        land_ln2 = sem("land_ln2")
        out_stored = sem("out_stored")
        hi_made = sem("hi_made")
        lo_made = sem("lo_made")
        unit_used = sem("unit_used")
        half_used = sem("half_used")
        pair_free = [sem("pair_free0"), sem("pair_free1")]
        dve_own = sem("dve_own")
        act_own = sem("act_own")
        root_made = sem("root_made")
        turned_ps = sem("turned_ps")
        full_made = sem("full_made")
        upper_made = sem("upper_made")
        split_made = sem("split_made")
        PS_H, PS_R, PS_X2, PS_G, PS_X3 = 0, 4, 8, 12, 16
        SP_H, SP_X2, SP_G, SP_X3 = 0, 4, 8, 12
        FULL_H, FULL_G = 0, 4
        bf_made = sem("bf_made")
        xn_made = sem("xn_made")
        qk_sq = sem("qk_sq")
        qk_ss = sem("qk_ss")
        qk_made = sem("qk_made")
        qkT_ps = sem("qkT_ps")
        qkT_made = sem("qkT_made")
        v_made = sem("v_made")
        z_ps = sem("z_ps")
        log_made = sem("log_made")
        sp_made = sem("sp_made")
        la_ps = sem("la_ps")
        attw_made = sem("attw_made")
        av_ps = sem("av_ps")
        brhi_made = sem("brhi_made")
        br_made = sem("br_made")
        cc_made = sem("cc_made")
        conv_made = sem("conv_made")
        convhi_made = sem("convhi_made")
        conv_split = sem("conv_split")
        ga_sig = sem("ga_sig")
        gb_sig = sem("gb_sig")
        mg_made = sem("mg_made")
        mghi_made = sem("mghi_made")
        mgT_made = sem("mgT_made")
        x2_made = sem("x2_made")
        h2n_made = sem("h2n_made")
        h2T_made = sem("h2T_made")
        logit_ps = sem("logit_ps")
        gdiff_made = sem("gdiff_made")
        gexp_made = sem("gexp_made")
        assign_made = sem("assign_made")
        rank_ps = sem("rank_ps")
        place_made = sem("place_made")
        count_made = sem("count_made")

        def moe_sems(tag):
            names = ("pick_made", "pickw_made", "gath_ps", "heT_made", "used", "sil_made", "act_made", "aT_ps",
                     "actT_made", "y_made", "spread")
            return {n: sem(f"{n}{tag}") for n in names}

        STARTED = ("y_made", "act_made", "actT_made", "gath_ps", "aT_ps", "spread")
        first = moe_sems("_a")
        more = moe_sems("_b")
        land_more = [sem(f"land_more{i}") for i in range(UPQ)]
        spT_ps = sem("spT_ps")
        spT_made = sem("spT_made")
        rope_made = sem("rope_made")
        rT_ps = sem("rT_ps")
        rT_made = sem("rT_made")
        v2_made = sem("v2_made")
        s_ps = sem("s_ps")
        mx_made = sem("mx_made")
        p_made = sem("p_made")
        pT_ps = sem("pT_ps")
        pT_made = sem("pT_made")
        o_ps = sem("o_ps")
        o_made = sem("o_made")
        zg_made = sem("zg_made")
        zmean_made = sem("zmean_made")
        zc_made = sem("zc_made")
        zq_made = sem("zq_made")
        zss_made = sem("zss_made")
        zy_ready = sem("zy_ready")
        zn_made = sem("zn_made")
        z_made = sem("z_made")
        u_made = sem("u_made")
        mix_ps = sem("mix_ps")
        sg_made = sem("sg_made")
        cat_made = sem("cat_made")
        sum_a = sem("sum_a")
        sum_d = sem("sum_d")
        xhat_made = sem("xhat_made")
        x3g_made = sem("x3g_made")
        y_ps = sem("y_ps")
        var_made = sem("var_made")
        x3_made = sem("x3_made")
        sil2_made = sem("sil2_made")
        hid_made = sem("hid_made")
        hidhi_made = sem("hidhi_made")
        hidT_made = sem("hidT_made")
        y_out = sem("y_out")

        win = w_in[0].rearrange("(p k) n -> p k n", k=KD)
        win2 = w_in_2[0].rearrange("(p k) n -> p k n", k=KD)
        wsb = w_sb_branch[0].rearrange("(k p) n -> p k n", p=P)
        wcv = w_conv_branch[0].rearrange("(k p) n -> p k n", p=P)
        wo = w_out[0].rearrange("(k p) n -> p k n", p=P)
        wo2 = w_out_2[0].rearrange("(k p) n -> p k n", p=P)
        wg2 = w_gate_2[0].rearrange("(p k) n -> p k n", k=KD)
        wu2 = w_up_2[0].rearrange("(p k) n -> p k n", k=KD)
        wd2 = w_down_2[0].rearrange("(c m p) n -> p c m n", m=MF, p=P)
        wge = w_gate_e[0].rearrange("(q j) (p k) f -> q p j k f", j=QUAD, k=KD)
        wue = w_up_e[0].rearrange("(q j) (p k) f -> q p j k f", j=QUAD, k=KD)
        wde = w_down_e[0].rearrange("(e) (p k) n -> e p (k n)", k=KF)

        CH_K, CH_Q, CH_V, CH_GA, CH_CC, CH_CU, CH_CB, CH_GB = 0, 1, 2, 3, 5, 6, 7, 8
        WIN_COL = [1, 0, 2, 6, 7, 4, 5, 3, 8, 9]
        units1 = []
        for c in WIN_COL:
            for h in range(2):
                units1.append(win[:, KU * h:KU * h + KU, 512 * c:512 * c + 512])
        for h in range(2):
            units1.append(wsb[:, :, 512 * h:512 * h + 512])
            units1.append(wcv[:, :, 512 * h:512 * h + 512])
        for kh in range(2):
            for h in range(2):
                units1.append(wo[:, KU * kh:KU * kh + KU, 512 * h:512 * h + 512])
        assert len(units1) == B1_UNITS
        WIN2_COL = [1, 0, 4, 3, 2]
        units2 = []
        for c in WIN2_COL:
            for h in range(2):
                units2.append(win2[:, KU * h:KU * h + KU, 512 * c:512 * c + 512])
        for kh in (1, 0):
            for h in range(2):
                units2.append(wo2[:, KU * kh:KU * kh + KU, 512 * h:512 * h + 512])
        assert len(units2) == B2_PRE

        def slot_of(n):
            return n % RING, 16 * (n // RING + 1)

        def load_of(i):
            return i if i < B1_UNITS else i + MOE_UNITS - EARLY

        QS = [(B1_UNITS + m) % RING for m in range(RING)]
        QV = [slot_of(B1_UNITS + m)[1] for m in range(RING)]

        def quad_slot(u):
            return (u + RING - EARLY) % RING
        EARLY_AT = [(6, B1_UNITS - 4), (7, B1_UNITS - 4), (0, B1_UNITS - 1), (2, B1_UNITS - 1), (1, B1_UNITS),
                    (3, B1_UNITS), (4, B1_UNITS), (5, B1_UNITS)]
        LOOP_B = RING // 3
        LOOP_N = (NCH - 3) // LOOP_B
        assert 2 + LOOP_N * LOOP_B == NCH - 1

        def body_unit(c):
            return SFF + 2 + 3 * (c - 1)

        block = ctx.enter_context(nc.Block())

        @block.sync
        def _(sp):
            def small(dst, src, landed):
                sp.dma_start(dst, src).then_inc(landed, 16)

            for t in range(T):
                sp.dma_start(X[:, t, :], x[0, t * P:(t + 1) * P, :]).then_inc(land_x[t], 16)
            for i, src in enumerate(units1):
                slot, _ = slot_of(i)
                if i >= RING:
                    sp.wait_ge(lo_made, i - RING + 1)
                sp.dma_start(ring[:, slot, :].rearrange("p (k n) -> p k n", k=KU), src).then_inc(land[slot], 16)
                if i == 1:
                    small(cst[:, P:C_N], consts[:, P:C_N], land_cst)
                    for h in range(2):
                        small(gq[HD * h:HD * h + HD, :], q_norm_g[0].rearrange("(d o) -> d o", o=1), land_qk)
                        small(gk[HD * h:HD * h + HD, :], k_norm_g[0].rearrange("(d o) -> d o", o=1), land_qk)
                if i == RING - 1:
                    with nc.allow_non_contiguous_dma(reason="a few thousand gains and biases"):
                        small(cw, conv_w[0].rearrange("j (m p) -> p j m", p=P), land_taps)
                        small(bsp, b_spatial_2[0].rearrange("g i -> i g"), land_small)
                        small(gmix[:, 0:4], attn_out_g_2[0].rearrange("(k p) -> p k", p=P), land_small)
                        small(gmix[:, 4:8], gmlp_out_g_2[0].rearrange("(k p) -> p k", p=P), land_small)
                    small(g2, norm_ffn_g[0].rearrange("(p k) -> p k", k=KD), land_small)
                    small(ln1gT, ln1_g_2[0].rearrange("(p k) -> p k", k=KD), land_small)
                    small(ln1bT, ln1_b_2[0].rearrange("(p k) -> p k", k=KD), land_small)
                    small(wr[:, :, 0:NG], w_router_group[0].rearrange("(p k) n -> p k n", k=KD), land_small)
                    small(wr[:, :, NG:NG + NE], w_router_expert[0].rearrange("(p k) n -> p k n", k=KD), land_small)
                    small(rbias[:, 0:NG], b_router_group[0].partition_broadcast(P), land_small)
                    small(rbias[:, NG:NG + NE], b_router_expert[0].partition_broadcast(P), land_small)

            def quad_unit(q, u, dst, landed):
                if u < 8:
                    src = (wge if u < 4 else wue)[q, :, :, 2 * (u % 4):2 * (u % 4) + 2, :]
                    sp.dma_start(dst.rearrange("p (j k f) -> p j k f", j=QUAD, k=2), src).then_inc(landed, 16)
                else:
                    sp.dma_start(dst, wde[q * QUAD + (u - 8)]).then_inc(landed, 16)

            def ring_unit(q, u, sems):
                m = quad_slot(u)
                quad_unit(q, u, ring[:, QS[m], :], sems[m])

            def early_unit(u):
                spot, used = EARLY_AT[u]
                sp.wait_ge(unit_used, used)
                quad_unit(0, u, early[:, spot, :], land_early[u])

            main_sems = [land[s] for s in QS]
            for m in range(RING):
                if m == 8:
                    early_unit(0)
                    early_unit(1)
                sp.wait_ge(lo_made, B1_UNITS + m - RING + 1)
                q, u = divmod(EARLY + m, UPQ)
                ring_unit(q, u, main_sems)
            for u in range(2, EARLY):
                early_unit(u)
            for u in range(8, UPQ):
                sp.wait_ge(first["used"], u + 1)
                ring_unit(1, u, main_sems)
            with sp.Fori(2, NQ) as q:
                for u in range(UPQ):
                    sp.wait_ge(first["used"], q * UPQ + (u + 1 - UPQ))
                    ring_unit(q, u, main_sems)

            sp.wait_ge(count_made, 1)
            extra = sp.value_load(cnt[0:1, 0:1], min_val=0, max_val=7)
            with sp.If(extra > 0):
                sp.wait_ge(first["used"], MOE_UNITS)
                with sp.Fori(0, extra) as r:
                    with sp.Fori(0, NQ) as q:
                        for u in range(UPQ):
                            sp.wait_ge(more["used"], (r * NQ + q) * UPQ + (u + 1))
                            ring_unit(q, u, land_more)
            sp.wait_ge(more["used"], extra * MOE_UNITS + UPQ)

            sp.wait_ge(first["pick_made"], 1)
            sp.dma_start(spraw[:], w_spatial_2[0].rearrange("g i j -> i g j")).then_inc(land_b2, 16)
            for i, g in enumerate((gmlp_ln_g_2, gmlp_ln_b_2)):
                sp.dma_start(lngb[:, i, :], g[0].rearrange("g d -> (g d)").partition_broadcast(P)
                             ).then_inc(land_b2, 16)

            def b2_free(i):
                n = load_of(i)
                if n - RING < B1_UNITS + MOE_UNITS - EARLY:
                    sp.wait_ge(first["used"], n - RING - B1_UNITS + EARLY + 1)
                else:
                    sp.wait_ge(lo_made, i - RING + 1)

            for j, src in enumerate(units2):
                i = S1 + j
                slot, _ = slot_of(load_of(i))
                b2_free(i)
                sp.dma_start(ring[:, slot, :].rearrange("p (k n) -> p k n", k=KU), src).then_inc(land[slot], 16)

            def ffn_gu(i, w, c, turn=None):
                slot, _ = slot_of(load_of(i))
                if turn is None:
                    b2_free(i)
                else:
                    sp.wait_ge(lo_made, turn * RING + (i - RING + 1))
                if turn is not None:
                    src = w[:, :, bass.ds(turn * (LOOP_B * FCHUNK) + c * FCHUNK, FCHUNK)]
                else:
                    src = w[:, :, c * FCHUNK:(c + 1) * FCHUNK]
                sp.dma_start(ring[:, slot, :].rearrange("p (k n) -> p k n", k=KD), src).then_inc(land[slot], 16)

            def ffn_d(i, c, turn=None):
                slot, _ = slot_of(load_of(i))
                if turn is None:
                    b2_free(i)
                else:
                    sp.wait_ge(lo_made, turn * RING + (i - RING + 1))
                src = wd2[:, c] if turn is None else wd2[:, bass.ds(turn * LOOP_B + c, 1)].rearrange(
                    "p o m n -> p (o m) n")
                sp.dma_start(ring[:, slot, :].rearrange("p (m n) -> p m n", m=MF), src).then_inc(land[slot], 16)

            def ffn_body(c, turn=None):
                i = body_unit(c)
                ffn_gu(i, wg2, c, turn)
                ffn_gu(i + 1, wu2, c, turn)
                ffn_d(i + 2, c - 1, turn)

            ffn_gu(SFF, wg2, 0)
            ffn_gu(SFF + 1, wu2, 0)
            ffn_body(1)
            sp.wait_ge(s_ps, NH)
            for i, g in enumerate((ln1_g_2, ln1_b_2)):
                sp.dma_start(ln1[:, i, :], g[0].partition_broadcast(P)).then_inc(land_ln1, 16)
            with sp.Fori(0, LOOP_N) as turn:
                for c in range(2, 2 + LOOP_B):
                    ffn_body(c, turn)
            sp.wait_ge(split_made, SP_X3 + 4)
            for i, g in enumerate((ln2_g_2, ln2_b_2)):
                sp.dma_start(ln2[:, i, :], g[0].partition_broadcast(P)).then_inc(land_ln2, 16)
            ffn_body(NCH - 1)
            ffn_d(body_unit(NCH), NCH - 1)
            for t in range(T):
                for c in range(2):
                    sp.wait_ge(y_out, 2 * t + c + 1)
                    sp.dma_start(out[0, t * P:(t + 1) * P, c * 512:(c + 1) * 512], X[:, t, c * 512:(c + 1) * 512]
                                 ).then_inc(out_stored, 16)
            sp.wait_ge(out_stored, 16 * 2 * T)

        @block.tensor
        def _(pe):
            mm = nc.tensor.matmul

            def mm3(o, a_hi, a_lo, b_hi, b_lo, start, stop):
                mm(o, a_hi, b_hi, start=start, stop=False, skip_group_check=True)
                mm(o, a_hi, b_lo, start=False, stop=False, skip_group_check=True)
                return mm(o, a_lo, b_hi, start=False, stop=stop, skip_group_check=True)

            def token_unit(i, c, k0, aT_hi, aT_lo, first, last, ready=None, between=None, half=False):
                bank = 2 * (c % 2)
                if c >= 2 and first:
                    pe.wait_ge(pair_free[c % 2], c // 2)
                pe.wait_ge(lo_made, i + 1)
                b = i % 2
                hi = w_hi[:, b, :].rearrange("p (k n) -> p k n", k=KU)
                lo = w_lo[:, b, :].rearrange("p (k n) -> p k n", k=KU)
                for t in range(T):
                    if ready:
                        pe.wait_ge(ready[0], ready[1 + t])
                    for kk in range(KU):
                        k = k0 + kk
                        tok = slice(t * P, (t + 1) * P)
                        ins = mm3(ps[:, bank + t, :], aT_hi[:, k, tok], aT_lo[:, k, tok], hi[:, kk, :],
                                  lo[:, kk, :], start=(first and kk == 0), stop=(last and kk == KU - 1))
                    if t == 0 and half:
                        ins.then_inc(half_used, 1)
                    if t == 0 and between:
                        between()
                ins.then_inc(unit_used, 1)

            def feature_unit(i, c, k0, aT_hi, aT_lo, n_k=KD):
                bank = 2 * (c % 2)
                if c >= 2 and k0 == 0:
                    pe.wait_ge(pair_free[c % 2], c // 2)
                pe.wait_ge(lo_made, i + 1)
                b = i % 2
                hi = w_hi[:, b, :].rearrange("p (k n) -> p k n", k=KU)
                lo = w_lo[:, b, :].rearrange("p (k n) -> p k n", k=KU)
                for m in range(4):
                    o = ps[:, bank + m // 2, (m % 2) * SEQ:(m % 2 + 1) * SEQ]
                    for kk in range(KU):
                        k = k0 + kk
                        col = slice(m * P, (m + 1) * P)
                        last = mm3(o, hi[:, kk, col], lo[:, kk, col], aT_hi[:, k, :], aT_lo[:, k, :],
                                   start=(k == 0 and m % 2 == 0), stop=(k == n_k - 1))
                last.then_inc(unit_used, 1)

            def transposes(src, bank, ready):
                for t in range(T):
                    for made, value in ready:
                        pe.wait_ge(made, value + t)
                    for k in range(KD):
                        tile = src[:, t, k:D:KD]
                        ins = nc.tensor.transpose(ps[:, bank + 2 * t + k // 4, (k % 4) * P:(k % 4 + 1) * P],
                                                  tile, ident)
                        if k % 4 == 3:
                            ins.then_inc(turned_ps, 1)

            pe.wait_ge(land_id, 16 * 2)
            transposes(xn, 0, [(xn_made, 1)])

            def proj(i, feature):
                if feature:
                    feature_unit(i, i // 2, KU * (i % 2), hT_hi, hT_lo)
                else:
                    token_unit(i, i // 2, KU * (i % 2), hT_hi, hT_lo, i % 2 == 0, i % 2 == 1, (split_made, SP_H + 2, SP_H + 4))

            def head_transposes(which):
                pe.wait_ge(qk_made, which + 1)
                for t in range(T):
                    for p in range(PAIRS):
                        ins = nc.tensor.transpose(ps[:, 4 + 2 * which + t, p * P:(p + 1) * P],
                                                  qk[:, which, t, p * P:(p + 1) * P], ident)
                ins.then_inc(qkT_ps, 1)

            def zbank(p):
                return 4 + 2 * (p % 2)

            def z_step(p):
                if p == 0:
                    pe.wait_ge(qkT_made, 2)
                    pe.wait_ge(bf_made, 1)
                if p >= 2:
                    pe.wait_ge(br_made, p - 1)
                for h in range(2):
                    row = slice(HD * h, HD * h + HD)
                    o = ps[:, zbank(p) + h, :]
                    mm(o[:, 0:SEQ], qkT[row, 0, p, 0:P], qkT[row, 1, p, :], start=True, stop=False,
                       skip_group_check=True)
                    mm(o[:, SEQ:SEQ + P], qkT[row, 0, p, P:SEQ], qkT[row, 1, p, P:SEQ], start=False, stop=False,
                       skip_group_check=True)
                for h in range(2):
                    o = ps[:, zbank(p) + h, :]
                    mm(o[:, 0:P], ident_b, mask1_b, start=False, stop=False, skip_group_check=True)
                    last = mm(o[:, SEQ:SEQ + P], ident_b, mask1_b, start=False, stop=True, skip_group_check=True)
                last.then_inc(z_ps, 1)

            def la_step(p):
                pe.wait_ge(sp_made, p + 1)
                for h in range(2):
                    o = ps[:, zbank(p) + h, :]
                    mm(o[:, 0:SEQ], negu, stick[:, h, 0:SEQ], start=False, stop=False, skip_group_check=True)
                    mm(o[:, P:SEQ], nego, stick[:, h, SEQ:SEQ + P], start=False, stop=False, skip_group_check=True)
                    last = mm(o[:, SEQ:SEQ + P], negu, stick[:, h, SEQ:SEQ + P], start=False, stop=True,
                              skip_group_check=True)
                last.then_inc(la_ps, 1)

            def av_step(p):
                pe.wait_ge(attw_made, p + 1)
                if p == 0:
                    pe.wait_ge(v_made, 1)
                for h in range(2):
                    head = slice((2 * p + h) * HD, (2 * p + h + 1) * HD)
                    o = ps[HD * h:HD * h + HD, zbank(p), 0:SEQ]
                    mm(o, v[:, 0, head], attw[:, h, 0:SEQ], start=True, stop=False, skip_group_check=True)
                    last = mm(o[:, P:SEQ], v[:, 1, head], attw[:, h, SEQ:SEQ + P], start=False, stop=True,
                              skip_group_check=True)
                last.then_inc(av_ps, 1)

            for i in range(4):
                proj(i, False)
            head_transposes(0)
            proj(4, False)
            proj(5, False)
            head_transposes(1)
            proj(6, True)
            z_step(0)
            proj(7, True)
            z_step(1)
            la_step(0)
            proj(8, True)
            av_step(0)
            la_step(1)
            proj(9, True)
            av_step(1)
            z_step(2)
            proj(10, True)
            z_step(3)
            la_step(2)
            proj(11, True)
            av_step(2)
            la_step(3)
            proj(12, True)
            av_step(3)
            for i in range(13, 20):
                proj(i, True)
            pe.wait_ge(br_made, PAIRS)
            pe.wait_ge(conv_split, 1)
            for h in range(2):
                for branch in range(2):
                    feature_unit(20 + 2 * h + branch, 10 + 2 * h + branch, 0, brT_hi[:, branch], brT_lo[:, branch],
                                 n_k=KU)
            for kh in range(2):
                pe.wait_ge(mgT_made, kh + 1)
                for h in range(2):
                    token_unit(24 + 2 * kh + h, 14 + h, KU * kh, mgT_hi, mgT_lo, kh == 0, kh == 1,
                               half=(kh == 1 and h == 1))

            transposes(X, 4, [(x2_made, 3)])
            pe.wait_ge(land_small, 16 * 10)
            for t in range(T):
                pe.wait_ge(h2T_made, 2 * t + 2)
                if t == 0:
                    pe.wait_ge(h2T_made, 4)
                for k in range(KD):
                    last = mm(ps[:, 6, t * 36:t * 36 + 36], h2T[:, k, t * P:(t + 1) * P], wr[:, k, :],
                              start=(k == 0), stop=(k == KD - 1))
            last.then_inc(logit_ps, 1)
            for t in range(T):
                for h in range(2):
                    mm(ps[:, 2 * t + h, :], ident, X[:, t, h * 512:(h + 1) * 512], start=True, stop=False,
                       skip_group_check=True)
            pe.wait_ge(assign_made, 1)
            asg = rt[:, 0:64].rearrange("p (t e) -> p t e", t=T)
            mm(ps[:, 7, 0:NE], ltri, asg[:, 0, :], start=True, stop=True)
            mm(ps[:, 7, NE:2 * NE], ones, asg[:, 0, :], start=True, stop=False)
            mm(ps[:, 7, NE:2 * NE], ltri, asg[:, 1, :], start=False, stop=True)
            mm(ps[:, 7, 2 * NE:3 * NE], ones, asg[:, 0, :], start=True, stop=False)
            mm(ps[:, 7, 2 * NE:3 * NE], ones, asg[:, 1, :], start=False, stop=True).then_inc(rank_ps, 1)

            def quad(it, s, weights, landed):
                pe.wait_ge(s["pick_made"], it + 1)
                pe.wait_ge(s["y_made"], it * 2 + 1)
                for k in range(KD):
                    for t in range(T):
                        last = mm(ps[:, 6 + k // 4, (k % 4) * P:(k % 4 + 1) * P], h2n[:, t, k:D:KD], pick[:, t, :],
                                  start=(t == 0), stop=(t == T - 1))
                last.then_inc(s["gath_ps"], 1)
                pe.wait_ge(s["heT_made"], it + 1)
                pe.wait_ge(s["actT_made"], it + 1)
                for u in range(8):
                    if u == 4:
                        pe.wait_ge(s["act_made"], it + 1)
                    landed(u)
                    wv = weights(u).rearrange("p (j k f) -> p j k f", j=QUAD, k=2)
                    for kk in range(2):
                        k = 2 * (u % 4) + kk
                        for j in range(QUAD):
                            last = mm(ps[32 * j:32 * j + 32, 4 + u // 4, 0:FE], heT[:, k, 32 * j:32 * j + 32],
                                      wv[:, j, kk, :], start=(k == 0), stop=(k == KD - 1))
                    last.then_inc(s["used"], 1)
                pe.wait_ge(s["sil_made"], it + 1)
                pe.wait_ge(s["pickw_made"], it + 1)
                for t in range(T):
                    nc.tensor.transpose(ps[:, 4, t * P:(t + 1) * P], pickw[:, t, :], ident)
                pe.wait_ge(s["act_made"], it + 2)
                for k in range(KF):
                    last = nc.tensor.transpose(ps[:, 4, (T + k) * P:(T + k + 1) * P], act_e[:, k:FE:KF], ident)
                last.then_inc(s["aT_ps"], 1)
                pe.wait_ge(s["actT_made"], it + 2)
                for u in range(8, UPQ):
                    landed(u)
                for h in range(2):
                    for k in range(KF):
                        for j in range(QUAD):
                            wv = weights(8 + j).rearrange("p (k n) -> p k n", k=KF)
                            last = mm(ps[32 * j:32 * j + 32, 6 + h, :], actT[:, k, 32 * j:32 * j + 32],
                                      wv[:, k, h * 512:(h + 1) * 512], start=(k == 0), stop=(k == KF - 1))
                            if h == 1 and k == KF - 1:
                                last.then_inc(s["used"], 1)
                pe.wait_ge(s["y_made"], it * 2 + 3)
                for t in range(T):
                    for h in range(2):
                        last = mm(ps[:, 2 * t + h, :], pickT[:, t, :], ysb[:, h * 512:(h + 1) * 512], start=False,
                                  stop=False, skip_group_check=True)
                last.then_inc(s["spread"], 1)

            def in_ring(u):
                return ring[:, QS[quad_slot(u)], :]

            def first_weights(u):
                return early[:, EARLY_AT[u][0], :] if u < EARLY else in_ring(u)

            def landed_first(u):
                if u < EARLY:
                    pe.wait_ge(land_early[u], 16)
                else:
                    pe.wait_ge(land[QS[u - EARLY]], QV[u - EARLY])

            def landed_ring(q):
                def wait(u):
                    m = quad_slot(u)
                    pe.wait_ge(land[QS[m]], q * 16 + (QV[m] if u >= EARLY else QV[m] - 16))
                return wait

            def landed_more(it):
                return lambda u: pe.wait_ge(land_more[quad_slot(u)], it * 16 + 16)

            for s in (first, more):
                for name in STARTED:
                    pe.sem_inc(s[name], 1)
            pe.sem_inc(more["used"], UPQ)
            quad(0, first, first_weights, landed_first)
            with pe.Fori(1, NQ) as q:
                quad(q, first, in_ring, landed_ring(q))
            pe.wait_ge(count_made, 1)
            extra = pe.value_load(cnt[0:1, 0:1], min_val=0, max_val=7)
            with pe.If(extra > 0):
                with pe.Fori(0, extra) as r:
                    with pe.Fori(0, NQ) as q:
                        quad(r * NQ + q, more, in_ring, landed_more(r * NQ + q))

            transposes(X, 4, [(sum_a, 1), (sum_d, 1)])

            def proj2(j, between=None):
                token_unit(S1 + j, 16 + j // 2, KU * (j % 2), xT_hi, xT_lo, j % 2 == 0, j % 2 == 1,
                           (split_made, SP_X2 + 2, SP_X2 + 4), between)

            def spatial_transposes():
                pe.wait_ge(land_b2, 16 * 3)
                pe.wait_ge(split_made, SP_X2 + 4)
                for g in range(NH):
                    ins = nc.tensor.transpose(ps[:, 4 + g // 4, (g % 4) * P:(g % 4 + 1) * P], spraw[:, g, :], ident)
                ins.then_inc(spT_ps, 1)

            def rope_transposes(which):
                if which == 0:
                    pe.wait_ge(spT_made, 1)
                pe.wait_ge(rope_made, which + 1)
                for t in range(T):
                    for p in range(PAIRS):
                        ins = nc.tensor.transpose(ps[:, 4 + 2 * which + t, p * P:(p + 1) * P],
                                                  qk[:, which, t, p * P:(p + 1) * P], ident)
                ins.then_inc(rT_ps, 1)

            def score_step(h):
                if h == 0:
                    pe.wait_ge(rT_made, 2)
                if h >= 2:
                    pe.wait_ge(pT_made, h - 1)
                row = slice(HD * (h % 2), HD * (h % 2) + HD)
                o = ps[:, 4 + h % 2, :]
                mm(o[:, 0:P], qkT[row, 1, h // 2, 0:P], qkT[row, 0, h // 2, 0:P], start=True, stop=False,
                   skip_group_check=True)
                mm(o[:, P:P + SEQ], qkT[row, 1, h // 2, P:SEQ], qkT[row, 0, h // 2, :], start=False, stop=False,
                   skip_group_check=True)
                mm(o[:, 0:P], ident_b, mask2_b, start=False, stop=False, skip_group_check=True)
                mm(o[:, SEQ:SEQ + P], ident_b, mask2_b, start=False, stop=True, skip_group_check=True
                   ).then_inc(s_ps, 1)

            def prob_transposes(h):
                pe.wait_ge(p_made, T * (h + 1))
                for j in range(3):
                    ins = nc.tensor.transpose(ps[:, 4 + h % 2, j * P:(j + 1) * P], prob[:, h % 2, j * P:(j + 1) * P],
                                              ident)
                ins.then_inc(pT_ps, 1)

            def out_step(h):
                pe.wait_ge(pT_made, h + 1)
                head = slice(h * HD, (h + 1) * HD)
                w = pT[:, h, :]
                mm(ps[:, 6, head], w[:, 0:P], v[:, 0, head], start=True, stop=True)
                mm(ps[:, 7, head], w[:, P:SEQ], v[:, 0, head], start=True, stop=False)
                return mm(ps[:, 7, head], w[:, SEQ:SEQ + P], v[:, 1, head], start=False, stop=True)

            def heads(scores, turns):
                def work():
                    for h in scores:
                        score_step(h)
                    for h in turns:
                        prob_transposes(h)
                return work

            def mix_step():
                heads((), (7,))()
                pe.wait_ge(pair_free[1], 10)
                pe.wait_ge(z_made, 1)
                for g in range(NH):
                    last = mm(ps[:, 2 + g // 4, (g % 4) * P:(g % 4 + 1) * P].rearrange("p (t d) -> p t d", t=T),
                              spT[:, g, :], zz[:, :, g * HD:(g + 1) * HD], start=True, stop=True)
                last.then_inc(mix_ps, 1)

            proj2(0)
            proj2(1, spatial_transposes)
            proj2(2)
            proj2(3, lambda: rope_transposes(0))
            proj2(4)
            rope_transposes(1)
            proj2(5, heads((0,), ()))
            heads((1,), (0,))()
            proj2(6, heads((2,), (1,)))
            heads((3,), (2,))()
            proj2(7, heads((4,), (3,)))
            heads((5,), (4,))()
            proj2(8, heads((6,), (5,)))
            heads((7,), (6,))()
            proj2(9, mix_step)
            pe.wait_ge(v2_made, 1)
            for h in range(NH):
                last = out_step(h)
            last.then_inc(o_ps, 1)

            def branch_transposes(b):
                pe.wait_ge(cat_made, b + 1)
                src = (zz, atto)[b // 2]
                for k in range(4):
                    ins = nc.tensor.transpose(ps[:, 4 + b, k * P:(k + 1) * P], src[:, b % 2, k * P:(k + 1) * P], ident)
                ins.then_inc(turned_ps, 1)

            def attention_transposes():
                branch_transposes(2)
                branch_transposes(3)

            branch_transposes(0)
            branch_transposes(1)
            token_unit(S1 + 10, 22, 4, gT_hi, gT_lo, True, False, (split_made, SP_G + 1, SP_G + 2))
            token_unit(S1 + 11, 23, 4, gT_hi, gT_lo, True, False, None, attention_transposes)
            token_unit(S1 + 12, 22, 0, gT_hi, gT_lo, False, True, (split_made, SP_G + 3, SP_G + 4))
            token_unit(S1 + 13, 23, 0, gT_hi, gT_lo, False, True, half=True)
            transposes(X, 4, [(xhat_made, 1)])
            pe.wait_ge(split_made, SP_X3 + 4)

            def ffn_up(i, c, kind, turn=None):
                off = 0 if turn is None else turn * RING
                done = c - 1 if turn is None else turn * LOOP_B + (c - 1)
                if c >= 2:
                    pe.wait_ge((sil2_made, hid_made)[kind], done)
                pe.wait_ge(lo_made, off + (i + 1))
                hi = w_hi[:, i % 2, :].rearrange("p (k n) -> p k n", k=KD)
                lo = w_lo[:, i % 2, :].rearrange("p (k n) -> p k n", k=KD)
                for m in range(MF):
                    o = ps[:, 4 + 2 * (c % 2) + kind, m * SEQ:(m + 1) * SEQ]
                    for k in range(KD):
                        col = slice(m * P, (m + 1) * P)
                        last = mm3(o, hi[:, k, col], lo[:, k, col], xT_hi[:, k, :], xT_lo[:, k, :],
                                   start=(k == 0 and m == 0), stop=(k == KD - 1))
                last.then_inc(unit_used, 1)

            def ffn_down(i, c, turn=None):
                off = 0 if turn is None else turn * RING
                done = c + 1 if turn is None else turn * LOOP_B + (c + 1)
                pe.wait_ge(hidT_made, done)
                pe.wait_ge(lo_made, off + (i + 1))
                hi = w_hi[:, i % 2, :].rearrange("p (m n) -> p m n", m=MF)
                lo = w_lo[:, i % 2, :].rearrange("p (m n) -> p m n", m=MF)
                for t in range(T):
                    tok = slice(t * P, (t + 1) * P)
                    for h in range(2):
                        for m in range(MF):
                            last = mm3(ps[:, 2 * t + h, :], hid_hi[:, m, tok], hid_lo[:, m, tok],
                                       hi[:, m, h * 512:(h + 1) * 512], lo[:, m, h * 512:(h + 1) * 512],
                                       start=(c == 0 and m == 0), stop=False)
                        if c == NCH - 1:
                            last.then_inc(y_ps, 1)
                if c < NCH - 1:
                    last.then_inc(unit_used, 1)

            def ffn_body(c, turn=None):
                i = body_unit(c)
                ffn_up(i, c, 0, turn)
                ffn_up(i + 1, c, 1, turn)
                ffn_down(i + 2, c - 1, turn)

            ffn_up(SFF, 0, 0)
            ffn_up(SFF + 1, 0, 1)
            ffn_body(1)
            with pe.Fori(0, LOOP_N) as turn:
                for c in range(2, 2 + LOOP_B):
                    ffn_body(c, turn)
            ffn_body(NCH - 1)
            ffn_down(body_unit(NCH), NCH - 1)

        @block.scalar
        def _(act):
            LOG_EXP = "natural_log_exp_and_others"
            own = [0]

            def step(ins):
                own[0] += 1
                ins.then_inc(act_own, 1)
                act.wait_ge(act_own, own[0])

            def copy(o, i):
                return nc.scalar.activation(o, i, ACT.Copy)

            junk2 = full[:, 0:2, :]
            junk = [sq[:].rearrange("p t w -> p (t w)"), full[:, 0:2, :].rearrange("p b n -> p (b n)")]

            act.dma_start(cst[:, 0:P], consts[:, 0:P]).then_inc(land_id, 16)
            act.dma_start(g1, norm_mix_g[0].rearrange("(p k) -> p k", k=KD)).then_inc(land_id, 16)
            nc.scalar.preload_act_table_set(LOG_EXP)

            def rsqrt(y, ss, n, eps):
                step(nc.scalar.activation(y, ss, ACT.Ln, scale=1.0 / n, bias=eps))
                nc.scalar.activation(y, y, ACT.Exp, scale=-0.5).then_inc(root_made, 1)

            def hi(i):
                slot, value = slot_of(load_of(i))
                act.wait_ge(land[slot], value)
                if i >= 2:
                    act.wait_ge(unit_used, i - 1)
                copy(w_hi[:, i % 2, :], ring[:, slot, :]).then_inc(hi_made, 1)

            for t in range(T):
                act.wait_ge(land_x[t], 16)
                step(nc.scalar.activation(junk[t], X[:, t, :], ACT.Square, accum_out=ss1[:, t:t + 1]))
                rsqrt(y1[:, t:t + 1], ss1[:, t:t + 1], D, RMS_EPS)

            def hT_copy(b):
                t, k0 = b // 2, 4 * (b % 2)
                act.wait_ge(full_made, FULL_H + b + 1)
                copy(hT_hi[:, k0:k0 + 4, t * P:(t + 1) * P],
                     full[:, b, :].rearrange("p (k n) -> p k n", k=4)).then_inc(upper_made, 1)

            hT_copy(0)
            hT_copy(1)
            hi(0)
            hT_copy(2)
            hT_copy(3)
            hi(1)
            act.wait_ge(land_cst, 16)
            for j, c in enumerate((C_ID, C_MK1, C_MK2)):
                last = copy(bfc[:, j, :], cst[:, c:c + P])
            last.then_inc(bf_made, 1)
            hi(2)

            def qk_square(which):
                act.wait_ge(unit_used, 2 * which + 2)
                if which == 1:
                    act.wait_ge(qk_ss, 1)
                nc.scalar.activation(sq[:].rearrange("p t w -> p (t w)"),
                                     ps[:, 2 * which:2 * which + 2, :].rearrange("p t w -> p (t w)"),
                                     ACT.Square).then_inc(qk_sq, 1)
                act.wait_ge(qk_ss, which + 1)
                rsqrt((yk, yq)[which], (ssk, ssq)[which], HD, RMS_EPS)

            def qkT_copy(which):
                act.wait_ge(qkT_ps, which + 1)
                for t in range(T):
                    last = nc.scalar.activation(
                        qkT[:, which, :, t * P:(t + 1) * P],
                        ps[:, 4 + 2 * which + t, :].rearrange("p (a n) -> p a n", a=PAIRS), ACT.Identity,
                        scale=(gk, gq)[which])
                last.then_inc(qkT_made, 1)

            def chunk_done(c):
                act.wait_ge(unit_used, 2 * c + 2)

            def two_banks(c):
                return ps[:, 2 * (c % 2):2 * (c % 2) + 2, :].rearrange("p b n -> p (b n)")

            def log1p_step(p):
                act.wait_ge(z_ps, p + 1)
                if p >= 1:
                    act.wait_ge(la_ps, p)
                b = 4 + 2 * (p % 2)
                step(nc.scalar.activation(stick[:], ps[:, b:b + 2, 0:384], ACT.Abs))
                step(nc.scalar.activation(stick[:], stick[:], ACT.Exp, scale=-1.0))
                nc.scalar.activation(stick[:], stick[:], ACT.Ln, bias=1.0).then_inc(log_made, 1)

            def attw_step(p):
                act.wait_ge(la_ps, p + 1)
                if p >= 1:
                    act.wait_ge(av_ps, p)
                b = 4 + 2 * (p % 2)
                nc.scalar.activation(attw[:], ps[:, b:b + 2, 0:384], ACT.Exp).then_inc(attw_made, 1)

            def brhi_step(p):
                act.wait_ge(av_ps, p + 1)
                copy(brT_hi[:, 0, p, :], ps[:, 4 + 2 * (p % 2), 0:SEQ]).then_inc(brhi_made, 1)

            hi(3)
            qk_square(0)
            hi(4)
            hi(5)
            qk_square(1)
            qkT_copy(0)
            hi(6)
            qkT_copy(1)
            hi(7)
            chunk_done(CH_V)
            copy(v[:].rearrange("p t w -> p (t w)"), two_banks(CH_V)).then_inc(pair_free[0], 1)
            act.wait_ge(pair_free[0], 2)
            nc.scalar.nop().then_inc(v_made, 1)
            hi(8)
            log1p_step(0)
            hi(9)
            chunk_done(CH_GA)
            copy(ga[:, 0:4, :].rearrange("p m n -> p (m n)"), two_banks(CH_GA)).then_inc(pair_free[1], 1)
            attw_step(0)
            log1p_step(1)
            hi(10)
            brhi_step(0)
            attw_step(1)
            hi(11)
            chunk_done(CH_GA + 1)
            copy(ga[:, 4:8, :].rearrange("p m n -> p (m n)"), two_banks(CH_GA + 1)).then_inc(pair_free[0], 1)
            brhi_step(1)
            log1p_step(2)
            hi(12)
            attw_step(2)
            log1p_step(3)
            hi(13)
            brhi_step(2)
            attw_step(3)
            hi(14)
            brhi_step(3)
            chunk_done(CH_CC)
            act.wait_ge(av_ps, PAIRS)
            copy(cu[:].rearrange("p m n -> p (m n)"), two_banks(CH_CC)).then_inc(cc_made, 1)
            act.wait_ge(cc_made, 1)
            nc.scalar.nop().then_inc(pair_free[1], 1)
            act.wait_ge(pair_free[0], 3)
            nc.scalar.activation(ga[:], ga[:], ACT.Sigmoid).then_inc(ga_sig, 1)
            hi(15)
            hi(16)
            hi(17)
            act.wait_ge(conv_made, 1)
            copy(brT_hi[:, 1], cy[:]).then_inc(convhi_made, 1)
            hi(18)
            hi(19)
            for h in range(2):
                chunk_done(CH_GB + h)
                nc.scalar.activation(gb[:, 4 * h:4 * h + 4, :].rearrange("p m n -> p (m n)"), two_banks(CH_GB + h),
                                     ACT.Sigmoid).then_inc(pair_free[h], 1)
                hi(20 + h)
            act.wait_ge(pair_free[1], 5)
            act.wait_ge(pair_free[0], 5)
            nc.scalar.nop().then_inc(gb_sig, 1)
            nc.scalar.preload_act_table_set(LOG_EXP)
            hi(22)
            hi(23)
            for h in range(2):
                act.wait_ge(mg_made, h + 1)
                copy(mgT_hi[:, 4 * h:4 * h + 4, :], mg1[:]).then_inc(mghi_made, 1)
                hi(24 + 2 * h)
                hi(25 + 2 * h)

            for t in range(T):
                act.wait_ge(x2_made, T + 1 + t)
                step(nc.scalar.activation(junk[t], X[:, t, :], ACT.Square, accum_out=ss2[:, t:t + 1]))
            rsqrt(y2, ss2, D, RMS_EPS)
            for j in range(2):
                act.wait_ge(gdiff_made, j + 1)
                buf = rt[:, 64:72] if j == 0 else rt[:, 72:74]
                nc.scalar.activation(buf, buf, ACT.Exp).then_inc(gexp_made, 1)
            nc.scalar.preload_act_table_set("silu_and_others")

            def quad(it, s):
                act.wait_ge(s["used"], it * UPQ + (4 + s["start"]))
                act.wait_ge(s["act_made"], it + 1)
                nc.scalar.activation(sil[:], ps[:, 4, 0:FE], ACT.Silu).then_inc(s["sil_made"], 1)
                act.wait_ge(s["aT_ps"], it + 2)
                copy(turned[:].rearrange("p k n -> p (k n)"), ps[:, 4, :]).then_inc(s["actT_made"], 1)
                act.wait_ge(s["used"], it * UPQ + (UPQ + s["start"]))
                copy(ysb[:, 0:512], ps[:, 6, :]).then_inc(s["y_made"], 1)

            quad(0, first | {"start": 0})
            with act.Fori(1, NQ) as q:
                quad(q, first | {"start": 0})
            act.wait_ge(count_made, 1)
            extra = act.value_load(cnt[0:1, 0:1], min_val=0, max_val=7)
            with act.If(extra > 0):
                with act.Fori(0, extra) as r:
                    with act.Fori(0, NQ) as q:
                        quad(r * NQ + q, more | {"start": UPQ})
            act.wait_ge(more["spread"], extra * NQ + 1)
            hi(S1)

            act.wait_ge(first["spread"], NQ + 1)
            for t in range(T):
                copy(X[:, t, 0:512], ps[:, 2 * t, :]).then_inc(sum_a, 1)

            def xT_copy(b):
                t, k0 = b // 2, 4 * (b % 2)
                act.wait_ge(turned_ps, PS_X2 + b + 1)
                copy(xT_hi[:, k0:k0 + 4, t * P:(t + 1) * P],
                     ps[:, 4 + b, :].rearrange("p (k n) -> p k n", k=4)).then_inc(upper_made, 1)

            for b in range(4):
                xT_copy(b)
            nc.scalar.preload_act_table_set("gelu_and_others")

            def rT_copy(which):
                act.wait_ge(rT_ps, which + 1)
                for t in range(T):
                    last = copy(qkT[:, which, :, t * P:(t + 1) * P],
                                ps[:, 4 + 2 * which + t, :].rearrange("p (a n) -> p a n", a=PAIRS))
                last.then_inc(rT_made, 1)

            def exp_step(h):
                act.wait_ge(mx_made, h + 1)
                if h >= 2:
                    act.wait_ge(pT_ps, h - 1)
                for t in range(T):
                    a, b = (0, P) if t == 0 else (P, P + SEQ)
                    nc.scalar.activation(prob[:, h % 2, a:b], ps[:, 4 + h % 2, a:b], ACT.Exp, bias=mxn[:, h, t:t + 1],
                                         scale=HD ** -0.5, accum_out=rsum[:, h, t:t + 1]).then_inc(p_made, 1)

            def pT_copy(h):
                act.wait_ge(pT_ps, h + 1)
                copy(pT[:, h, :], ps[:, 4 + h % 2, 0:384]).then_inc(pT_made, 1)

            def gelu(dst, c, done):
                act.wait_ge(unit_used, S1 + 2 * (c - 16) + 2)
                for t in range(T):
                    nc.scalar.activation(dst[:, t, :], ps[:, 2 * (c % 2) + t, :], ACT.Gelu).then_inc(done, 1)
                act.wait_ge(done, T)
                nc.scalar.nop().then_inc(pair_free[c % 2], 1)
                nc.scalar.preload_act_table_set(LOG_EXP)

            for i in range(1, 5):
                hi(S1 + i)
            rT_copy(0)
            hi(S1 + 5)
            rT_copy(1)
            hi(S1 + 6)
            gelu(zz, 18, zg_made)
            exp_step(0)
            hi(S1 + 7)
            exp_step(1)
            pT_copy(0)
            exp_step(2)
            pT_copy(1)
            hi(S1 + 8)
            exp_step(3)
            pT_copy(2)
            exp_step(4)
            act.wait_ge(zss_made, 1)
            rsqrt(zy, zss, HD, LN_EPS)
            pT_copy(3)
            hi(S1 + 9)
            exp_step(5)
            pT_copy(4)
            nc.scalar.preload_act_table_set("gelu_and_others")
            gelu(uu, 19, u_made)
            exp_step(6)
            pT_copy(5)
            hi(S1 + 10)
            exp_step(7)
            pT_copy(6)
            pT_copy(7)
            act.wait_ge(unit_used, S1 + 10)
            copy(v[:].rearrange("p t w -> p (t w)"), two_banks(20)).then_inc(v2_made, 1)
            act.wait_ge(v2_made, 1)
            nc.scalar.nop().then_inc(pair_free[0], 1)

            def branch_norm(src, made, ss, y):
                for t in range(T):
                    act.wait_ge(made, t + 1)
                    step(nc.scalar.activation(junk2[:, t, :], src[:, t, :], ACT.Square, accum_out=ss[:, t:t + 1]))
                rsqrt(y, ss, W, RMS_EPS)

            def gT_copy(b):
                t, k0 = b % 2, 4 - 4 * (b // 2)
                act.wait_ge(full_made, FULL_G + b + 1)
                copy(gT_hi[:, k0:k0 + 4, t * P:(t + 1) * P],
                     full[:, b, :].rearrange("p (k n) -> p k n", k=4)).then_inc(upper_made, 1)

            branch_norm(zz, sg_made, ssg[:, 2:4], yg[:, 2:4])
            hi(S1 + 11)
            gT_copy(0)
            gT_copy(1)
            branch_norm(atto, o_made, ssg[:, 0:2], yg[:, 0:2])
            hi(S1 + 12)
            gT_copy(2)
            gT_copy(3)
            hi(S1 + 13)
            hi(SFF)
            hi(SFF + 1)
            for t in range(T):
                act.wait_ge(var_made, t + 1)
                rsqrt(yl[:, t:t + 1], mv[:, t, 1:2], 1, LN_EPS)
            for b in range(4):
                t, k0 = b // 2, 4 * (b % 2)
                act.wait_ge(turned_ps, PS_X3 + b + 1)
                for k in range(4):
                    ins = nc.scalar.activation(full[:, b, k * P:(k + 1) * P], ps[:, 4 + b, k * P:(k + 1) * P],
                                               ACT.Identity, scale=ln1gT[:, k0 + k:k0 + k + 1],
                                               bias=ln1bT[:, k0 + k:k0 + k + 1])
                step(ins)
                copy(xT_hi[:, k0:k0 + 4, t * P:(t + 1) * P],
                     full[:, b, :].rearrange("p (k n) -> p k n", k=4)).then_inc(upper_made, 1)
            nc.scalar.preload_act_table_set("silu_and_others")

            def hi_in(i, turn):
                if turn is None:
                    return hi(i)
                slot, value = slot_of(load_of(i))
                act.wait_ge(land[slot], turn * 16 + value)
                act.wait_ge(unit_used, turn * RING + (i - 1))
                copy(w_hi[:, i % 2, :], ring[:, slot, :]).then_inc(hi_made, 1)

            def ffn_hidden(c, turn, between):
                n = c if turn is None else turn * LOOP_B + c
                u = SFF + 1 if c == 0 else body_unit(c)
                act.wait_ge(unit_used, (u if c == 0 else u + 1) if turn is None else turn * RING + (u + 1))
                if c >= 1:
                    act.wait_ge(hid_made, n)
                nc.scalar.activation(sil2[:].rearrange("p m n -> p (m n)"), ps[:, 4 + 2 * (c % 2), :],
                                     ACT.Silu).then_inc(sil2_made, 1)
                between()
                act.wait_ge(hid_made, n + 1)
                if c == NCH - 1:
                    act.wait_ge(unit_used, body_unit(c) + 3)
                copy(hid_hi[:], hid[:]).then_inc(hidhi_made, 1)

            def ffn_body(c, turn=None):
                i = body_unit(c)
                if i >= SFF + 2:
                    hi_in(i, turn)
                ffn_hidden(c - 1, turn, lambda: hi_in(i + 1, turn))
                hi_in(i + 2, turn)

            ffn_body(1)
            with act.Fori(0, LOOP_N) as turn:
                for c in range(2, 2 + LOOP_B):
                    ffn_body(c, turn)
            ffn_body(NCH - 1)
            ffn_hidden(NCH - 1, None, lambda: hi(body_unit(NCH)))
            nc.scalar.preload_act_table_set(LOG_EXP)
            for t in range(T):
                act.wait_ge(var_made, T + t + 1)
                rsqrt(yl[:, t:t + 1], mv[:, t, 1:2], 1, LN_EPS)

        @block.vector
        def _(dve):
            tt, ts, stt = nc.vector.tensor_tensor, nc.vector.tensor_scalar, nc.vector.scalar_tensor_tensor
            red = nc.vector.tensor_reduce
            own = [0]

            def step(ins):
                own[0] += 1
                ins.then_inc(dve_own, 1)
                dve.wait_ge(dve_own, own[0])

            def f32(ap):
                return ap.bitcast(F32)

            roots = [0]

            def refine(y, ss, n, eps):
                roots[0] += 1
                dve.wait_ge(root_made, roots[0])
                k = y.shape[1]
                a, b = nw[:, 0, 0:k], nw[:, 1, 0:k]
                ts(a, ss, 1.0 / n, eps, ALU.mult, ALU.add)
                step(tt(b, y, y, ALU.mult))
                step(tt(a, a, b, ALU.mult))
                step(ts(a, a, -0.5, 1.5, ALU.mult, ALU.add))
                step(tt(y, y, a, ALU.mult))

            def lo(i):
                slot, _ = slot_of(load_of(i))
                dve.wait_ge(hi_made, i + 1)
                tt(w_lo[:, i % 2, :], ring[:, slot, :], f32(w_hi[:, i % 2, :]), ALU.subtract).then_inc(lo_made, 1)

            def bc(ap, n):
                return ap.unsqueeze(2).to_broadcast([ap.shape[0], ap.shape[1], n])

            for t in range(T):
                refine(y1[:, t:t + 1], ss1[:, t:t + 1], D, RMS_EPS)
                ts(xn[:, t, :], X[:, t, :], y1[:, t:t + 1], None, ALU.mult).then_inc(xn_made, 1)
            dve.wait_ge(land_id, 16 * 2)

            def scaled(b, base, g, bank):
                dve.wait_ge(turned_ps, base + b + 1)
                tt(full[:, b, :].rearrange("p (k n) -> p k n", k=4),
                   ps[:, bank + b, :].rearrange("p (k n) -> p k n", k=4), bc(g, P), ALU.mult).then_inc(full_made, 1)

            def lower_split(b, k0, t, base, dst_hi, dst_lo):
                dve.wait_ge(upper_made, base + b + 1)
                tok = slice(t * P, (t + 1) * P)
                tt(dst_lo[:, k0:k0 + 4, tok], full[:, b, :].rearrange("p (k n) -> p k n", k=4),
                   f32(dst_hi[:, k0:k0 + 4, tok]), ALU.subtract).then_inc(split_made, 1)

            def h_scaled(b):
                scaled(b, PS_H, g1[:, 4 * (b % 2):4 * (b % 2) + 4], 0)

            def h_lower(b):
                lower_split(b, 4 * (b % 2), b // 2, SP_H, hT_hi, hT_lo)

            h_scaled(0)
            h_scaled(1)
            h_lower(0)
            h_scaled(2)
            h_lower(1)
            h_scaled(3)
            lo(0)
            h_lower(2)
            h_lower(3)
            lo(1)
            dve.wait_ge(land_qk, 16 * 4)
            ts(gq, gq, HD ** -0.5, None, ALU.mult).then_inc(dve_own, 1)
            own[0] += 1
            lo(2)

            def qk_norm(which):
                dve.wait_ge(qk_sq, which + 1)
                y, ss = (yk, yq)[which], (ssk, ssq)[which]
                red(ss, sq[:].rearrange("p t (h d) -> p (t h) d", d=HD), AX, ALU.add).then_inc(qk_ss, 1)
                refine(y, ss, HD, RMS_EPS)
                tt(qk[:, which].rearrange("p t (h d) -> p (t h) d", d=HD),
                   ps[:, 2 * which:2 * which + 2, :].rearrange("p t (h d) -> p (t h) d", d=HD), bc(y, HD),
                   ALU.mult).then_inc(qk_made, 1)
                dve.wait_ge(qk_made, which + 1)
                nc.vector.engine_nop().then_inc(pair_free[which], 1)

            def zb(p):
                return ps[:, 4 + 2 * (p % 2):6 + 2 * (p % 2), 0:384]

            def sp_step(p):
                dve.wait_ge(log_made, p + 1)
                stt(stick[:], zb(p), 0.0, stick[:], ALU.max, ALU.add).then_inc(sp_made, 1)

            def brlo_step(p):
                dve.wait_ge(brhi_made, p + 1)
                tt(brT_lo[:, 0, p, :], ps[:, 4 + 2 * (p % 2), 0:SEQ], f32(brT_hi[:, 0, p, :]),
                   ALU.subtract).then_inc(br_made, 1)

            lo(3)
            qk_norm(0)
            lo(4)
            lo(5)
            qk_norm(1)
            lo(6)
            lo(7)
            lo(8)
            sp_step(0)
            lo(9)
            sp_step(1)
            lo(10)
            brlo_step(0)
            lo(11)
            brlo_step(1)
            sp_step(2)
            lo(12)
            sp_step(3)
            lo(13)
            brlo_step(2)
            lo(14)
            brlo_step(3)
            lo(15)

            def banks4(c):
                return ps[:, 2 * (c % 2):2 * (c % 2) + 2, :].rearrange("p b (m n) -> p (b m) n", n=SEQ)

            dve.wait_ge(land_taps, 16)
            dve.wait_ge(cc_made, 1)
            dve.wait_ge(unit_used, 2 * CH_CU + 2)
            tt(cu[:], banks4(CH_CU), cu[:], ALU.mult).then_inc(pair_free[0], 1)
            dve.wait_ge(pair_free[0], 4)
            for m in range(4):
                ts(cy[:, m, :], cu[:, m, :], cw[:, 2, m:m + 1], None, ALU.mult).then_inc(dve_own, 1)
            own[0] += 4
            dve.wait_ge(dve_own, own[0])
            lo(16)
            for j in (1, 0):
                off = 2 - j
                for m in range(4):
                    stt(cy[:, m, off:SEQ], cu[:, m, 0:SEQ - off], cw[:, j, m:m + 1], cy[:, m, off:SEQ], ALU.mult,
                        ALU.add).then_inc(dve_own, 1)
                own[0] += 4
                dve.wait_ge(dve_own, own[0])
            lo(17)
            dve.wait_ge(unit_used, 2 * CH_CB + 2)
            tt(cy[:], banks4(CH_CB), cy[:], ALU.mult).then_inc(conv_made, 1)
            dve.wait_ge(conv_made, 1)
            nc.vector.engine_nop().then_inc(pair_free[1], 1)
            dve.wait_ge(convhi_made, 1)
            tt(brT_lo[:, 1], cy[:], f32(brT_hi[:, 1]), ALU.subtract).then_inc(conv_split, 1)
            for i in range(18, 23):
                lo(i)
            dve.wait_ge(ga_sig, 1)
            dve.wait_ge(gb_sig, 1)
            for h in range(2):
                m4 = slice(4 * h, 4 * h + 4)
                dve.wait_ge(unit_used, 21 + 2 * h)
                if h == 1:
                    dve.wait_ge(mgT_made, 1)
                tt(mg1[:], banks4(10 + 2 * h), ga[:, m4, :], ALU.mult).then_inc(pair_free[0], 1)
                if h == 0:
                    lo(23)
                dve.wait_ge(unit_used, 22 + 2 * h)
                tt(mg2[:], banks4(11 + 2 * h), gb[:, m4, :], ALU.mult).then_inc(pair_free[1], 1)
                dve.wait_ge(pair_free[0], 6 + h)
                dve.wait_ge(pair_free[1], 6 + h)
                tt(mg1[:], mg1[:], mg2[:], ALU.add).then_inc(mg_made, 1)
                dve.wait_ge(mghi_made, h + 1)
                tt(mgT_lo[:, m4, :], mg1[:], f32(mgT_hi[:, m4, :]), ALU.subtract).then_inc(mgT_made, 1)
                lo(24 + 2 * h)
                lo(25 + 2 * h)
            for h in range(2):
                for t in range(T):
                    if h == 0:
                        dve.wait_ge(unit_used, 27)
                    elif t == 0:
                        dve.wait_ge(half_used, 1)
                    else:
                        dve.wait_ge(unit_used, 28)
                    tt(X[:, t, h * 512:(h + 1) * 512], ps[:, 2 * h + t, :], X[:, t, h * 512:(h + 1) * 512],
                       ALU.add).then_inc(x2_made, 1)
                dve.wait_ge(x2_made, T * (h + 1))
                nc.vector.engine_nop().then_inc(pair_free[h], 1)

            dve.wait_ge(land_small, 16 * 10)
            for b in range(4):
                t, k0 = b // 2, 4 * (b % 2)
                dve.wait_ge(turned_ps, PS_R + b + 1)
                tt(h2T[:, k0:k0 + 4, t * P:(t + 1) * P], ps[:, 4 + b, :].rearrange("p (k n) -> p k n", k=4),
                   bc(g2[:, k0:k0 + 4], P), ALU.mult).then_inc(h2T_made, 1)
            refine(y2, ss2, D, RMS_EPS)
            for t in range(T):
                ts(h2n[:, t, :], X[:, t, :], y2[:, t:t + 1], None, ALU.mult).then_inc(h2n_made, 1)

            pos = [0]

            def cell(n):
                a = pos[0]
                pos[0] += n
                return rt[:, a:a + n]

            def tg(ap, n):
                return ap.rearrange("p (t n) -> p t n", n=n)

            assign = cell(T * NE)
            gexp = cell(T * NG)
            eexp = cell(T)
            comb = cell(T * NE)
            place = cell(T * NE)
            logits = tg(cell(T * 36), 36)
            goh, gtmp = tg(cell(T * NG), NG), tg(cell(T * NG), NG)
            egrp, emask = tg(cell(T * EPG), EPG), tg(cell(T * EPG), EPG)
            oh1, oh2, etmp = (tg(cell(T * EPG), EPG) for _ in range(3))
            prod = cell(T * NE)
            gmax, gi, gsum, m1, m2, i1, den, wt1, wt2, gw = (cell(T) for _ in range(10))
            counts, over = cell(1), cell(8)
            i8 = iota[:, 0:EPG].unsqueeze(1).to_broadcast([P, T, EPG])
            i4 = iota[:, 0:NG].unsqueeze(1).to_broadcast([P, T, NG])

            def first_max(vals, n, mxv, idx, onehot, tmp, iot):
                step(red(mxv, vals, AX, ALU.max))
                step(tt(tmp, vals, bc(mxv, n), ALU.is_ge))
                step(stt(tmp, tmp, -64.0, iot, ALU.mult, ALU.add))
                step(red(idx, tmp, AX, ALU.min))
                step(tt(onehot, tmp, bc(idx, n), ALU.is_equal))

            dve.wait_ge(logit_ps, 1)
            dve.wait_ge(h2n_made, T)
            for t in range(T):
                ins = stt(logits[:, t, :], ps[:, 6, t * 36:t * 36 + 36], y2[:, t:t + 1], rbias, ALU.mult, ALU.add)
            step(ins)
            lg = logits[:, :, 0:NG]
            first_max(lg, NG, gmax, gi, goh, gtmp, i4)
            tt(tg(gexp, NG), lg, bc(gmax, NG), ALU.subtract).then_inc(gdiff_made, 1)
            for t in range(T):
                tt(prod[:, t * NE:(t + 1) * NE].rearrange("p (g e) -> p g e", g=NG),
                   logits[:, t, NG:NG + NE].rearrange("p (g e) -> p g e", g=NG),
                   bc(goh[:, t, :], EPG), ALU.mult).then_inc(dve_own, 1)
            own[0] += T
            dve.wait_ge(dve_own, own[0])
            step(red(egrp, prod.rearrange("p (t g e) -> p t e g", t=T, g=NG), AX, ALU.add))
            first_max(egrp, EPG, m1, i1, oh1, etmp, i8)
            step(stt(emask, oh1, -3e38, egrp, ALU.mult, ALU.add))
            first_max(emask, EPG, m2, i1, oh2, etmp, i8)
            tt(eexp, m2, m1, ALU.subtract).then_inc(gdiff_made, 1)
            step(tt(etmp, oh1, oh2, ALU.add))
            for t in range(T):
                ins = tt(assign[:, t * NE:(t + 1) * NE].rearrange("p (g e) -> p g e", g=NG), bc(goh[:, t, :], EPG),
                         etmp[:, t, :].unsqueeze(1).to_broadcast([P, NG, EPG]), ALU.mult)
                step(ins)
            nc.vector.engine_nop().then_inc(assign_made, 1)
            dve.wait_ge(rank_ps, 1)
            step(stt(place, ps[:, 7, 0:T * NE], 1.0, assign, ALU.add, ALU.mult))
            ts(place, place, -1.0, None, ALU.add).then_inc(place_made, 1)
            red(counts, ps[:, 7, T * NE:T * NE + NE], AX, ALU.max).then_inc(place_made, 1)

            def slots(it, q, s, r=None):
                if r is not None:
                    dve.wait_ge(next_round, r + 1)
                dve.wait_ge(s["gath_ps"], it + 1)
                for t in range(T):
                    e = q * QUAD + t * NE
                    ins = tt(pick[:, t, :].rearrange("p (j c) -> p j c", j=QUAD),
                             iota.unsqueeze(1).to_broadcast([P, QUAD, CAP]),
                             place[:, bass.ds(e, QUAD)].unsqueeze(2).to_broadcast([P, QUAD, CAP]), ALU.is_equal)
                ins.then_inc(s["pick_made"], 1)

            def weighted_slots(it, q, s):
                dve.wait_ge(s["pick_made"], it + 1)
                dve.wait_ge(s["aT_ps"], it + 1)
                for t in range(T):
                    e = q * QUAD + t * NE
                    ins = tt(pickw[:, t, :].rearrange("p (j c) -> p j c", j=QUAD),
                             pick[:, t, :].rearrange("p (j c) -> p j c", j=QUAD),
                             comb[:, bass.ds(e, QUAD)].unsqueeze(2).to_broadcast([P, QUAD, CAP]), ALU.mult)
                ins.then_inc(s["pickw_made"], 1)

            def gathered(it, s):
                dve.wait_ge(s["gath_ps"], it + 2)
                for b in range(2):
                    ins = tt(heT[:, 4 * b:4 * b + 4, :], ps[:, 6 + b, :].rearrange("p (k n) -> p k n", k=4),
                             bc(g2[:, 4 * b:4 * b + 4], P), ALU.mult)
                ins.then_inc(s["heT_made"], 1)

            def hidden(it, s):
                dve.wait_ge(s["sil_made"], it + 1)
                dve.wait_ge(s["used"], it * UPQ + (8 + s["start"]))
                tt(act_e[:], ps[:, 5, 0:FE], sil[:], ALU.mult).then_inc(s["act_made"], 1)
                dve.wait_ge(s["used"], it * UPQ + (UPQ + s["start"]))
                nc.vector.tensor_copy(ysb[:, 512:1024], ps[:, 7, :]).then_inc(s["y_made"], 1)

            def quad(it, q, s, r=None):
                slots(it, q, s, r)
                weighted_slots(it, q, s)
                gathered(it, s)
                hidden(it, s)

            next_round = sem("next_round")
            start0, start1 = first | {"start": 0}, more | {"start": UPQ}
            dve.wait_ge(place_made, 2)
            slots(0, 0, start0)
            dve.wait_ge(gexp_made, 2)
            step(red(gsum, tg(gexp, NG), AX, ALU.add))
            step(nc.vector.reciprocal(gw, gsum))
            step(ts(den, eexp, 1.0, None, ALU.add))
            step(nc.vector.reciprocal(den, den))
            step(tt(wt1, den, gw, ALU.mult))
            step(tt(wt2, wt1, eexp, ALU.mult))
            step(tt(egrp, oh1, bc(wt1, EPG), ALU.mult))
            gathered(0, start0)
            step(tt(emask, oh2, bc(wt2, EPG), ALU.mult))
            step(tt(egrp, egrp, emask, ALU.add))
            for t in range(T):
                step(tt(comb[:, t * NE:(t + 1) * NE].rearrange("p (g e) -> p g e", g=NG), bc(goh[:, t, :], EPG),
                        egrp[:, t, :].unsqueeze(1).to_broadcast([P, NG, EPG]), ALU.mult))
            weighted_slots(0, 0, start0)
            step(ts(over[:, 0:7], thr, counts, None, ALU.is_lt))
            step(red(over[:, 7:8], over[:, 0:7], AX, ALU.add))
            nc.vector.tensor_copy(cnt[:, 0:1], over[:, 7:8]).then_inc(count_made, 1)
            hidden(0, start0)
            with dve.Fori(1, NQ) as q:
                quad(q, q, start0)
            dve.wait_ge(count_made, 1)
            extra = dve.value_load(cnt[0:1, 0:1], min_val=0, max_val=7)
            with dve.If(extra > 0):
                with dve.Fori(0, extra) as r:
                    ts(place, place, -float(CAP), None, ALU.add).then_inc(next_round, 1)
                    with dve.Fori(0, NQ) as q:
                        quad(r * NQ + q, q, start1, r)
            dve.wait_ge(more["spread"], extra * NQ + 1)
            lo(S1)

            dve.wait_ge(first["spread"], NQ + 1)
            for t in range(T):
                nc.vector.tensor_copy(X[:, t, 512:D], ps[:, 2 * t + 1, :]).then_inc(sum_d, 1)

            def lower_ps(b):
                t, k0 = b // 2, 4 * (b % 2)
                tok = slice(t * P, (t + 1) * P)
                dve.wait_ge(upper_made, SP_X2 + b + 1)
                tt(xT_lo[:, k0:k0 + 4, tok], ps[:, 4 + b, :].rearrange("p (k n) -> p k n", k=4),
                   f32(xT_hi[:, k0:k0 + 4, tok]), ALU.subtract).then_inc(split_made, 1)

            for b in range(4):
                lower_ps(b)
            lo(S1 + 1)
            lo(S1 + 2)
            dve.wait_ge(spT_ps, 1)
            tt(spT[:], ps[:, 4:6, :].rearrange("p b (g n) -> p (b g) n", n=P),
               triu.unsqueeze(1).to_broadcast([P, NH, P]), ALU.mult).then_inc(spT_made, 1)
            lo(S1 + 3)

            def rope(which):
                dve.wait_ge(unit_used, S1 + 2 * which + 2)
                if which:
                    dve.wait_ge(rope_made, 1)
                for t in range(T):
                    src = ps[:, 2 * (which % 2) + t, :].rearrange("p (h d) -> p h d", d=HD)
                    dst = qk[:, which, t, :].rearrange("p (h d) -> p h d", d=HD)
                    tmp = sq[:, t, :].rearrange("p (h d) -> p h d", d=HD)

                    def along(tab, a, b):
                        return tab[:, t, a:b].unsqueeze(1).to_broadcast([P, NH, b - a])

                    tt(dst, src, along(cos, 0, HD), ALU.mult)
                    tt(tmp[:, :, 0:HD // 2], src[:, :, HD // 2:HD], along(sin, 0, HD // 2), ALU.mult)
                    ins = tt(tmp[:, :, HD // 2:HD], src[:, :, 0:HD // 2], along(sin, HD // 2, HD), ALU.mult)
                ins.then_inc(pair_free[which], 1)
                dve.wait_ge(pair_free[which], 9)
                tt(qk[:, which], qk[:, which], sq[:], ALU.add).then_inc(rope_made, 1)

            def max_step(h):
                dve.wait_ge(s_ps, h + 1)
                red(mx[:, h, 0:1], ps[:, 4 + h % 2, 0:P], AX, ALU.max)
                step(red(mx[:, h, 1:2], ps[:, 4 + h % 2, P:P + SEQ], AX, ALU.max))
                ts(mxn[:, h, :], mx[:, h, :], -(HD ** -0.5), None, ALU.mult).then_inc(mx_made, 1)

            rope(0)
            lo(S1 + 4)
            lo(S1 + 5)
            rope(1)
            lo(S1 + 6)
            max_step(0)
            dve.wait_ge(zg_made, T)
            step(red(zs, zz[:].rearrange("p t (g d) -> p (t g) d", d=HD), AX, ALU.add))
            ts(zs, zs, 1.0 / HD, None, ALU.mult).then_inc(zmean_made, 1)
            max_step(1)
            lo(S1 + 7)
            max_step(2)
            max_step(3)
            lo(S1 + 8)
            max_step(4)
            dve.wait_ge(zq_made, 1)
            red(zss, sq[:].rearrange("p t (g d) -> p (t g) d", d=HD), AX, ALU.add).then_inc(zss_made, 1)
            max_step(5)
            lo(S1 + 9)
            refine(zy, zss, HD, LN_EPS)
            nc.vector.engine_nop().then_inc(zy_ready, 1)
            max_step(6)
            max_step(7)
            lo(S1 + 10)
            dve.wait_ge(mix_ps, 1)
            for t in range(T):
                mixed = ps[:, 2:4, :].rearrange("p b n -> p (b n)").rearrange("p (g t d) -> p t g d", g=NH, t=T)
                ins = tt(zz[:, t, :].rearrange("p (g d) -> p g d", d=HD), mixed[:, t], bc(bsp, HD), ALU.add)
            step(ins)
            nc.vector.engine_nop().then_inc(pair_free[1], 1)
            dve.wait_ge(u_made, T)
            for t in range(T):
                tt(zz[:, t, :], zz[:, t, :], uu[:, t, :], ALU.mult).then_inc(sg_made, 1)

            def branch_norm(src, ss, y):
                refine(y, ss, W, RMS_EPS)
                for t in range(T):
                    ts(src[:, t, :], src[:, t, :], y[:, t:t + 1], None, ALU.mult).then_inc(cat_made, 1)

            def g_scaled(b):
                k0 = 4 - 4 * (b // 2)
                scaled(b, PS_G, gmix[:, k0:k0 + 4], 4)

            def g_lower(b):
                lower_split(b, 4 - 4 * (b // 2), b % 2, SP_G, gT_hi, gT_lo)

            branch_norm(zz, ssg[:, 2:4], yg[:, 2:4])
            lo(S1 + 11)
            g_scaled(0)
            g_scaled(1)
            g_lower(0)
            g_lower(1)
            step(nc.vector.reciprocal(rinv, rsum))
            dve.wait_ge(o_ps, 1)
            for t in range(T):
                tt(atto[:, t, :].rearrange("p (h d) -> p h d", d=HD), ps[:, 6 + t, :].rearrange("p (h d) -> p h d", d=HD),
                   rinv[:, :, t:t + 1].to_broadcast([P, NH, HD]), ALU.mult).then_inc(o_made, 1)
            branch_norm(atto, ssg[:, 0:2], yg[:, 0:2])
            lo(S1 + 12)
            g_scaled(2)
            g_scaled(3)
            g_lower(2)
            g_lower(3)
            lo(S1 + 13)

            def half(h):
                return slice(h * 512, (h + 1) * 512)

            def residual(h, t, bank):
                step(stt(X[:, t, half(h)], X[:, t, half(h)], ALPHA, ps[:, bank, :], ALU.mult, ALU.add))
                nc.vector.bn_stats(bst[:, t, h, :], X[:, t, half(h)]).then_inc(dve_own, 1)
                own[0] += 1

            def tile_stats(t):
                dve.wait_ge(dve_own, own[0])
                nc.vector.bn_aggr(mv[:, t, :], bst[:, t, :, :]).then_inc(var_made, 1)
                refine(yl[:, t:t + 1], mv[:, t, 1:2], 1, LN_EPS)

            dve.wait_ge(unit_used, S1 + 13)
            for t in range(T):
                residual(0, t, t)
            lo(SFF)
            for t in range(T):
                if t == 0:
                    dve.wait_ge(half_used, 2)
                else:
                    dve.wait_ge(unit_used, S1 + 14)
                residual(1, t, 2 + t)
                tile_stats(t)
                ts(X[:, t, :], X[:, t, :], mv[:, t, 0:1], yl[:, t:t + 1], ALU.subtract,
                   ALU.mult).then_inc(xhat_made, 1)
            lo(SFF + 1)
            for b in range(4):
                lower_split(b, 4 * (b % 2), b // 2, SP_X3, xT_hi, xT_lo)

            def lo_in(i, turn):
                if turn is None:
                    return lo(i)
                slot, _ = slot_of(load_of(i))
                dve.wait_ge(hi_made, turn * RING + (i + 1))
                tt(w_lo[:, i % 2, :], ring[:, slot, :], f32(w_hi[:, i % 2, :]), ALU.subtract).then_inc(lo_made, 1)

            def ffn_hidden(c, turn, between):
                n = c if turn is None else turn * LOOP_B + c
                u = SFF + 1 if c == 0 else body_unit(c) + 1
                dve.wait_ge(sil2_made, n + 1)
                if c >= 1:
                    dve.wait_ge(hidT_made, n)
                dve.wait_ge(unit_used, u + 1 if turn is None else turn * RING + (u + 1))
                tt(hid[:].rearrange("p m n -> p (m n)"), ps[:, 5 + 2 * (c % 2), :],
                   sil2[:].rearrange("p m n -> p (m n)"), ALU.mult).then_inc(hid_made, 1)
                between()
                dve.wait_ge(hidhi_made, n + 1)
                tt(hid_lo[:], hid[:], f32(hid_hi[:]), ALU.subtract).then_inc(hidT_made, 1)

            def ffn_body(c, turn=None):
                i = body_unit(c)
                lo_in(i, turn)
                ffn_hidden(c - 1, turn, lambda: lo_in(i + 1, turn))
                lo_in(i + 2, turn)

            ffn_body(1)
            with dve.Fori(0, LOOP_N) as turn:
                for c in range(2, 2 + LOOP_B):
                    ffn_body(c, turn)
            ffn_body(NCH - 1)
            ffn_hidden(NCH - 1, None, lambda: lo(body_unit(NCH)))
            dve.wait_ge(x3_made, T)
            dve.wait_ge(land_ln2, 16 * 2)
            for t in range(T):
                for h in range(2):
                    dve.wait_ge(y_ps, 2 * t + h + 1)
                    residual(h, t, 2 * t + h)
                tile_stats(t)
                for h in range(2):
                    x = X[:, t, half(h)]
                    step(ts(x, x, mv[:, t, 0:1], yl[:, t:t + 1], ALU.subtract, ALU.mult))
                    step(tt(x, x, ln2[:, 0, half(h)], ALU.mult))
                    tt(x, x, ln2[:, 1, half(h)], ALU.add).then_inc(y_out, 1)

        @block.gpsimd
        def _(pool):
            tt = nc.gpsimd.tensor_tensor

            def groups(ap):
                return ap.rearrange("p t (g d) -> p (t g) d", d=HD)

            def by_group(ap):
                return ap.unsqueeze(2).to_broadcast([P, T * NH, HD])

            def row(i):
                return lngb[:, i, :].unsqueeze(1).to_broadcast([P, T, W])

            pool.wait_ge(zmean_made, 1)
            tt(groups(zz[:]), groups(zz[:]), by_group(zs), ALU.subtract).then_inc(zc_made, 1)
            pool.wait_ge(zc_made, 1)
            tt(sq[:], zz[:], zz[:], ALU.mult).then_inc(zq_made, 1)
            pool.wait_ge(zq_made, 1)
            pool.wait_ge(land_b2, 16 * 3)
            pool.wait_ge(zy_ready, 1)
            tt(groups(zz[:]), groups(zz[:]), by_group(zy), ALU.mult).then_inc(zn_made, 1)
            pool.wait_ge(zn_made, 1)
            tt(zz[:], zz[:], row(0), ALU.mult).then_inc(zn_made, 1)
            pool.wait_ge(zn_made, 2)
            tt(zz[:], zz[:], row(1), ALU.add).then_inc(z_made, 1)
            pool.wait_ge(land_ln1, 16 * 2)
            pool.wait_ge(turned_ps, PS_X3 + 4)
            for t in range(T):
                tt(X[:, t, :], X[:, t, :], ln1[:, 0, :], ALU.mult).then_inc(x3g_made, 1)
                pool.wait_ge(x3g_made, t + 1)
                tt(X[:, t, :], X[:, t, :], ln1[:, 1, :], ALU.add).then_inc(x3_made, 1)


_INS = ["x", "norm_mix_g", "w_in", "q_norm_g", "k_norm_g", "conv_w", "w_sb_branch", "w_conv_branch", "w_out",
        "norm_ffn_g", "w_router_group", "b_router_group", "w_router_expert", "b_router_expert", "w_gate_e",
        "w_up_e", "w_down_e", "w_in_2", "attn_out_g_2", "gmlp_out_g_2", "gmlp_ln_g_2", "gmlp_ln_b_2",
        "w_spatial_2", "b_spatial_2", "w_out_2", "ln1_g_2", "ln1_b_2", "w_gate_2", "w_up_2", "w_down_2",
        "ln2_g_2", "ln2_b_2"]


def kernel(**inputs):
    import concourse.bacc as _bacc
    from concourse import mybir as _mybir
    from concourse.bass_utils import run_bass_kernel_spmd as _run

    nc = _bacc.Bacc("TRN2", target_bir_lowering=False, num_devices=1, dynamic_dma_scratch_size=256)
    arrays = {"in_consts": shape_constants()}
    for name in _INS:
        arrays[f"in_{name}"] = np.ascontiguousarray(inputs[name])
    args = [nc.dram_tensor(n, a.shape, _mybir.dt.from_np(a.dtype), kind="ExternalInput").ap()
            for n, a in arrays.items()]
    res = nc.dram_tensor("out_0", (1, SEQ, D), _mybir.dt.float32, kind="ExternalOutput").ap()
    build(nc, *args, res)
    r = _run(nc, [arrays], core_ids=[0])
    return r.results[0]["out_0"]
```

```python
from contextlib import ExitStack

import numpy as np

import concourse.bass as bass
from concourse import mybir

F32 = mybir.dt.float32
F32R = mybir.dt.float32r
BF16 = mybir.dt.bfloat16
I32 = mybir.dt.int32
ALU = mybir.AluOpType
ACT = mybir.ActivationFunctionType
AX = mybir.AxisListType.X

P = 128
KB = 1024
SEQ, D = 256, 1024
T = SEQ // P
KD = D // P
HD = 64
NH = 8
W = NH * HD
PAIRS = NH // 2
NG, EPG = 4, 8
NE = NG * EPG
FE = 256
KF = FE // P
QUAD = 4
NQ = NE // QUAD
CAP = 32
FFN = -(-(8 * D) // (3 * 256)) * 256
FCHUNK = 256
NCH = FFN // FCHUNK
MF = FCHUNK // P
ALPHA = 2.0 ** 0.25
RMS_EPS, LN_EPS = 1e-6, 1e-5
NEG = -1e30

RING = 12
UNIT = 2048
KU = 4
UPQ = 12
GU = 8
EARLY = 11
AGAIN = 3
AGAIN_AT = GU + EARLY + RING
SKIP = EARLY + AGAIN
B1_UNITS = 28
B1_PROJ = 20
MOE_UNITS = UPQ * NQ
B2_PRE = 14
S1 = B1_UNITS
SFF = S1 + B2_PRE

C_ID, C_NEGU, C_NEGO, C_LTRI, C_ONE, C_TRIU, C_MK1, C_MK2 = (P * i for i in range(8))
C_COS = 8 * P
C_SIN = C_COS + T * HD
C_IOTA = C_SIN + T * HD
C_THR = C_IOTA + CAP
C_N = C_THR + 8


def shape_constants():
    c = np.zeros((P, C_N), np.float32)
    r, k = np.arange(P)[:, None], np.arange(P)[None, :]
    c[:, C_ID:C_ID + P] = r == k
    c[:, C_NEGU:C_NEGU + P] = -(r >= k).astype(np.float32)
    c[:, C_NEGO:C_NEGO + P] = -1.0
    c[:, C_LTRI:C_LTRI + P] = r < k
    c[:, C_ONE:C_ONE + P] = 1.0
    c[:, C_TRIU:C_TRIU + P] = k >= r
    c[:, C_MK1:C_MK1 + P] = np.where(r < k, 0.0, NEG)
    c[:, C_MK2:C_MK2 + P] = np.where(k <= r, 0.0, NEG)
    inv = (np.float32(10000.0) ** (-np.arange(0, HD, 2, dtype=np.float32) / np.float32(HD))).astype(np.float32)
    ang = np.arange(SEQ, dtype=np.float32)[:, None] * inv[None, :]
    cos, sin = np.cos(ang).astype(np.float32), np.sin(ang).astype(np.float32)
    cos = np.concatenate([cos, cos], -1).reshape(T, P, HD)
    sin = np.concatenate([-sin, sin], -1).reshape(T, P, HD)
    c[:, C_COS:C_COS + T * HD] = cos.transpose(1, 0, 2).reshape(P, T * HD)
    c[:, C_SIN:C_SIN + T * HD] = sin.transpose(1, 0, 2).reshape(P, T * HD)
    c[:, C_IOTA:C_IOTA + CAP] = np.arange(CAP)
    c[:, C_THR:C_THR + 8] = CAP * (np.arange(8) + 1)
    return c


def build(nc, consts, x, norm_mix_g, w_in, q_norm_g, k_norm_g, conv_w, w_sb_branch, w_conv_branch, w_out,
          norm_ffn_g, w_router_group, b_router_group, w_router_expert, b_router_expert, w_gate_e, w_up_e,
          w_down_e, w_in_2, attn_out_g_2, gmlp_out_g_2, gmlp_ln_g_2, gmlp_ln_b_2, w_spatial_2, b_spatial_2,
          w_out_2, ln1_g_2, ln1_b_2, w_gate_2, w_up_2, w_down_2, ln2_g_2, ln2_b_2, out):
    with ExitStack() as ctx:
        def sem(name):
            return ctx.enter_context(nc.semaphore(name))

        def at(name, kib, shape, dt=F32):
            return nc.alloc_sbuf_tensor_at(name, shape, dt, offset=256 + int(kib * KB))

        ps = ctx.enter_context(nc.psum_tensor("ps", [P, 8, 512], F32))

        ring = at("ring", 0, [P, RING, UNIT])
        w_hi = at("w_hi", 96, [P, 2, UNIT], F32R)
        w_lo = at("w_lo", 112, [P, 2, UNIT], F32R)
        hT_hi = at("hT_hi", 128, [P, KD, SEQ], F32R)
        hT_lo = at("hT_lo", 136, [P, KD, SEQ], F32R)
        brT_hi = at("brT_hi", 144, [P, 2, 4, SEQ], F32R)
        brT_lo = at("brT_lo", 152, [P, 2, 4, SEQ], F32R)
        early = at("early", 96, [P, 8, UNIT])
        early_a = at("early_a", 212, [P, UNIT])
        early_b = at("early_b", 184, [P, UNIT])
        early_c = at("early_c", 168, [P, UNIT])
        xT_hi = at("xT_hi", 128, [P, KD, SEQ], F32R)
        xT_lo = at("xT_lo", 136, [P, KD, SEQ], F32R)
        pT = at("pT", 144, [P, NH, 384])
        gT_hi = at("gT_hi", 128, [P, KD, SEQ], F32R)
        gT_lo = at("gT_lo", 136, [P, KD, SEQ], F32R)
        out_hi = [at("out0_hi", 144, [P, UNIT], F32R), at("out1_hi", 196, [P, UNIT], F32R)]
        out_lo = [at("out0_lo", 152, [P, UNIT], F32R), at("out1_lo", 176, [P, UNIT], F32R)]
        hid_hi = at("hid_hi", 144, [P, MF, SEQ], F32R)
        hid_lo = at("hid_lo", 146, [P, MF, SEQ], F32R)
        hid = at("hid", 148, [P, MF, SEQ])
        sil2 = at("sil2", 150, [P, MF, SEQ])
        end_hi = at("end_hi", 152, [P, MF, SEQ], F32R)
        end_lo = at("end_lo", 154, [P, MF, SEQ], F32R)
        cst = at("cst", 160, [P, C_N])
        bfc = at("bfc", 160 + 5.5, [P, 3, P], BF16)
        wr = at("wr", 160 + 6.25, [P, KD, 36])
        gain = at("gain", 160 + 7.5, [P, 112])
        X = at("X", 168, [P, T, D])
        xn = at("xn", 176, [P, T, D])
        qk = at("qk", 176, [P, 2, T, W])
        ga = at("ga", 176, [P, KD, SEQ])
        h2n = at("h2n", 176, [P, T, D])
        prob = at("prob", 176, [P, 2, 384])
        h2T = at("h2T", 184, [P, KD, SEQ])
        heT = at("heT", 192, [P, KD, P])
        pick = at("pick", 196, [P, T, P])
        pickw = at("pickw", 197, [P, T, P])
        turned = at("turned", 198, [P, 4, P])
        ysb = at("ysb", 200, [P, D])
        rt = at("rt", 204, [P, 1024])
        sil = at("sil", 208, [P, FE])
        act_e = at("act_e", 209, [P, FE])
        qkT = at("qkT", 184, [P, 2, PAIRS, SEQ])
        gb = at("gb", 184, [P, KD, SEQ])
        v = at("v", 192, [P, T, W])
        stick = at("stick", 196, [P, 2, 384])
        attw = at("attw", 200, [P, 2, 384])
        cu = at("cu", 196, [P, 4, SEQ])
        cy = at("cy", 200, [P, 4, SEQ])
        uu = at("uu", 196, [P, T, W])
        zz = at("zz", 200, [P, T, W])
        sq = at("sq", 204, [P, T, W])
        full = at("full", 208, [P, 4, 512])
        mgT_hi = at("mgT_hi", 192, [P, KD, SEQ], F32R)
        mgT_lo = at("mgT_lo", 204, [P, KD, SEQ], F32R)
        junk = at("junk", 200, [P, D])
        spT = at("spT", 216, [P, NH, P])
        spraw = at("spraw", 216, [P, NH, P])
        lngb = at("lngb", 212, [P, 2, W])
        atto = at("atto", 192, [P, T, W])
        ln1 = at("ln1", 184, [P, 2, D])
        ln2 = at("ln2", 212, [P, 2, D])
        st = at("st", 220, [P, 512])
        cnt = at("cnt", 222, [P, 8], I32)

        ident = cst[:, C_ID:C_ID + P]
        negu = cst[:, C_NEGU:C_NEGU + P]
        nego = cst[:, C_NEGO:C_NEGO + P]
        ltri = cst[:, C_LTRI:C_LTRI + P]
        ones = cst[:, C_ONE:C_ONE + P]
        triu = cst[:, C_TRIU:C_TRIU + P]
        cos = cst[:, C_COS:C_COS + T * HD].rearrange("p (t d) -> p t d", t=T)
        sin = cst[:, C_SIN:C_SIN + T * HD].rearrange("p (t d) -> p t d", t=T)
        iota = cst[:, C_IOTA:C_IOTA + CAP]
        thr = cst[:, C_THR:C_THR + 7]
        ident_b, mask1_b, mask2_b = bfc[:, 0, :], bfc[:, 1, :], bfc[:, 2, :]
        g1 = gain[:, 0:8]
        g2 = gain[:, 8:16]
        gq, gk = gain[:, 16:17], gain[:, 17:18]
        cw = gain[:, 18:30].rearrange("p (j m) -> p j m", j=3)
        rbias = gain[:, 30:66]
        gmix = gain[:, 66:74]
        bsp = gain[:, 74:82]
        ln1gT, ln1bT = gain[:, 82:90], gain[:, 90:98]
        pickT, actT = turned[:, 0:T, :], turned[:, T:T + KF, :]

        ss1, y1, n1 = st[:, 0:2], st[:, 2:4], st[:, 4:10]
        ssk, yk, nk = st[:, 16:32], st[:, 32:48], st[:, 48:96]
        ssq, yq = st[:, 96:112], st[:, 112:128]
        ss2, y2 = st[:, 128:130], st[:, 130:132]
        bst = st[:, 136:160].rearrange("p (t c s) -> p t c s", t=T, c=2)
        mv = st[:, 160:164].rearrange("p (t s) -> p t s", t=T)
        yl = st[:, 164:166]
        shift = st[:, 166:167]
        mx = st[:, 176:192].rearrange("p (h t) -> p h t", t=T)
        mxn = st[:, 192:208].rearrange("p (h t) -> p h t", t=T)
        rsum = st[:, 208:224].rearrange("p (h t) -> p h t", t=T)
        rinv = st[:, 224:240].rearrange("p (h t) -> p h t", t=T)
        zs, zy, zss = st[:, 240:256], st[:, 256:272], st[:, 400:416]
        ssg, yg = st[:, 272:276], st[:, 276:280]
        nw = st[:, 288:400].rearrange("p (i n) -> p i n", n=16)

        land = [sem(f"land{i}") for i in range(RING)]
        land_x = [sem(f"land_x{t}") for t in range(T)]
        land_id = sem("land_id")
        land_cst = sem("land_cst")
        land_qk = sem("land_qk")
        land_small = sem("land_small")
        land_early = [sem(f"land_early{i}") for i in range(EARLY)]
        land_taps = sem("land_taps")
        land_b2 = sem("land_b2")
        land_ln1 = sem("land_ln1")
        land_ln2 = sem("land_ln2")
        out_stored = sem("out_stored")
        hi_made = sem("hi_made")
        lo_made = sem("lo_made")
        unit_used = sem("unit_used")
        half_used = sem("half_used")
        pair_free = [sem("pair_free0"), sem("pair_free1")]
        dve_own = sem("dve_own")
        act_own = sem("act_own")
        root_made = sem("root_made")
        turned_ps = sem("turned_ps")
        full_made = sem("full_made")
        upper_made = sem("upper_made")
        split_made = sem("split_made")
        PS_H, PS_R, PS_X2, PS_G, PS_X3 = 0, 4, 8, 12, 16
        SP_H, SP_X2, SP_G, SP_X3 = 0, 4, 8, 12
        FULL_H, FULL_G, FULL_X3 = 0, 4, 8
        bf_made = sem("bf_made")
        xn_made = sem("xn_made")
        qk_sq = sem("qk_sq")
        qk_ss = sem("qk_ss")
        qk_made = sem("qk_made")
        qkT_ps = sem("qkT_ps")
        qkT_made = sem("qkT_made")
        v_made = sem("v_made")
        z_ps = sem("z_ps")
        log_made = sem("log_made")
        sp_made = sem("sp_made")
        la_ps = sem("la_ps")
        attw_made = sem("attw_made")
        av_ps = sem("av_ps")
        brhi_made = sem("brhi_made")
        br_made = sem("br_made")
        cc_made = sem("cc_made")
        conv_made = sem("conv_made")
        convhi_made = sem("convhi_made")
        conv_split = sem("conv_split")
        ga_sig = sem("ga_sig")
        gb_sig = sem("gb_sig")
        mg_made = sem("mg_made")
        mghi_made = sem("mghi_made")
        mgT_made = sem("mgT_made")
        x2_made = sem("x2_made")
        h2n_made = sem("h2n_made")
        h2T_made = sem("h2T_made")
        logit_ps = sem("logit_ps")
        gdiff_made = sem("gdiff_made")
        gexp_made = sem("gexp_made")
        assign_made = sem("assign_made")
        rank_ps = sem("rank_ps")
        place_made = sem("place_made")

        def moe_sems(tag):
            names = ("pick_made", "pickw_made", "gath_ps", "heT_made", "used", "sil_made", "act_made", "aT_ps",
                     "actT_made", "y_made", "spread")
            return {n: sem(f"{n}{tag}") for n in names}

        STARTED = ("y_made", "act_made", "actT_made", "gath_ps", "aT_ps", "spread")
        first = moe_sems("_a")
        more = moe_sems("_b")
        land_more = [sem(f"land_more{i}") for i in range(UPQ)]
        spT_ps = sem("spT_ps")
        spT_made = sem("spT_made")
        rope_made = sem("rope_made")
        rT_ps = sem("rT_ps")
        rT_made = sem("rT_made")
        v2_made = sem("v2_made")
        s_ps = sem("s_ps")
        mx_made = sem("mx_made")
        p_made = sem("p_made")
        pT_ps = sem("pT_ps")
        pT_made = sem("pT_made")
        o_ps = sem("o_ps")
        o_made = sem("o_made")
        zg_made = sem("zg_made")
        zmean_made = sem("zmean_made")
        zc_made = sem("zc_made")
        zq_made = sem("zq_made")
        zss_made = sem("zss_made")
        zy_ready = sem("zy_ready")
        zn_made = sem("zn_made")
        z_made = sem("z_made")
        u_made = sem("u_made")
        mix_ps = sem("mix_ps")
        sg_made = sem("sg_made")
        cat_made = sem("cat_made")
        sum_a = sem("sum_a")
        sum_d = sem("sum_d")
        xhat_made = sem("xhat_made")
        x3g_made = sem("x3g_made")
        ffn_lo_made = sem("ffn_lo_made")
        y_ps = sem("y_ps")
        var_made = sem("var_made")
        x3_made = sem("x3_made")
        sil2_made = sem("sil2_made")
        hid_made = sem("hid_made")
        hidhi_made = sem("hidhi_made")
        hidT_made = sem("hidT_made")
        y_out = [sem(f"y_out{t}") for t in range(T)]
        shift_made = sem("shift_made")
        normed = sem("normed")

        win = w_in[0].rearrange("(p k) n -> p k n", k=KD)
        win2 = w_in_2[0].rearrange("(p k) n -> p k n", k=KD)
        wsb = w_sb_branch[0].rearrange("(k p) n -> p k n", p=P)
        wcv = w_conv_branch[0].rearrange("(k p) n -> p k n", p=P)
        wo = w_out[0].rearrange("(k p) n -> p k n", p=P)
        wo2 = w_out_2[0].rearrange("(k p) n -> p k n", p=P)
        wg2 = w_gate_2[0].rearrange("(p k) n -> p k n", k=KD)
        wu2 = w_up_2[0].rearrange("(p k) n -> p k n", k=KD)
        wd2 = w_down_2[0].rearrange("(c m p) n -> p c m n", m=MF, p=P)
        wge = w_gate_e[0].rearrange("(q j) (p k) f -> q p j k f", j=QUAD, k=KD)
        wue = w_up_e[0].rearrange("(q j) (p k) f -> q p j k f", j=QUAD, k=KD)
        wde = w_down_e[0].rearrange("(q j) (p k) (h n) -> q h k p j n", j=QUAD, k=KF, h=2)

        CH_K, CH_Q, CH_V, CH_GA, CH_CC, CH_CU, CH_CB, CH_GB = 0, 1, 2, 3, 5, 6, 7, 8
        WIN_COL = [1, 0, 2, 6, 7, 4, 5, 3, 8, 9]
        units1 = []
        for c in WIN_COL:
            for h in range(2):
                units1.append(win[:, KU * h:KU * h + KU, 512 * c:512 * c + 512])
        for h in range(2):
            units1.append(wsb[:, :, 512 * h:512 * h + 512])
            units1.append(wcv[:, :, 512 * h:512 * h + 512])
        for kh in range(2):
            for h in range(2):
                units1.append(wo[:, KU * kh:KU * kh + KU, 512 * h:512 * h + 512])
        assert len(units1) == B1_UNITS
        WIN2_COL = [1, 0, 4, 3, 2]
        units2 = []
        for c in WIN2_COL:
            for h in range(2):
                units2.append(win2[:, KU * h:KU * h + KU, 512 * c:512 * c + 512])
        for kh in (1, 0):
            for h in range(2):
                units2.append(wo2[:, KU * kh:KU * kh + KU, 512 * h:512 * h + 512])
        assert len(units2) == B2_PRE

        def slot_of(n):
            return n % RING, 16 * (n // RING + 1)

        def load_of(i):
            return i if i < B1_UNITS else i + MOE_UNITS - SKIP

        QS = [(B1_UNITS + m) % RING for m in range(RING)]
        QV = [slot_of(B1_UNITS + m)[1] for m in range(RING)]

        def is_early(n):
            return GU <= n < GU + EARLY or AGAIN_AT <= n < AGAIN_AT + AGAIN

        def early_spot(n):
            return (n - GU, 16) if n < AGAIN_AT else (n - AGAIN_AT, 32)

        ring_units = [n for n in range(MOE_UNITS) if not is_early(n)]

        def quad_slot(u):
            return (u - SKIP) % RING

        EARLY_AT = [(early_a, 0), (4, B1_PROJ), (5, B1_PROJ), (6, B1_UNITS - 4), (7, B1_UNITS - 4), (0, B1_UNITS - 1),
                    (2, B1_UNITS - 1), (1, B1_UNITS), (3, B1_UNITS), (early_b, 0), (early_c, 0)]
        assert len(EARLY_AT) == EARLY

        def early_area(n):
            spot = EARLY_AT[early_spot(n)[0]][0]
            return early[:, spot, :] if isinstance(spot, int) else spot[:]

        LOOP_B = RING // 3
        LOOP_N = (NCH - 3) // LOOP_B
        assert 2 + LOOP_N * LOOP_B == NCH - 1

        def body_unit(c):
            return SFF + 2 + 3 * (c - 1)

        block = ctx.enter_context(nc.Block())

        @block.sync
        def _(sp):
            def small(dst, src, landed):
                sp.dma_start(dst, src).then_inc(landed, 16)

            for t in range(T):
                sp.dma_start(X[:, t, :], x[0, t * P:(t + 1) * P, :]).then_inc(land_x[t], 16)
            for i, src in enumerate(units1):
                slot, _ = slot_of(i)
                if i >= RING:
                    sp.wait_ge(lo_made, i - RING + 1)
                sp.dma_start(ring[:, slot, :].rearrange("p (k n) -> p k n", k=KU), src).then_inc(land[slot], 16)
                if i == 1:
                    small(cst[:, P:C_N], consts[:, P:C_N], land_cst)
                    for h in range(2):
                        small(gq[HD * h:HD * h + HD, :], q_norm_g[0].rearrange("(d o) -> d o", o=1), land_qk)
                        small(gk[HD * h:HD * h + HD, :], k_norm_g[0].rearrange("(d o) -> d o", o=1), land_qk)
                if i == RING - 1:
                    with nc.allow_non_contiguous_dma(reason="a few thousand gains and biases"):
                        small(cw, conv_w[0].rearrange("j (m p) -> p j m", p=P), land_taps)
                        small(bsp, b_spatial_2[0].rearrange("g i -> i g"), land_small)
                        small(gmix[:, 0:4], attn_out_g_2[0].rearrange("(k p) -> p k", p=P), land_small)
                        small(gmix[:, 4:8], gmlp_out_g_2[0].rearrange("(k p) -> p k", p=P), land_small)
                    small(g2, norm_ffn_g[0].rearrange("(p k) -> p k", k=KD), land_small)
                    small(ln1gT, ln1_g_2[0].rearrange("(p k) -> p k", k=KD), land_small)
                    small(ln1bT, ln1_b_2[0].rearrange("(p k) -> p k", k=KD), land_small)
                    small(wr[:, :, 0:NG], w_router_group[0].rearrange("(p k) n -> p k n", k=KD), land_small)
                    small(wr[:, :, NG:NG + NE], w_router_expert[0].rearrange("(p k) n -> p k n", k=KD), land_small)
                    small(rbias[:, 0:NG], b_router_group[0].partition_broadcast(P), land_small)
                    small(rbias[:, NG:NG + NE], b_router_expert[0].partition_broadcast(P), land_small)

            def quad_unit(q, u, dst, landed):
                if u < 8:
                    src = (wge if u < 4 else wue)[q, :, :, 2 * (u % 4):2 * (u % 4) + 2, :]
                    sp.dma_start(dst.rearrange("p (j k f) -> p j k f", j=QUAD, k=2), src).then_inc(landed, 16)
                else:
                    src = wde[q, (u - 8) // KF, (u - 8) % KF]
                    sp.dma_start(dst.rearrange("p (j n) -> p j n", j=QUAD), src).then_inc(landed, 16)

            def ring_unit(q, u, sems):
                m = quad_slot(u)
                quad_unit(q, u, ring[:, QS[m], :], sems[m])

            def early_unit(n):
                spot, used = EARLY_AT[n - GU]
                if spot is early_a:
                    sp.wait_ge(split_made, SP_H + 4)
                elif spot is early_b:
                    sp.wait_ge(logit_ps, 1)
                elif spot is early_c:
                    sp.wait_ge(rank_ps, 1)
                    sp.wait_ge(h2n_made, T)
                else:
                    sp.wait_ge(unit_used, used)
                quad_unit(n // UPQ, n % UPQ, early_area(n), land_early[n - GU])

            main_sems = [land[s] for s in QS]
            early_unit(GU)
            for m in range(RING):
                if m == GU - 4:
                    early_unit(GU + 1)
                    early_unit(GU + 2)
                if m == GU:
                    early_unit(GU + 3)
                    early_unit(GU + 4)
                sp.wait_ge(lo_made, B1_UNITS + m - RING + 1)
                n = m if m < GU else m + EARLY
                quad_unit(n // UPQ, n % UPQ, ring[:, QS[m], :], main_sems[m])
            for n in range(GU + 5, GU + EARLY):
                early_unit(n)
            for n in range(RING + EARLY, 4 * UPQ):
                if is_early(n):
                    k = early_spot(n)[0]
                    sp.wait_ge(first["used"], GU + k + 1)
                    quad_unit(n // UPQ, n % UPQ, early_area(n), land_early[k])
                else:
                    i = ring_units.index(n)
                    sp.wait_ge(first["used"], ring_units[i - RING] + 1)
                    quad_unit(n // UPQ, n % UPQ, ring[:, QS[i % RING], :], main_sems[i % RING])
            with sp.Fori(4, NQ) as q:
                for u in range(UPQ):
                    sp.wait_ge(first["used"], q * UPQ + (u + 1 - UPQ))
                    ring_unit(q, u, main_sems)

            sp.wait_ge(place_made, 3)
            extra = sp.value_load(cnt[0:1, 0:1], min_val=0, max_val=7)
            with sp.If(extra > 0):
                sp.wait_ge(first["used"], MOE_UNITS)
                with sp.Fori(0, extra) as r:
                    with sp.Fori(0, NQ) as q:
                        for u in range(UPQ):
                            sp.wait_ge(more["used"], (r * NQ + q) * UPQ + (u + 1))
                            ring_unit(q, u, land_more)
            sp.wait_ge(more["used"], extra * MOE_UNITS + UPQ)

            def b2_free(i):
                n = load_of(i)
                if n - RING < B1_UNITS + MOE_UNITS - SKIP:
                    sp.wait_ge(first["used"], n - RING - B1_UNITS + SKIP + 1)
                else:
                    sp.wait_ge(lo_made, i - RING + 1)

            for j, src in enumerate(units2):
                i = S1 + j
                slot, _ = slot_of(load_of(i))
                b2_free(i)
                sp.dma_start(ring[:, slot, :].rearrange("p (k n) -> p k n", k=KU), src).then_inc(land[slot], 16)
                if j == 1:
                    sp.wait_ge(first["used"], AGAIN_AT + AGAIN)
                    sp.dma_start(spraw[:], w_spatial_2[0].rearrange("g i j -> i g j")).then_inc(land_b2, 16)
                    for i, g in enumerate((gmlp_ln_g_2, gmlp_ln_b_2)):
                        sp.dma_start(lngb[:, i, :], g[0].rearrange("g d -> (g d)").partition_broadcast(P)
                                     ).then_inc(land_b2, 16)

            def ffn_gu(i, w, c, turn=None):
                slot, _ = slot_of(load_of(i))
                if turn is None:
                    b2_free(i)
                else:
                    sp.wait_ge(lo_made, turn * RING + (i - RING + 1))
                if turn is not None:
                    src = w[:, :, bass.ds(turn * (LOOP_B * FCHUNK) + c * FCHUNK, FCHUNK)]
                else:
                    src = w[:, :, c * FCHUNK:(c + 1) * FCHUNK]
                sp.dma_start(ring[:, slot, :].rearrange("p (k n) -> p k n", k=KD), src).then_inc(land[slot], 16)

            def ffn_d(i, c, turn=None):
                slot, _ = slot_of(load_of(i))
                if turn is None:
                    b2_free(i)
                else:
                    sp.wait_ge(lo_made, turn * RING + (i - RING + 1))
                src = wd2[:, c] if turn is None else wd2[:, bass.ds(turn * LOOP_B + c, 1)].rearrange(
                    "p o m n -> p (o m) n")
                sp.dma_start(ring[:, slot, :].rearrange("p (m n) -> p m n", m=MF), src).then_inc(land[slot], 16)

            def ffn_body(c, turn=None):
                i = body_unit(c)
                ffn_gu(i, wg2, c, turn)
                ffn_gu(i + 1, wu2, c, turn)
                ffn_d(i + 2, c - 1, turn)

            ffn_gu(SFF, wg2, 0)
            ffn_gu(SFF + 1, wu2, 0)
            ffn_body(1)
            sp.wait_ge(s_ps, NH)
            for i, g in enumerate((ln1_g_2, ln1_b_2)):
                sp.dma_start(ln1[:, i, :], g[0].partition_broadcast(P)).then_inc(land_ln1, 16)
            with sp.Fori(0, LOOP_N) as turn:
                for c in range(2, 2 + LOOP_B):
                    ffn_body(c, turn)
            sp.wait_ge(split_made, SP_X3 + 4)
            for i, g in enumerate((ln2_g_2, ln2_b_2)):
                sp.dma_start(ln2[:, i, :], g[0].partition_broadcast(P)).then_inc(land_ln2, 16)
            ffn_body(NCH - 1)
            ffn_d(body_unit(NCH), NCH - 1)
            for t in range(T):
                for c in range(2):
                    sp.wait_ge(y_out[t], c + 1)
                    sp.dma_start(out[0, t * P:(t + 1) * P, c * 512:(c + 1) * 512], X[:, t, c * 512:(c + 1) * 512]
                                 ).then_inc(out_stored, 16)
            sp.wait_ge(out_stored, 16 * 2 * T)

        @block.tensor
        def _(pe):
            mm = nc.tensor.matmul

            def mm3(o, a_hi, a_lo, b_hi, b_lo, start, stop):
                mm(o, a_hi, b_hi, start=start, stop=False, skip_group_check=True)
                mm(o, a_hi, b_lo, start=False, stop=False, skip_group_check=True)
                return mm(o, a_lo, b_hi, start=False, stop=stop, skip_group_check=True)

            def token_unit(i, c, k0, aT_hi, aT_lo, first, last, ready=None, between=None, half=False):
                bank = 2 * (c % 2)
                if c >= 2 and first:
                    pe.wait_ge(pair_free[c % 2], c // 2)
                pe.wait_ge(lo_made, i + 1)
                b = i % 2
                hi = w_hi[:, b, :].rearrange("p (k n) -> p k n", k=KU)
                lo = w_lo[:, b, :].rearrange("p (k n) -> p k n", k=KU)
                for t in range(T):
                    if ready:
                        pe.wait_ge(ready[0], ready[1 + t])
                    for kk in range(KU):
                        k = k0 + kk
                        tok = slice(t * P, (t + 1) * P)
                        ins = mm3(ps[:, bank + t, :], aT_hi[:, k, tok], aT_lo[:, k, tok], hi[:, kk, :],
                                  lo[:, kk, :], start=(first and kk == 0), stop=(last and kk == KU - 1))
                    if t == 0 and half:
                        ins.then_inc(half_used, 1)
                    if t == 0 and between:
                        between()
                ins.then_inc(unit_used, 1)

            def feature_unit(i, c, k0, aT_hi, aT_lo, n_k=KD):
                bank = 2 * (c % 2)
                if c >= 2 and k0 == 0:
                    pe.wait_ge(pair_free[c % 2], c // 2)
                pe.wait_ge(lo_made, i + 1)
                b = i % 2
                hi = w_hi[:, b, :].rearrange("p (k n) -> p k n", k=KU)
                lo = w_lo[:, b, :].rearrange("p (k n) -> p k n", k=KU)
                for m in range(4):
                    o = ps[:, bank + m // 2, (m % 2) * SEQ:(m % 2 + 1) * SEQ]
                    for kk in range(KU):
                        k = k0 + kk
                        col = slice(m * P, (m + 1) * P)
                        last = mm3(o, hi[:, kk, col], lo[:, kk, col], aT_hi[:, k, :], aT_lo[:, k, :],
                                   start=(k == 0 and m % 2 == 0), stop=(k == n_k - 1))
                last.then_inc(unit_used, 1)

            def transposes(src, bank, ready, tiles=range(T)):
                for t in tiles:
                    for made, value in ready:
                        pe.wait_ge(made, value + t)
                    for k in range(KD):
                        tile = src[:, t, k:D:KD]
                        ins = nc.tensor.transpose(ps[:, bank + 2 * t + k // 4, (k % 4) * P:(k % 4 + 1) * P],
                                                  tile, ident)
                        if k % 4 == 3:
                            ins.then_inc(turned_ps, 1)

            pe.wait_ge(land_id, 16 * 2)
            transposes(xn, 0, [(xn_made, 1)])

            def proj(i, feature):
                if feature:
                    feature_unit(i, i // 2, KU * (i % 2), hT_hi, hT_lo)
                else:
                    token_unit(i, i // 2, KU * (i % 2), hT_hi, hT_lo, i % 2 == 0, i % 2 == 1, (split_made, SP_H + 2, SP_H + 4))

            def head_transposes(which):
                pe.wait_ge(qk_made, which + 1)
                for t in range(T):
                    for p in range(PAIRS):
                        ins = nc.tensor.transpose(ps[:, 4 + 2 * which + t, p * P:(p + 1) * P],
                                                  qk[:, which, t, p * P:(p + 1) * P], ident)
                ins.then_inc(qkT_ps, 1)

            def zbank(p):
                return 4 + 2 * (p % 2)

            def z_step(p):
                if p == 0:
                    pe.wait_ge(qkT_made, 2)
                    pe.wait_ge(bf_made, 1)
                if p >= 2:
                    pe.wait_ge(br_made, p - 1)
                for h in range(2):
                    row = slice(HD * h, HD * h + HD)
                    o = ps[:, zbank(p) + h, :]
                    mm(o[:, 0:SEQ], qkT[row, 0, p, 0:P], qkT[row, 1, p, :], start=True, stop=False,
                       skip_group_check=True)
                    mm(o[:, SEQ:SEQ + P], qkT[row, 0, p, P:SEQ], qkT[row, 1, p, P:SEQ], start=False, stop=False,
                       skip_group_check=True)
                for h in range(2):
                    o = ps[:, zbank(p) + h, :]
                    mm(o[:, 0:P], ident_b, mask1_b, start=False, stop=False, skip_group_check=True)
                    last = mm(o[:, SEQ:SEQ + P], ident_b, mask1_b, start=False, stop=True, skip_group_check=True)
                last.then_inc(z_ps, 1)

            def la_step(p):
                pe.wait_ge(sp_made, p + 1)
                for h in range(2):
                    o = ps[:, zbank(p) + h, :]
                    mm(o[:, 0:SEQ], negu, stick[:, h, 0:SEQ], start=False, stop=False, skip_group_check=True)
                    mm(o[:, P:SEQ], nego, stick[:, h, SEQ:SEQ + P], start=False, stop=False, skip_group_check=True)
                    last = mm(o[:, SEQ:SEQ + P], negu, stick[:, h, SEQ:SEQ + P], start=False, stop=True,
                              skip_group_check=True)
                last.then_inc(la_ps, 1)

            def av_step(p):
                pe.wait_ge(attw_made, p + 1)
                if p == 0:
                    pe.wait_ge(v_made, 1)
                for h in range(2):
                    head = slice((2 * p + h) * HD, (2 * p + h + 1) * HD)
                    o = ps[HD * h:HD * h + HD, zbank(p), 0:SEQ]
                    mm(o, v[:, 0, head], attw[:, h, 0:SEQ], start=True, stop=False, skip_group_check=True)
                    last = mm(o[:, P:SEQ], v[:, 1, head], attw[:, h, SEQ:SEQ + P], start=False, stop=True,
                              skip_group_check=True)
                last.then_inc(av_ps, 1)

            for i in range(4):
                proj(i, False)
            head_transposes(0)
            proj(4, False)
            proj(5, False)
            head_transposes(1)
            proj(6, True)
            z_step(0)
            proj(7, True)
            z_step(1)
            la_step(0)
            proj(8, True)
            av_step(0)
            la_step(1)
            proj(9, True)
            av_step(1)
            z_step(2)
            proj(10, True)
            z_step(3)
            la_step(2)
            proj(11, True)
            av_step(2)
            la_step(3)
            proj(12, True)
            av_step(3)
            for i in range(13, 20):
                proj(i, True)
            pe.wait_ge(br_made, PAIRS)
            pe.wait_ge(conv_split, 1)
            for h in range(2):
                for branch in range(2):
                    feature_unit(20 + 2 * h + branch, 10 + 2 * h + branch, 0, brT_hi[:, branch], brT_lo[:, branch],
                                 n_k=KU)
            for kh in range(2):
                pe.wait_ge(mgT_made, kh + 1)
                for h in range(2):
                    token_unit(24 + 2 * kh + h, 14 + h, KU * kh, mgT_hi, mgT_lo, kh == 0, kh == 1,
                               half=(kh == 1 and h == 1))

            transposes(X, 4, [(x2_made, 3)])
            pe.wait_ge(land_small, 16 * 10)
            for t in range(T):
                pe.wait_ge(h2T_made, 2 * t + 2)
                for k in range(KD):
                    last = mm(ps[:, 0, t * 36:t * 36 + 36], h2T[:, k, t * P:(t + 1) * P], wr[:, k, :],
                              start=(k == 0), stop=(k == KD - 1))
            last.then_inc(logit_ps, 1)
            for t, h in ((0, 1), (1, 0), (1, 1), (0, 0)):
                if (t, h) == (0, 0):
                    pe.wait_ge(gdiff_made, 1)
                mm(ps[:, 2 * t + h, :], ident, X[:, t, h * 512:(h + 1) * 512], start=True, stop=False,
                   skip_group_check=True)
            pe.wait_ge(assign_made, 1)
            asg = rt[:, 0:64].rearrange("p (t e) -> p t e", t=T)
            mm(ps[:, 7, 0:NE], ltri, asg[:, 0, :], start=True, stop=True)
            mm(ps[:, 7, NE:2 * NE], ones, asg[:, 0, :], start=True, stop=False)
            mm(ps[:, 7, NE:2 * NE], ltri, asg[:, 1, :], start=False, stop=True)
            mm(ps[:, 7, 2 * NE:3 * NE], ones, asg[:, 0, :], start=True, stop=False)
            mm(ps[:, 7, 2 * NE:3 * NE], ones, asg[:, 1, :], start=False, stop=True).then_inc(rank_ps, 1)

            def quad(it, s, weights, landed):
                pe.wait_ge(s["pick_made"], it + 1)
                pe.wait_ge(s["y_made"], it * 2 + 1)

                def gather(features):
                    for k in features:
                        for t in range(T):
                            last = mm(ps[:, 6 + k // 4, (k % 4) * P:(k % 4 + 1) * P], h2n[:, t, k:D:KD],
                                      pick[:, t, :], start=(t == 0), stop=(t == T - 1))
                        if k % 4 == 3:
                            last.then_inc(s["gath_ps"], 1)

                gather(range(0, 6))
                pe.wait_ge(s["actT_made"], it + 1)
                for u in range(8):
                    if u == 4:
                        pe.wait_ge(s["act_made"], it + 1)
                    if u in (0, 2):
                        pe.wait_ge(s["heT_made"], it * 2 + (1 + u // 2))
                    landed(u)
                    wv = weights(u).rearrange("p (j k f) -> p j k f", j=QUAD, k=2)
                    for kk in range(2):
                        k = 2 * (u % 4) + kk
                        for j in range(QUAD):
                            last = mm(ps[32 * j:32 * j + 32, 4 + u // 4, 0:FE], heT[:, k, 32 * j:32 * j + 32],
                                      wv[:, j, kk, :], start=(k == 0), stop=(k == KD - 1))
                    last.then_inc(s["used"], 1)
                    if u == 0:
                        gather(range(6, KD))
                pe.wait_ge(s["sil_made"], it + 1)
                pe.wait_ge(s["pickw_made"], it + 1)
                for t in range(T):
                    nc.tensor.transpose(ps[:, 4, t * P:(t + 1) * P], pickw[:, t, :], ident)
                pe.wait_ge(s["act_made"], it + 2)
                for k in range(KF):
                    last = nc.tensor.transpose(ps[:, 4, (T + k) * P:(T + k + 1) * P], act_e[:, k:FE:KF], ident)
                last.then_inc(s["aT_ps"], 1)
                pe.wait_ge(s["actT_made"], it + 2)
                for u in range(8, UPQ):
                    h, k = (u - 8) // KF, (u - 8) % KF
                    landed(u)
                    wv = weights(u).rearrange("p (j n) -> p j n", j=QUAD)
                    for j in range(QUAD):
                        last = mm(ps[32 * j:32 * j + 32, 6 + h, :], actT[:, k, 32 * j:32 * j + 32], wv[:, j, :],
                                  start=(k == 0), stop=(k == KF - 1))
                    last.then_inc(s["used"], 1)
                for h in range(2):
                    pe.wait_ge(s["y_made"], it * 2 + (2 + h))
                    for t in range(T):
                        last = mm(ps[:, 2 * t + h, :], pickT[:, t, :], ysb[:, h * 512:(h + 1) * 512], start=False,
                                  stop=False, skip_group_check=True)
                    last.then_inc(s["spread"], 1)

            def in_ring(u):
                return ring[:, QS[quad_slot(u)], :]

            def weights_of(q):
                def weights(u):
                    n = q * UPQ + u
                    return early_area(n) if is_early(n) else ring[:, QS[ring_units.index(n) % RING], :]
                return weights

            def landed_of(q):
                def wait(u):
                    n = q * UPQ + u
                    if is_early(n):
                        k, value = early_spot(n)
                        pe.wait_ge(land_early[k], value)
                    else:
                        turn, m = divmod(ring_units.index(n), RING)
                        pe.wait_ge(land[QS[m]], QV[m] + 16 * turn)
                return wait

            def landed_ring(q):
                def wait(u):
                    m = quad_slot(u)
                    pe.wait_ge(land[QS[m]], q * 16 + (QV[m] + 16 * ((u - SKIP) // RING)))
                return wait

            def landed_more(it):
                return lambda u: pe.wait_ge(land_more[quad_slot(u)], it * 16 + 16)

            for s in (first, more):
                for name in STARTED:
                    pe.sem_inc(s[name], 1)
            pe.sem_inc(more["used"], UPQ)
            for q in range(3):
                quad(q, first, weights_of(q), landed_of(q))
            with pe.Fori(3, NQ) as q:
                quad(q, first, in_ring, landed_ring(q))
            pe.wait_ge(place_made, 3)
            extra = pe.value_load(cnt[0:1, 0:1], min_val=0, max_val=7)
            with pe.If(extra > 0):
                with pe.Fori(0, extra) as r:
                    with pe.Fori(0, NQ) as q:
                        quad(r * NQ + q, more, in_ring, landed_more(r * NQ + q))

            transposes(X, 4, [(sum_a, 1), (sum_d, 1)])

            def proj2(j, between=None, half=False):
                token_unit(S1 + j, 16 + j // 2, KU * (j % 2), xT_hi, xT_lo, j % 2 == 0, j % 2 == 1,
                           (split_made, SP_X2 + 2, SP_X2 + 4), between, half)

            def spatial_transposes():
                pe.wait_ge(land_b2, 16 * 3)
                pe.wait_ge(split_made, SP_X2 + 4)
                for g in range(NH):
                    ins = nc.tensor.transpose(ps[:, 4 + g // 4, (g % 4) * P:(g % 4 + 1) * P], spraw[:, g, :], ident)
                ins.then_inc(spT_ps, 1)

            def rope_transposes(which):
                if which == 0:
                    pe.wait_ge(spT_made, 1)
                pe.wait_ge(rope_made, which + 1)
                for t in range(T):
                    for p in range(PAIRS):
                        ins = nc.tensor.transpose(ps[:, 4 + 2 * which + t, p * P:(p + 1) * P],
                                                  qk[:, which, t, p * P:(p + 1) * P], ident)
                ins.then_inc(rT_ps, 1)

            def score_step(h):
                if h == 0:
                    pe.wait_ge(rT_made, 2)
                if h >= 2:
                    pe.wait_ge(pT_made, h - 1)
                row = slice(HD * (h % 2), HD * (h % 2) + HD)
                o = ps[:, 4 + h % 2, :]
                mm(o[:, 0:P], qkT[row, 1, h // 2, 0:P], qkT[row, 0, h // 2, 0:P], start=True, stop=False,
                   skip_group_check=True)
                mm(o[:, P:P + SEQ], qkT[row, 1, h // 2, P:SEQ], qkT[row, 0, h // 2, :], start=False, stop=False,
                   skip_group_check=True)
                mm(o[:, 0:P], ident_b, mask2_b, start=False, stop=False, skip_group_check=True)
                mm(o[:, SEQ:SEQ + P], ident_b, mask2_b, start=False, stop=True, skip_group_check=True
                   ).then_inc(s_ps, 1)

            def prob_transposes(h):
                pe.wait_ge(p_made, T * (h + 1))
                for j in range(3):
                    ins = nc.tensor.transpose(ps[:, 4 + h % 2, j * P:(j + 1) * P], prob[:, h % 2, j * P:(j + 1) * P],
                                              ident)
                ins.then_inc(pT_ps, 1)

            def out_step(h):
                pe.wait_ge(pT_made, h + 1)
                head = slice(h * HD, (h + 1) * HD)
                w = pT[:, h, :]
                mm(ps[:, 6, head], w[:, 0:P], v[:, 0, head], start=True, stop=True)
                mm(ps[:, 7, head], w[:, P:SEQ], v[:, 0, head], start=True, stop=False)
                return mm(ps[:, 7, head], w[:, SEQ:SEQ + P], v[:, 1, head], start=False, stop=True)

            def heads(scores, turns):
                def work():
                    for h in scores:
                        score_step(h)
                    for h in turns:
                        prob_transposes(h)
                return work

            def mix_step():
                heads((7,), (6,))()
                pe.wait_ge(pair_free[1], 10)
                pe.wait_ge(z_made, 1)
                for g in range(NH):
                    last = mm(ps[:, 2 + g // 4, (g % 4) * P:(g % 4 + 1) * P].rearrange("p (t d) -> p t d", t=T),
                              spT[:, g, :], zz[:, :, g * HD:(g + 1) * HD], start=True, stop=True)
                last.then_inc(mix_ps, 1)

            proj2(0)
            proj2(1, spatial_transposes)
            proj2(2)
            proj2(3, lambda: rope_transposes(0))
            proj2(4)
            proj2(5, lambda: rope_transposes(1))
            heads((0,), ())()
            proj2(6, heads((1,), (0,)))
            heads((2,), (1,))()
            proj2(7, heads((3,), (2,)))
            heads((4,), (3,))()
            proj2(8, heads((5,), (4,)))
            heads((6,), (5,))()
            proj2(9, mix_step, half=True)
            heads((), (7,))()

            def branch_transposes(b):
                pe.wait_ge(cat_made, b + 1)
                src = (zz, atto)[b // 2]
                for k in range(4):
                    ins = nc.tensor.transpose(ps[:, 4 + b, k * P:(k + 1) * P], src[:, b % 2, k * P:(k + 1) * P], ident)
                ins.then_inc(turned_ps, 1)

            def attention_transposes():
                branch_transposes(2)
                branch_transposes(3)

            pe.wait_ge(v2_made, T)
            for h in range(4):
                out_step(h)
            branch_transposes(0)
            branch_transposes(1)
            for h in range(4, NH):
                last = out_step(h)
            last.then_inc(o_ps, 1)
            token_unit(S1 + 10, 22, 4, gT_hi, gT_lo, True, False, (split_made, SP_G + 1, SP_G + 2))
            token_unit(S1 + 11, 23, 4, gT_hi, gT_lo, True, False, None, attention_transposes)
            for t in range(T):
                tok = slice(t * P, (t + 1) * P)
                pe.wait_ge(split_made, SP_G + 3 + t)
                for j in range(2):
                    pe.wait_ge(lo_made, S1 + 13 + j)
                    hi = out_hi[j].rearrange("p (k n) -> p k n", k=KU)
                    lo = out_lo[j].rearrange("p (k n) -> p k n", k=KU)
                    for k in range(KU):
                        last = mm3(ps[:, 2 * j + t, :], gT_hi[:, k, tok], gT_lo[:, k, tok], hi[:, k, :], lo[:, k, :],
                                   start=False, stop=(k == KU - 1))
                        if (t, j, k) == (1, 1, 1):
                            transposes(X, 4, [(xhat_made, 1)], (0,))
                    last.then_inc(half_used if t == 0 else unit_used, 1)
            transposes(X, 4, [(xhat_made, 1)], (1,))

            def ffn_up(i, c, kind, turn=None):
                off = 0 if turn is None else turn * RING
                done = c - 1 if turn is None else turn * LOOP_B + (c - 1)
                if c >= 2:
                    pe.wait_ge((sil2_made, hid_made)[kind], done)
                pe.wait_ge(lo_made, off + (i + 1))
                hi = w_hi[:, i % 2, :].rearrange("p (k n) -> p k n", k=KD)
                lo = w_lo[:, i % 2, :].rearrange("p (k n) -> p k n", k=KD)
                for m in range(MF):
                    o = ps[:, 4 + 2 * (c % 2) + kind, m * SEQ:(m + 1) * SEQ]
                    for k in range(KD):
                        if i == SFF and m == 0 and k % 4 == 0:
                            pe.wait_ge(split_made, SP_X3 + (3 + k // 4))
                        col = slice(m * P, (m + 1) * P)
                        last = mm3(o, hi[:, k, col], lo[:, k, col], xT_hi[:, k, :], xT_lo[:, k, :],
                                   start=(k == 0 and m == 0), stop=(k == KD - 1))
                last.then_inc(unit_used, 1)

            def ffn_down(i, c, turn=None):
                off = 0 if turn is None else turn * RING
                done = c + 1 if turn is None else turn * LOOP_B + (c + 1)
                pe.wait_ge(hidT_made, done)
                pe.wait_ge(lo_made, off + (i + 1))
                hi = w_hi[:, i % 2, :].rearrange("p (m n) -> p m n", m=MF)
                lo = w_lo[:, i % 2, :].rearrange("p (m n) -> p m n", m=MF)
                h_hi, h_lo = (end_hi, end_lo) if c == NCH - 1 and turn is None else (hid_hi, hid_lo)
                for t in range(T):
                    tok = slice(t * P, (t + 1) * P)
                    for h in range(2):
                        for m in range(MF):
                            last = mm3(ps[:, 2 * t + h, :], h_hi[:, m, tok], h_lo[:, m, tok],
                                       hi[:, m, h * 512:(h + 1) * 512], lo[:, m, h * 512:(h + 1) * 512],
                                       start=(c == 0 and m == 0), stop=False)
                        if c == NCH - 1:
                            last.then_inc(y_ps, 1)
                if c < NCH - 1:
                    last.then_inc(unit_used, 1)

            def ffn_body(c, turn=None):
                i = body_unit(c)
                ffn_up(i, c, 0, turn)
                ffn_up(i + 1, c, 1, turn)
                ffn_down(i + 2, c - 1, turn)

            ffn_up(SFF, 0, 0)
            ffn_up(SFF + 1, 0, 1)
            ffn_body(1)
            with pe.Fori(0, LOOP_N) as turn:
                for c in range(2, 2 + LOOP_B):
                    ffn_body(c, turn)
            ffn_body(NCH - 1)
            ffn_down(body_unit(NCH), NCH - 1)

        @block.scalar
        def _(act):
            LOG_EXP = "natural_log_exp_and_others"
            own = [0]

            def step(ins):
                own[0] += 1
                ins.then_inc(act_own, 1)
                act.wait_ge(act_own, own[0])

            def copy(o, i):
                return nc.scalar.activation(o, i, ACT.Copy)

            act.dma_start(cst[:, 0:P], consts[:, 0:P]).then_inc(land_id, 16)
            act.dma_start(g1, norm_mix_g[0].rearrange("(p k) -> p k", k=KD)).then_inc(land_id, 16)
            nc.scalar.preload_act_table_set(LOG_EXP)

            def rsqrt(y, ss, n, eps):
                step(nc.scalar.activation(y, ss, ACT.Ln, scale=1.0 / n, bias=eps))
                nc.scalar.activation(y, y, ACT.Exp, scale=-0.5).then_inc(root_made, 1)

            def hi(i, dst=None, before=None):
                slot, value = slot_of(load_of(i))
                act.wait_ge(land[slot], value)
                if dst is None and i >= 2:
                    act.wait_ge(unit_used, i - 1 if before is None else before + 1)
                copy(w_hi[:, i % 2, :] if dst is None else dst, ring[:, slot, :]).then_inc(hi_made, 1)

            for t in range(T):
                act.wait_ge(land_x[t], 16)
                step(nc.scalar.activation(junk[:], X[:, t, :], ACT.Square, accum_out=ss1[:, t:t + 1]))
                rsqrt(y1[:, t:t + 1], ss1[:, t:t + 1], D, RMS_EPS)

            def hT_copy(b):
                t, k0 = b // 2, 4 * (b % 2)
                act.wait_ge(full_made, FULL_H + b + 1)
                copy(hT_hi[:, k0:k0 + 4, t * P:(t + 1) * P],
                     full[:, b, :].rearrange("p (k n) -> p k n", k=4)).then_inc(upper_made, 1)

            hi(0)
            hT_copy(0)
            hT_copy(1)
            hi(1)
            hT_copy(2)
            hT_copy(3)
            act.wait_ge(land_cst, 16)
            for j, c in enumerate((C_ID, C_MK1, C_MK2)):
                last = copy(bfc[:, j, :], cst[:, c:c + P])
            last.then_inc(bf_made, 1)
            hi(2)

            def qk_square(which):
                act.wait_ge(unit_used, 2 * which + 2)
                if which == 1:
                    act.wait_ge(qk_ss, 1)
                nc.scalar.activation(sq[:].rearrange("p t w -> p (t w)"),
                                     ps[:, 2 * which:2 * which + 2, :].rearrange("p t w -> p (t w)"),
                                     ACT.Square).then_inc(qk_sq, 1)
                act.wait_ge(qk_ss, which + 1)
                rsqrt((yk, yq)[which], (ssk, ssq)[which], HD, RMS_EPS)

            def qkT_copy(which):
                act.wait_ge(qkT_ps, which + 1)
                for t in range(T):
                    last = nc.scalar.activation(
                        qkT[:, which, :, t * P:(t + 1) * P],
                        ps[:, 4 + 2 * which + t, :].rearrange("p (a n) -> p a n", a=PAIRS), ACT.Identity,
                        scale=(gk, gq)[which])
                last.then_inc(qkT_made, 1)

            def chunk_done(c):
                act.wait_ge(unit_used, 2 * c + 2)

            def two_banks(c):
                return ps[:, 2 * (c % 2):2 * (c % 2) + 2, :].rearrange("p b n -> p (b n)")

            def log1p_step(p):
                act.wait_ge(z_ps, p + 1)
                if p >= 1:
                    act.wait_ge(la_ps, p)
                b = 4 + 2 * (p % 2)
                step(nc.scalar.activation(stick[:], ps[:, b:b + 2, 0:384], ACT.Abs))
                step(nc.scalar.activation(stick[:], stick[:], ACT.Exp, scale=-1.0))
                nc.scalar.activation(stick[:], stick[:], ACT.Ln, bias=1.0).then_inc(log_made, 1)

            def attw_step(p):
                act.wait_ge(la_ps, p + 1)
                if p >= 1:
                    act.wait_ge(av_ps, p)
                b = 4 + 2 * (p % 2)
                nc.scalar.activation(attw[:], ps[:, b:b + 2, 0:384], ACT.Exp).then_inc(attw_made, 1)

            def brhi_step(p):
                act.wait_ge(av_ps, p + 1)
                copy(brT_hi[:, 0, p, :], ps[:, 4 + 2 * (p % 2), 0:SEQ]).then_inc(brhi_made, 1)

            hi(3)
            qk_square(0)
            hi(4)
            hi(5)
            qk_square(1)
            qkT_copy(0)
            hi(6)
            qkT_copy(1)
            hi(7)
            chunk_done(CH_V)
            copy(v[:].rearrange("p t w -> p (t w)"), two_banks(CH_V)).then_inc(pair_free[0], 1)
            act.wait_ge(pair_free[0], 2)
            nc.scalar.nop().then_inc(v_made, 1)
            hi(8)
            log1p_step(0)
            hi(9)
            chunk_done(CH_GA)
            copy(ga[:, 0:4, :].rearrange("p m n -> p (m n)"), two_banks(CH_GA)).then_inc(pair_free[1], 1)
            attw_step(0)
            log1p_step(1)
            hi(10)
            brhi_step(0)
            attw_step(1)
            hi(11)
            chunk_done(CH_GA + 1)
            copy(ga[:, 4:8, :].rearrange("p m n -> p (m n)"), two_banks(CH_GA + 1)).then_inc(pair_free[0], 1)
            brhi_step(1)
            log1p_step(2)
            hi(12)
            attw_step(2)
            log1p_step(3)
            hi(13)
            brhi_step(2)
            attw_step(3)
            hi(14)
            brhi_step(3)
            chunk_done(CH_CC)
            act.wait_ge(av_ps, PAIRS)
            copy(cu[:].rearrange("p m n -> p (m n)"), two_banks(CH_CC)).then_inc(cc_made, 1)
            act.wait_ge(cc_made, 1)
            nc.scalar.nop().then_inc(pair_free[1], 1)
            act.wait_ge(pair_free[0], 3)
            nc.scalar.activation(ga[:], ga[:], ACT.Sigmoid).then_inc(ga_sig, 1)
            hi(15)
            hi(16)
            hi(17)
            act.wait_ge(conv_made, 1)
            copy(brT_hi[:, 1], cy[:]).then_inc(convhi_made, 1)
            hi(18)
            hi(19)
            for h in range(2):
                chunk_done(CH_GB + h)
                nc.scalar.activation(gb[:, 4 * h:4 * h + 4, :].rearrange("p m n -> p (m n)"), two_banks(CH_GB + h),
                                     ACT.Sigmoid).then_inc(pair_free[h], 1)
                hi(20 + h)
            act.wait_ge(pair_free[1], 5)
            act.wait_ge(pair_free[0], 5)
            nc.scalar.nop().then_inc(gb_sig, 1)
            nc.scalar.preload_act_table_set(LOG_EXP)
            for i in range(22, 25):
                hi(i)
            for h in range(2):
                act.wait_ge(mg_made, h + 1)
                copy(mgT_hi[:, 4 * h:4 * h + 4, :], ga[:, 4 * h:4 * h + 4, :]).then_inc(mghi_made, 1)
                hi(25 + h)
            hi(27)

            for t in range(T):
                act.wait_ge(x2_made, T + 1 + t)
                step(nc.scalar.activation(junk[:], X[:, t, :], ACT.Square, accum_out=ss2[:, t:t + 1]))
            rsqrt(y2, ss2, D, RMS_EPS)
            for j in range(2):
                act.wait_ge(gdiff_made, j + 1)
                buf = rt[:, 64:72] if j == 0 else rt[:, 72:74]
                nc.scalar.activation(buf, buf, ACT.Exp).then_inc(gexp_made, 1)
            nc.scalar.preload_act_table_set("silu_and_others")

            def quad(it, s):
                act.wait_ge(s["used"], it * UPQ + (4 + s["start"]))
                act.wait_ge(s["act_made"], it + 1)
                nc.scalar.activation(sil[:], ps[:, 4, 0:FE], ACT.Silu).then_inc(s["sil_made"], 1)
                act.wait_ge(s["aT_ps"], it + 2)
                copy(turned[:].rearrange("p k n -> p (k n)"), ps[:, 4, :]).then_inc(s["actT_made"], 1)
                act.wait_ge(s["spread"], it * 2 + 1)
                for h in range(2):
                    act.wait_ge(s["used"], it * UPQ + (8 + KF * (h + 1) + s["start"]))
                    copy(ysb[:, h * 512:(h + 1) * 512], ps[:, 6 + h, :]).then_inc(s["y_made"], 1)

            quad(0, first | {"start": 0})
            with act.Fori(1, NQ) as q:
                quad(q, first | {"start": 0})
            act.wait_ge(place_made, 3)
            extra = act.value_load(cnt[0:1, 0:1], min_val=0, max_val=7)
            with act.If(extra > 0):
                act.wait_ge(first["spread"], 2 * NQ + 1)
                with act.Fori(0, extra) as r:
                    with act.Fori(0, NQ) as q:
                        quad(r * NQ + q, more | {"start": UPQ})
            act.wait_ge(more["spread"], extra * (2 * NQ) + 1)
            hi(S1)

            act.wait_ge(first["spread"], 2 * NQ)
            for t in range(T):
                copy(X[:, t, 0:512], ps[:, 2 * t, :]).then_inc(sum_a, 1)

            def xT_copy(b):
                t, k0 = b // 2, 4 * (b % 2)
                act.wait_ge(turned_ps, PS_X2 + b + 1)
                copy(xT_hi[:, k0:k0 + 4, t * P:(t + 1) * P],
                     ps[:, 4 + b, :].rearrange("p (k n) -> p k n", k=4)).then_inc(upper_made, 1)

            for b in range(4):
                xT_copy(b)
            nc.scalar.preload_act_table_set("gelu_and_others")

            def rT_copy(which):
                act.wait_ge(rT_ps, which + 1)
                for t in range(T):
                    last = copy(qkT[:, which, :, t * P:(t + 1) * P],
                                ps[:, 4 + 2 * which + t, :].rearrange("p (a n) -> p a n", a=PAIRS))
                last.then_inc(rT_made, 1)

            def exp_step(h):
                act.wait_ge(mx_made, h + 1)
                if h >= 2:
                    act.wait_ge(pT_ps, h - 1)
                for t in range(T):
                    a, b = (0, P) if t == 0 else (P, P + SEQ)
                    nc.scalar.activation(prob[:, h % 2, a:b], ps[:, 4 + h % 2, a:b], ACT.Exp, bias=mxn[:, h, t:t + 1],
                                         scale=HD ** -0.5, accum_out=rsum[:, h, t:t + 1]).then_inc(p_made, 1)

            def pT_copy(h):
                act.wait_ge(pT_ps, h + 1)
                copy(pT[:, h, :], ps[:, 4 + h % 2, 0:384]).then_inc(pT_made, 1)

            def gelu(dst, c, done):
                act.wait_ge(unit_used, S1 + 2 * (c - 16) + 2)
                for t in range(T):
                    nc.scalar.activation(dst[:, t, :], ps[:, 2 * (c % 2) + t, :], ACT.Gelu).then_inc(done, 1)
                act.wait_ge(done, T)
                nc.scalar.nop().then_inc(pair_free[c % 2], 1)
                nc.scalar.preload_act_table_set(LOG_EXP)

            for i in range(1, 5):
                hi(S1 + i)
            rT_copy(0)
            hi(S1 + 5)
            hi(S1 + 6)
            rT_copy(1)
            gelu(zz, 18, zg_made)
            exp_step(0)
            hi(S1 + 7)
            pT_copy(0)
            exp_step(1)
            hi(S1 + 8)
            pT_copy(1)
            exp_step(2)
            pT_copy(2)
            exp_step(3)
            act.wait_ge(zss_made, 1)
            rsqrt(zy, zss, HD, LN_EPS)
            hi(S1 + 9)
            pT_copy(3)
            exp_step(4)
            nc.scalar.preload_act_table_set("gelu_and_others")
            gelu(uu, 19, u_made)
            pT_copy(4)
            exp_step(5)
            pT_copy(5)
            exp_step(6)
            act.wait_ge(half_used, 2)
            copy(v[:, 0, :], ps[:, 0, :]).then_inc(v2_made, 1)
            pT_copy(6)
            exp_step(7)
            hi(S1 + 10)
            act.wait_ge(unit_used, S1 + 10)
            copy(v[:, 1, :], ps[:, 1, :]).then_inc(v2_made, 1)
            act.wait_ge(v2_made, T)
            nc.scalar.nop().then_inc(pair_free[0], 1)
            pT_copy(7)

            def branch_norm(src, made, ss, y):
                for t in range(T):
                    act.wait_ge(made, t + 1)
                    step(nc.scalar.activation(full[:, t, :], src[:, t, :], ACT.Square, accum_out=ss[:, t:t + 1]))
                rsqrt(y, ss, W, RMS_EPS)

            def gT_copy(b):
                t, k0 = b % 2, 4 - 4 * (b // 2)
                act.wait_ge(full_made, FULL_G + b + 1)
                copy(gT_hi[:, k0:k0 + 4, t * P:(t + 1) * P],
                     full[:, b, :].rearrange("p (k n) -> p k n", k=4)).then_inc(upper_made, 1)

            branch_norm(zz, sg_made, ssg[:, 2:4], yg[:, 2:4])
            hi(S1 + 11)
            gT_copy(0)
            gT_copy(1)
            act.wait_ge(o_ps, 1)
            hi(S1 + 12, out_hi[0][:])
            branch_norm(atto, o_made, ssg[:, 0:2], yg[:, 0:2])
            act.wait_ge(turned_ps, PS_G + 2)
            hi(S1 + 13, out_hi[1][:])
            gT_copy(2)
            gT_copy(3)
            hi(SFF, before=S1 + 10)
            hi(SFF + 1, before=S1 + 11)

            def x3_affine(b):
                k0 = 4 * (b % 2)
                act.wait_ge(turned_ps, PS_X3 + b + 1)
                for k in range(4):
                    ins = nc.scalar.activation(full[:, b, k * P:(k + 1) * P], ps[:, 4 + b, k * P:(k + 1) * P],
                                               ACT.Identity, scale=ln1gT[:, k0 + k:k0 + k + 1],
                                               bias=ln1bT[:, k0 + k:k0 + k + 1])
                    if k < 3:
                        ins.then_inc(act_own, 1)
                        own[0] += 1
                step(ins)

            def x3_upper(b):
                t, k0 = b // 2, 4 * (b % 2)
                if b == 3:
                    act.wait_ge(full_made, FULL_X3 + 1)
                copy(xT_hi[:, k0:k0 + 4, t * P:(t + 1) * P],
                     full[:, b, :].rearrange("p (k n) -> p k n", k=4)).then_inc(upper_made, 1)

            def x3_root(t):
                act.wait_ge(var_made, t + 1)
                rsqrt(yl[:, t:t + 1], mv[:, t, 1:2], 1, LN_EPS)

            x3_root(0)
            x3_affine(0)
            x3_upper(0)
            x3_root(1)
            for b in (1, 2):
                x3_affine(b)
                x3_upper(b)
            x3_upper(3)
            nc.scalar.preload_act_table_set("silu_and_others")

            def hi_in(i, turn):
                if turn is None:
                    return hi(i)
                slot, value = slot_of(load_of(i))
                act.wait_ge(land[slot], turn * 16 + value)
                act.wait_ge(unit_used, turn * RING + (i - 1))
                copy(w_hi[:, i % 2, :], ring[:, slot, :]).then_inc(hi_made, 1)

            def ffn_hidden(c, turn, between):
                n = c if turn is None else turn * LOOP_B + c
                u = SFF + 1 if c == 0 else body_unit(c)
                act.wait_ge(unit_used, (u if c == 0 else u + 1) if turn is None else turn * RING + (u + 1))
                if c >= 1:
                    act.wait_ge(hid_made, n)
                nc.scalar.activation(sil2[:].rearrange("p m n -> p (m n)"), ps[:, 4 + 2 * (c % 2), :],
                                     ACT.Silu).then_inc(sil2_made, 1)
                between()
                act.wait_ge(hid_made, n + 1)
                upper = end_hi if c == NCH - 1 and turn is None else hid_hi
                copy(upper[:], hid[:]).then_inc(hidhi_made, 1)

            def ffn_body(c, turn=None):
                i = body_unit(c)
                if i >= SFF + 2:
                    hi_in(i, turn)
                ffn_hidden(c - 1, turn, lambda: hi_in(i + 1, turn))
                hi_in(i + 2, turn)

            ffn_body(1)
            with act.Fori(0, LOOP_N) as turn:
                for c in range(2, 2 + LOOP_B):
                    ffn_body(c, turn)
            ffn_body(NCH - 1)
            ffn_hidden(NCH - 1, None, lambda: hi(body_unit(NCH)))
            nc.scalar.preload_act_table_set(LOG_EXP)
            for t in range(T):
                act.wait_ge(var_made, T + t + 1)
                rsqrt(yl[:, t:t + 1], mv[:, t, 1:2], 1, LN_EPS)
                if t == 0:
                    act.wait_ge(shift_made, 1)
                    for h in range(2):
                        x = X[:, 0, h * 512:(h + 1) * 512]
                        nc.scalar.activation(x, x, ACT.Identity, scale=yl[:, 0:1], bias=shift).then_inc(normed, 1)

        @block.vector
        def _(dve):
            tt, ts, stt = nc.vector.tensor_tensor, nc.vector.tensor_scalar, nc.vector.scalar_tensor_tensor
            red = nc.vector.tensor_reduce
            own = [0]

            def step(ins):
                own[0] += 1
                ins.then_inc(dve_own, 1)
                dve.wait_ge(dve_own, own[0])

            def f32(ap):
                return ap.bitcast(F32)

            roots = [0]

            def refine(y, ss, n, eps):
                roots[0] += 1
                dve.wait_ge(root_made, roots[0])
                k = y.shape[1]
                a, b = nw[:, 0, 0:k], nw[:, 1, 0:k]
                ts(a, ss, 1.0 / n, eps, ALU.mult, ALU.add)
                step(tt(b, y, y, ALU.mult))
                step(tt(a, a, b, ALU.mult))
                step(ts(a, a, -0.5, 1.5, ALU.mult, ALU.add))
                step(tt(y, y, a, ALU.mult))

            def lo(i, dst=None, upper=None):
                slot, _ = slot_of(load_of(i))
                dve.wait_ge(hi_made, i + 1)
                tt(w_lo[:, i % 2, :] if dst is None else dst, ring[:, slot, :],
                   f32(w_hi[:, i % 2, :] if dst is None else upper), ALU.subtract).then_inc(lo_made, 1)

            def bc(ap, n):
                return ap.unsqueeze(2).to_broadcast([ap.shape[0], ap.shape[1], n])

            for t in range(T):
                refine(y1[:, t:t + 1], ss1[:, t:t + 1], D, RMS_EPS)
                ts(xn[:, t, :], X[:, t, :], y1[:, t:t + 1], None, ALU.mult).then_inc(xn_made, 1)
            dve.wait_ge(land_id, 16 * 2)

            def scaled(b, base, g, bank):
                dve.wait_ge(turned_ps, base + b + 1)
                tt(full[:, b, :].rearrange("p (k n) -> p k n", k=4),
                   ps[:, bank + b, :].rearrange("p (k n) -> p k n", k=4), bc(g, P), ALU.mult).then_inc(full_made, 1)

            def lower_split(b, k0, t, base, dst_hi, dst_lo):
                dve.wait_ge(upper_made, base + b + 1)
                tok = slice(t * P, (t + 1) * P)
                tt(dst_lo[:, k0:k0 + 4, tok], full[:, b, :].rearrange("p (k n) -> p k n", k=4),
                   f32(dst_hi[:, k0:k0 + 4, tok]), ALU.subtract).then_inc(split_made, 1)

            def h_scaled(b):
                scaled(b, PS_H, g1[:, 4 * (b % 2):4 * (b % 2) + 4], 0)

            def h_lower(b):
                lower_split(b, 4 * (b % 2), b // 2, SP_H, hT_hi, hT_lo)

            h_scaled(0)
            h_scaled(1)
            lo(0)
            h_lower(0)
            h_lower(1)
            h_scaled(2)
            h_scaled(3)
            h_lower(2)
            h_lower(3)
            lo(1)
            dve.wait_ge(land_qk, 16 * 4)
            ts(gq, gq, HD ** -0.5, None, ALU.mult).then_inc(dve_own, 1)
            own[0] += 1
            lo(2)

            def qk_norm(which):
                dve.wait_ge(qk_sq, which + 1)
                y, ss = (yk, yq)[which], (ssk, ssq)[which]
                red(ss, sq[:].rearrange("p t (h d) -> p (t h) d", d=HD), AX, ALU.add).then_inc(qk_ss, 1)
                refine(y, ss, HD, RMS_EPS)
                tt(qk[:, which].rearrange("p t (h d) -> p (t h) d", d=HD),
                   ps[:, 2 * which:2 * which + 2, :].rearrange("p t (h d) -> p (t h) d", d=HD), bc(y, HD),
                   ALU.mult).then_inc(qk_made, 1)
                dve.wait_ge(qk_made, which + 1)
                nc.vector.engine_nop().then_inc(pair_free[which], 1)

            def zb(p):
                return ps[:, 4 + 2 * (p % 2):6 + 2 * (p % 2), 0:384]

            def sp_step(p):
                dve.wait_ge(log_made, p + 1)
                stt(stick[:], zb(p), 0.0, stick[:], ALU.max, ALU.add).then_inc(sp_made, 1)

            def brlo_step(p):
                dve.wait_ge(brhi_made, p + 1)
                tt(brT_lo[:, 0, p, :], ps[:, 4 + 2 * (p % 2), 0:SEQ], f32(brT_hi[:, 0, p, :]),
                   ALU.subtract).then_inc(br_made, 1)

            lo(3)
            qk_norm(0)
            lo(4)
            lo(5)
            qk_norm(1)
            lo(6)
            lo(7)
            lo(8)
            sp_step(0)
            lo(9)
            sp_step(1)
            lo(10)
            brlo_step(0)
            lo(11)
            brlo_step(1)
            sp_step(2)
            lo(12)
            sp_step(3)
            lo(13)
            brlo_step(2)
            lo(14)
            brlo_step(3)
            lo(15)

            def banks4(c):
                return ps[:, 2 * (c % 2):2 * (c % 2) + 2, :].rearrange("p b (m n) -> p (b m) n", n=SEQ)

            dve.wait_ge(land_taps, 16)
            dve.wait_ge(cc_made, 1)
            dve.wait_ge(unit_used, 2 * CH_CU + 2)
            tt(cu[:], banks4(CH_CU), cu[:], ALU.mult).then_inc(pair_free[0], 1)
            dve.wait_ge(pair_free[0], 4)
            for m in range(4):
                ts(cy[:, m, :], cu[:, m, :], cw[:, 2, m:m + 1], None, ALU.mult).then_inc(dve_own, 1)
            own[0] += 4
            dve.wait_ge(dve_own, own[0])
            lo(16)
            for j in (1, 0):
                off = 2 - j
                for m in range(4):
                    stt(cy[:, m, off:SEQ], cu[:, m, 0:SEQ - off], cw[:, j, m:m + 1], cy[:, m, off:SEQ], ALU.mult,
                        ALU.add).then_inc(dve_own, 1)
                own[0] += 4
                dve.wait_ge(dve_own, own[0])
            lo(17)
            dve.wait_ge(unit_used, 2 * CH_CB + 2)
            tt(cy[:], banks4(CH_CB), cy[:], ALU.mult).then_inc(conv_made, 1)
            dve.wait_ge(conv_made, 1)
            nc.vector.engine_nop().then_inc(pair_free[1], 1)
            dve.wait_ge(convhi_made, 1)
            tt(brT_lo[:, 1], cy[:], f32(brT_hi[:, 1]), ALU.subtract).then_inc(conv_split, 1)
            for i in range(18, 23):
                lo(i)
            dve.wait_ge(ga_sig, 1)
            dve.wait_ge(gb_sig, 1)
            def merge_a(h):
                g = ga[:, 4 * h:4 * h + 4, :]
                dve.wait_ge(unit_used, 21 + 2 * h)
                tt(g, banks4(10 + 2 * h), g, ALU.mult).then_inc(pair_free[0], 1)

            def merge_b(h):
                g = gb[:, 4 * h:4 * h + 4, :]
                dve.wait_ge(unit_used, 22 + 2 * h)
                tt(g, banks4(11 + 2 * h), g, ALU.mult).then_inc(pair_free[1], 1)

            def merge_sum(h):
                m4 = slice(4 * h, 4 * h + 4)
                dve.wait_ge(pair_free[0], 6 + h)
                dve.wait_ge(pair_free[1], 6 + h)
                tt(ga[:, m4, :], ga[:, m4, :], gb[:, m4, :], ALU.add).then_inc(mg_made, 1)

            def merge_lower(h):
                m4 = slice(4 * h, 4 * h + 4)
                dve.wait_ge(mghi_made, h + 1)
                tt(mgT_lo[:, m4, :], ga[:, m4, :], f32(mgT_hi[:, m4, :]), ALU.subtract).then_inc(mgT_made, 1)

            merge_a(0)
            lo(23)
            merge_b(0)
            merge_sum(0)
            lo(24)
            merge_lower(0)
            merge_a(1)
            merge_b(1)
            lo(25)
            merge_sum(1)
            merge_lower(1)
            lo(26)
            lo(27)
            for h in range(2):
                for t in range(T):
                    if h == 0:
                        dve.wait_ge(unit_used, 27)
                    elif t == 0:
                        dve.wait_ge(half_used, 1)
                    else:
                        dve.wait_ge(unit_used, 28)
                    tt(X[:, t, h * 512:(h + 1) * 512], ps[:, 2 * h + t, :], X[:, t, h * 512:(h + 1) * 512],
                       ALU.add).then_inc(x2_made, 1)
                dve.wait_ge(x2_made, T * (h + 1))
                nc.vector.engine_nop().then_inc(pair_free[h], 1)

            dve.wait_ge(land_small, 16 * 10)
            for b in range(4):
                t, k0 = b // 2, 4 * (b % 2)
                dve.wait_ge(turned_ps, PS_R + b + 1)
                tt(h2T[:, k0:k0 + 4, t * P:(t + 1) * P], ps[:, 4 + b, :].rearrange("p (k n) -> p k n", k=4),
                   bc(g2[:, k0:k0 + 4], P), ALU.mult).then_inc(h2T_made, 1)
            refine(y2, ss2, D, RMS_EPS)
            for t in range(T):
                ts(h2n[:, t, :], X[:, t, :], y2[:, t:t + 1], None, ALU.mult).then_inc(h2n_made, 1)

            pos = [0]

            def cell(n):
                a = pos[0]
                pos[0] += n
                return rt[:, a:a + n]

            def tg(ap, n):
                return ap.rearrange("p (t n) -> p t n", n=n)

            assign = cell(T * NE)
            gexp = cell(T * NG)
            eexp = cell(T)
            comb = cell(T * NE)
            place = cell(T * NE)
            logits = tg(cell(T * 36), 36)
            goh, gtmp = tg(cell(T * NG), NG), tg(cell(T * NG), NG)
            egrp, emask = tg(cell(T * EPG), EPG), tg(cell(T * EPG), EPG)
            oh1, oh2, etmp = (tg(cell(T * EPG), EPG) for _ in range(3))
            prod = cell(T * NE)
            gmax, gi, gsum, m1, m2, i1, den, wt1, wt2, gw = (cell(T) for _ in range(10))
            counts, over = cell(1), cell(8)
            i8 = iota[:, 0:EPG].unsqueeze(1).to_broadcast([P, T, EPG])
            i4 = iota[:, 0:NG].unsqueeze(1).to_broadcast([P, T, NG])

            def first_max(vals, n, mxv, idx, onehot, tmp, iot):
                step(red(mxv, vals, AX, ALU.max))
                step(tt(tmp, vals, bc(mxv, n), ALU.is_ge))
                step(stt(tmp, tmp, -64.0, iot, ALU.mult, ALU.add))
                step(red(idx, tmp, AX, ALU.min))
                step(tt(onehot, tmp, bc(idx, n), ALU.is_equal))

            dve.wait_ge(logit_ps, 1)
            dve.wait_ge(h2n_made, T)
            for t in range(T):
                ins = stt(logits[:, t, :], ps[:, 0, t * 36:t * 36 + 36], y2[:, t:t + 1], rbias, ALU.mult, ALU.add)
            step(ins)
            lg = logits[:, :, 0:NG]
            first_max(lg, NG, gmax, gi, goh, gtmp, i4)
            tt(tg(gexp, NG), lg, bc(gmax, NG), ALU.subtract).then_inc(gdiff_made, 1)
            for t in range(T):
                tt(prod[:, t * NE:(t + 1) * NE].rearrange("p (g e) -> p g e", g=NG),
                   logits[:, t, NG:NG + NE].rearrange("p (g e) -> p g e", g=NG),
                   bc(goh[:, t, :], EPG), ALU.mult).then_inc(dve_own, 1)
            own[0] += T
            dve.wait_ge(dve_own, own[0])
            step(red(egrp, prod.rearrange("p (t g e) -> p t e g", t=T, g=NG), AX, ALU.add))
            first_max(egrp, EPG, m1, i1, oh1, etmp, i8)
            step(stt(emask, oh1, -3e38, egrp, ALU.mult, ALU.add))
            first_max(emask, EPG, m2, i1, oh2, etmp, i8)
            tt(eexp, m2, m1, ALU.subtract).then_inc(gdiff_made, 1)
            step(tt(etmp, oh1, oh2, ALU.add))
            for t in range(T):
                ins = tt(assign[:, t * NE:(t + 1) * NE].rearrange("p (g e) -> p g e", g=NG), bc(goh[:, t, :], EPG),
                         etmp[:, t, :].unsqueeze(1).to_broadcast([P, NG, EPG]), ALU.mult)
                step(ins)
            nc.vector.engine_nop().then_inc(assign_made, 1)
            dve.wait_ge(rank_ps, 1)
            step(stt(place, ps[:, 7, 0:T * NE], 1.0, assign, ALU.add, ALU.mult))
            ts(place, place, -1.0, None, ALU.add).then_inc(place_made, 1)
            red(counts, ps[:, 7, T * NE:T * NE + NE], AX, ALU.max).then_inc(place_made, 1)

            def slots(it, q, s, r=None):
                if r is not None:
                    dve.wait_ge(next_round, r + 1)
                dve.wait_ge(s["gath_ps"], it * 2 + 1)
                for t in range(T):
                    e = q * QUAD + t * NE
                    ins = tt(pick[:, t, :].rearrange("p (j c) -> p j c", j=QUAD),
                             iota.unsqueeze(1).to_broadcast([P, QUAD, CAP]),
                             place[:, bass.ds(e, QUAD)].unsqueeze(2).to_broadcast([P, QUAD, CAP]), ALU.is_equal)
                ins.then_inc(s["pick_made"], 1)

            def weighted_slots(it, q, s):
                dve.wait_ge(s["pick_made"], it + 1)
                dve.wait_ge(s["aT_ps"], it + 1)
                for t in range(T):
                    e = q * QUAD + t * NE
                    ins = tt(pickw[:, t, :].rearrange("p (j c) -> p j c", j=QUAD),
                             pick[:, t, :].rearrange("p (j c) -> p j c", j=QUAD),
                             comb[:, bass.ds(e, QUAD)].unsqueeze(2).to_broadcast([P, QUAD, CAP]), ALU.mult)
                ins.then_inc(s["pickw_made"], 1)

            def gathered(it, s):
                for b in range(2):
                    dve.wait_ge(s["gath_ps"], it * 2 + (2 + b))
                    tt(heT[:, 4 * b:4 * b + 4, :], ps[:, 6 + b, :].rearrange("p (k n) -> p k n", k=4),
                             bc(g2[:, 4 * b:4 * b + 4], P), ALU.mult).then_inc(s["heT_made"], 1)

            def hidden(it, s):
                dve.wait_ge(s["sil_made"], it + 1)
                dve.wait_ge(s["used"], it * UPQ + (8 + s["start"]))
                tt(act_e[:], ps[:, 5, 0:FE], sil[:], ALU.mult).then_inc(s["act_made"], 1)

            def quad(it, q, s, r=None):
                slots(it, q, s, r)
                weighted_slots(it, q, s)
                gathered(it, s)
                hidden(it, s)

            next_round = sem("next_round")
            start0, start1 = first | {"start": 0}, more | {"start": UPQ}
            dve.wait_ge(place_made, 2)
            slots(0, 0, start0)
            dve.wait_ge(gexp_made, 2)
            step(red(gsum, tg(gexp, NG), AX, ALU.add))
            step(nc.vector.reciprocal(gw, gsum))
            step(ts(den, eexp, 1.0, None, ALU.add))
            step(nc.vector.reciprocal(den, den))
            step(tt(wt1, den, gw, ALU.mult))
            step(tt(wt2, wt1, eexp, ALU.mult))
            step(tt(egrp, oh1, bc(wt1, EPG), ALU.mult))
            gathered(0, start0)
            step(tt(emask, oh2, bc(wt2, EPG), ALU.mult))
            step(tt(egrp, egrp, emask, ALU.add))
            for t in range(T):
                step(tt(comb[:, t * NE:(t + 1) * NE].rearrange("p (g e) -> p g e", g=NG), bc(goh[:, t, :], EPG),
                        egrp[:, t, :].unsqueeze(1).to_broadcast([P, NG, EPG]), ALU.mult))
            weighted_slots(0, 0, start0)
            step(ts(over[:, 0:7], thr, counts, None, ALU.is_lt))
            step(red(over[:, 7:8], over[:, 0:7], AX, ALU.add))
            nc.vector.tensor_copy(cnt[:, 0:1], over[:, 7:8]).then_inc(place_made, 1)
            hidden(0, start0)
            with dve.Fori(1, NQ) as q:
                quad(q, q, start0)
            dve.wait_ge(place_made, 3)
            extra = dve.value_load(cnt[0:1, 0:1], min_val=0, max_val=7)
            with dve.If(extra > 0):
                dve.wait_ge(first["spread"], 2 * NQ + 1)
                with dve.Fori(0, extra) as r:
                    ts(place, place, -float(CAP), None, ALU.add).then_inc(next_round, 1)
                    with dve.Fori(0, NQ) as q:
                        quad(r * NQ + q, q, start1, r)
            dve.wait_ge(more["spread"], extra * (2 * NQ) + 1)
            lo(S1)

            dve.wait_ge(first["spread"], 2 * NQ + 1)
            for t in range(T):
                nc.vector.tensor_copy(X[:, t, 512:D], ps[:, 2 * t + 1, :]).then_inc(sum_d, 1)

            def lower_ps(b):
                t, k0 = b // 2, 4 * (b % 2)
                tok = slice(t * P, (t + 1) * P)
                dve.wait_ge(upper_made, SP_X2 + b + 1)
                tt(xT_lo[:, k0:k0 + 4, tok], ps[:, 4 + b, :].rearrange("p (k n) -> p k n", k=4),
                   f32(xT_hi[:, k0:k0 + 4, tok]), ALU.subtract).then_inc(split_made, 1)

            for b in range(4):
                lower_ps(b)
            lo(S1 + 1)
            lo(S1 + 2)
            dve.wait_ge(spT_ps, 1)
            tt(spT[:], ps[:, 4:6, :].rearrange("p b (g n) -> p (b g) n", n=P),
               triu.unsqueeze(1).to_broadcast([P, NH, P]), ALU.mult).then_inc(spT_made, 1)
            lo(S1 + 3)

            def rope_products(which):
                dve.wait_ge(unit_used, S1 + 2 * which + 2)
                if which:
                    dve.wait_ge(rope_made, 1)
                for t in range(T):
                    src = ps[:, 2 * (which % 2) + t, :].rearrange("p (h d) -> p h d", d=HD)
                    dst = qk[:, which, t, :].rearrange("p (h d) -> p h d", d=HD)
                    tmp = sq[:, t, :].rearrange("p (h d) -> p h d", d=HD)

                    def along(tab, a, b):
                        return tab[:, t, a:b].unsqueeze(1).to_broadcast([P, NH, b - a])

                    tt(dst, src, along(cos, 0, HD), ALU.mult)
                    tt(tmp[:, :, 0:HD // 2], src[:, :, HD // 2:HD], along(sin, 0, HD // 2), ALU.mult)
                    ins = tt(tmp[:, :, HD // 2:HD], src[:, :, 0:HD // 2], along(sin, HD // 2, HD), ALU.mult)
                ins.then_inc(pair_free[which], 1)

            def rope_sum(which):
                dve.wait_ge(pair_free[which], 9)
                tt(qk[:, which], qk[:, which], sq[:], ALU.add).then_inc(rope_made, 1)

            def max_step(h):
                dve.wait_ge(s_ps, h + 1)
                red(mx[:, h, 0:1], ps[:, 4 + h % 2, 0:P], AX, ALU.max)
                step(red(mx[:, h, 1:2], ps[:, 4 + h % 2, P:P + SEQ], AX, ALU.max))
                ts(mxn[:, h, :], mx[:, h, :], -(HD ** -0.5), None, ALU.mult).then_inc(mx_made, 1)

            rope_products(0)
            rope_sum(0)
            lo(S1 + 4)
            rope_products(1)
            lo(S1 + 5)
            rope_sum(1)
            lo(S1 + 6)
            max_step(0)
            dve.wait_ge(zg_made, T)
            step(red(zs, zz[:].rearrange("p t (g d) -> p (t g) d", d=HD), AX, ALU.add))
            ts(zs, zs, 1.0 / HD, None, ALU.mult).then_inc(zmean_made, 1)
            max_step(1)
            lo(S1 + 7)
            max_step(2)
            dve.wait_ge(zq_made, 1)
            red(zss, sq[:].rearrange("p t (g d) -> p (t g) d", d=HD), AX, ALU.add).then_inc(zss_made, 1)
            lo(S1 + 8)
            max_step(3)
            refine(zy, zss, HD, LN_EPS)
            nc.vector.engine_nop().then_inc(zy_ready, 1)
            max_step(4)
            lo(S1 + 9)
            max_step(5)
            max_step(6)
            max_step(7)
            dve.wait_ge(mix_ps, 1)
            for t in range(T):
                mixed = ps[:, 2:4, :].rearrange("p b n -> p (b n)").rearrange("p (g t d) -> p t g d", g=NH, t=T)
                ins = tt(zz[:, t, :].rearrange("p (g d) -> p g d", d=HD), mixed[:, t], bc(bsp, HD), ALU.add)
            step(ins)
            nc.vector.engine_nop().then_inc(pair_free[1], 1)
            dve.wait_ge(u_made, T)
            for t in range(T):
                tt(zz[:, t, :], zz[:, t, :], uu[:, t, :], ALU.mult).then_inc(sg_made, 1)
            lo(S1 + 10)

            def branch_norm(src, ss, y):
                refine(y, ss, W, RMS_EPS)
                for t in range(T):
                    ts(src[:, t, :], src[:, t, :], y[:, t:t + 1], None, ALU.mult).then_inc(cat_made, 1)

            def g_scaled(b):
                k0 = 4 - 4 * (b // 2)
                scaled(b, PS_G, gmix[:, k0:k0 + 4], 4)

            def g_lower(b):
                lower_split(b, 4 - 4 * (b // 2), b % 2, SP_G, gT_hi, gT_lo)

            branch_norm(zz, ssg[:, 2:4], yg[:, 2:4])
            g_scaled(0)
            g_scaled(1)
            g_lower(0)
            g_lower(1)
            lo(S1 + 11)
            step(nc.vector.reciprocal(rinv, rsum))
            dve.wait_ge(o_ps, 1)
            for t in range(T):
                tt(atto[:, t, :].rearrange("p (h d) -> p h d", d=HD), ps[:, 6 + t, :].rearrange("p (h d) -> p h d", d=HD),
                   rinv[:, :, t:t + 1].to_broadcast([P, NH, HD]), ALU.mult).then_inc(o_made, 1)
            lo(S1 + 12, out_lo[0][:], out_hi[0][:])
            branch_norm(atto, ssg[:, 0:2], yg[:, 0:2])
            g_scaled(2)
            g_scaled(3)
            g_lower(2)
            g_lower(3)
            lo(S1 + 13, out_lo[1][:], out_hi[1][:])

            def half(h):
                return slice(h * 512, (h + 1) * 512)

            def residual(h, t, bank):
                step(stt(X[:, t, half(h)], X[:, t, half(h)], ALPHA, ps[:, bank, :], ALU.mult, ALU.add))
                nc.vector.bn_stats(bst[:, t, h, :], X[:, t, half(h)]).then_inc(dve_own, 1)
                own[0] += 1

            def tile_mean(t):
                dve.wait_ge(dve_own, own[0])
                nc.vector.bn_aggr(mv[:, t, :], bst[:, t, :, :]).then_inc(var_made, 1)
                dve.wait_ge(var_made, 1 + vars_made[0])
                vars_made[0] += 1

            vars_made = [0]

            def x3_normed(t):
                refine(yl[:, t:t + 1], mv[:, t, 1:2], 1, LN_EPS)
                ts(X[:, t, :], X[:, t, :], mv[:, t, 0:1], yl[:, t:t + 1], ALU.subtract,
                   ALU.mult).then_inc(xhat_made, 1)

            for h in range(2):
                dve.wait_ge(half_used, 3 + h)
                residual(h, 0, 2 * h)
            tile_mean(0)
            x3_normed(0)
            for h in range(2):
                dve.wait_ge(unit_used, S1 + 13 + h)
                residual(h, 1, 2 * h + 1)
            tile_mean(1)
            x3_normed(1)
            for n in range(2):
                dve.wait_ge(ffn_lo_made, n + 1)
                nc.vector.engine_nop().then_inc(lo_made, 1)
            lower_split(0, 0, 0, SP_X3, xT_hi, xT_lo)
            lower_split(1, 4, 0, SP_X3, xT_hi, xT_lo)
            dve.wait_ge(turned_ps, PS_X3 + 4)
            f4 = full[:, 3, :].rearrange("p (k n) -> p k n", k=4)
            step(tt(f4, ps[:, 7, :].rearrange("p (k n) -> p k n", k=4), bc(ln1gT[:, 4:8], P), ALU.mult))
            tt(f4, f4, bc(ln1bT[:, 4:8], P), ALU.add).then_inc(full_made, 1)
            lower_split(2, 0, 1, SP_X3, xT_hi, xT_lo)
            lower_split(3, 4, 1, SP_X3, xT_hi, xT_lo)

            def lo_in(i, turn):
                if turn is None:
                    return lo(i)
                slot, _ = slot_of(load_of(i))
                dve.wait_ge(hi_made, turn * RING + (i + 1))
                tt(w_lo[:, i % 2, :], ring[:, slot, :], f32(w_hi[:, i % 2, :]), ALU.subtract).then_inc(lo_made, 1)

            def ffn_hidden(c, turn, between):
                n = c if turn is None else turn * LOOP_B + c
                u = SFF + 1 if c == 0 else body_unit(c) + 1
                dve.wait_ge(sil2_made, n + 1)
                if c >= 1:
                    dve.wait_ge(hidT_made, n)
                dve.wait_ge(unit_used, u + 1 if turn is None else turn * RING + (u + 1))
                tt(hid[:].rearrange("p m n -> p (m n)"), ps[:, 5 + 2 * (c % 2), :],
                   sil2[:].rearrange("p m n -> p (m n)"), ALU.mult).then_inc(hid_made, 1)
                between()
                dve.wait_ge(hidhi_made, n + 1)
                upper, lower = (end_hi, end_lo) if c == NCH - 1 and turn is None else (hid_hi, hid_lo)
                tt(lower[:], hid[:], f32(upper[:]), ALU.subtract).then_inc(hidT_made, 1)

            def ffn_body(c, turn=None):
                i = body_unit(c)
                lo_in(i, turn)
                ffn_hidden(c - 1, turn, lambda: lo_in(i + 1, turn))
                lo_in(i + 2, turn)

            ffn_body(1)
            with dve.Fori(0, LOOP_N) as turn:
                for c in range(2, 2 + LOOP_B):
                    ffn_body(c, turn)
            ffn_body(NCH - 1)
            ffn_hidden(NCH - 1, None, lambda: lo(body_unit(NCH)))
            dve.wait_ge(x3_made, T)
            dve.wait_ge(land_ln2, 16 * 2)
            for t in range(T):
                for h in range(2):
                    dve.wait_ge(y_ps, 2 * t + h + 1)
                    residual(h, t, 2 * t + h)
                tile_mean(t)
                if t == 0:
                    refine(yl[:, 0:1], mv[:, 0, 1:2], 1, LN_EPS)
                    stt(shift, mv[:, 0, 0:1], -1.0, yl[:, 0:1], ALU.mult, ALU.mult).then_inc(shift_made, 1)
                    continue
                for h in range(2):
                    x = X[:, t, half(h)]
                    ins = stt(x, x, mv[:, t, 0:1], ln2[:, 0, half(h)], ALU.subtract, ALU.mult)
                step(ins)
                refine(yl[:, t:t + 1], mv[:, t, 1:2], 1, LN_EPS)
                for h in range(2):
                    x = X[:, t, half(h)]
                    stt(x, x, yl[:, t:t + 1], ln2[:, 1, half(h)], ALU.mult, ALU.add).then_inc(y_out[1], 1)

        @block.gpsimd
        def _(pool):
            tt = nc.gpsimd.tensor_tensor

            def groups(ap):
                return ap.rearrange("p t (g d) -> p (t g) d", d=HD)

            def by_group(ap):
                return ap.unsqueeze(2).to_broadcast([P, T * NH, HD])

            def row(i):
                return lngb[:, i, :].unsqueeze(1).to_broadcast([P, T, W])

            pool.wait_ge(zmean_made, 1)
            tt(groups(zz[:]), groups(zz[:]), by_group(zs), ALU.subtract).then_inc(zc_made, 1)
            pool.wait_ge(zc_made, 1)
            tt(sq[:], zz[:], zz[:], ALU.mult).then_inc(zq_made, 1)
            pool.wait_ge(zq_made, 1)
            pool.wait_ge(land_b2, 16 * 3)
            pool.wait_ge(zy_ready, 1)
            tt(groups(zz[:]), groups(zz[:]), by_group(zy), ALU.mult).then_inc(zn_made, 1)
            pool.wait_ge(zn_made, 1)
            tt(zz[:], zz[:], row(0), ALU.mult).then_inc(zn_made, 1)
            pool.wait_ge(zn_made, 2)
            tt(zz[:], zz[:], row(1), ALU.add).then_inc(z_made, 1)
            for i in (SFF, SFF + 1):
                pool.wait_ge(hi_made, i + 1)
                slot, _ = slot_of(load_of(i))
                tt(w_lo[:, i % 2, :], ring[:, slot, :], w_hi[:, i % 2, :].bitcast(F32), ALU.subtract
                   ).then_inc(ffn_lo_made, 1)
            pool.wait_ge(land_ln1, 16 * 2)
            pool.wait_ge(turned_ps, PS_X3 + 4)
            for t in range(T):
                tt(X[:, t, :], X[:, t, :], ln1[:, 0, :], ALU.mult).then_inc(x3g_made, 1)
                pool.wait_ge(x3g_made, t + 1)
                tt(X[:, t, :], X[:, t, :], ln1[:, 1, :], ALU.add).then_inc(x3_made, 1)
            pool.wait_ge(land_ln2, 16 * 2)
            for h in range(2):
                cols = slice(h * 512, (h + 1) * 512)
                pool.wait_ge(normed, h + 1)
                tt(X[:, 0, cols], X[:, 0, cols], ln2[:, 0, cols], ALU.mult).then_inc(x3g_made, 1)
                pool.wait_ge(x3g_made, T + h + 1)
                tt(X[:, 0, cols], X[:, 0, cols], ln2[:, 1, cols], ALU.add).then_inc(y_out[0], 1)


_INS = ["x", "norm_mix_g", "w_in", "q_norm_g", "k_norm_g", "conv_w", "w_sb_branch", "w_conv_branch", "w_out",
        "norm_ffn_g", "w_router_group", "b_router_group", "w_router_expert", "b_router_expert", "w_gate_e",
        "w_up_e", "w_down_e", "w_in_2", "attn_out_g_2", "gmlp_out_g_2", "gmlp_ln_g_2", "gmlp_ln_b_2",
        "w_spatial_2", "b_spatial_2", "w_out_2", "ln1_g_2", "ln1_b_2", "w_gate_2", "w_up_2", "w_down_2",
        "ln2_g_2", "ln2_b_2"]


def kernel(**inputs):
    import concourse.bacc as _bacc
    from concourse import mybir as _mybir
    from concourse.bass_utils import run_bass_kernel_spmd as _run

    nc = _bacc.Bacc("TRN2", target_bir_lowering=False, num_devices=1, dynamic_dma_scratch_size=256)
    arrays = {"in_consts": shape_constants()}
    for name in _INS:
        arrays[f"in_{name}"] = np.ascontiguousarray(inputs[name])
    args = [nc.dram_tensor(n, a.shape, _mybir.dt.from_np(a.dtype), kind="ExternalInput").ap()
            for n, a in arrays.items()]
    res = nc.dram_tensor("out_0", (1, SEQ, D), _mybir.dt.float32, kind="ExternalOutput").ap()
    build(nc, *args, res)
    r = _run(nc, [arrays], core_ids=[0])
    return r.results[0]["out_0"]
```
